# Optimizing a Trainium2 kernel written in Bass

```python
import math
import jax, jax.numpy as jnp
from jax import lax
import numpy as np

D_MODEL = 1024
BATCH = 1
SEQ = 1024
DEPTH = 1

BRANCH_WIDTH = D_MODEL // 2
N_BRANCHES = 4
CHUNK = 64
CONV_WIDTH = 4
NORM_EPS = 1e-6

HGRN_HEADS = 4
HGRN_EXPAND = BRANCH_WIDTH // HGRN_HEADS
HGRN_FDIM = HGRN_HEADS * HGRN_EXPAND
HGRN_VDIM = BRANCH_WIDTH
HGRN_VHEAD = HGRN_VDIM // HGRN_HEADS
SSD_DINNER = BRANCH_WIDTH
SSD_HEADDIM = 64
SSD_HEADS = SSD_DINNER // SSD_HEADDIM
SSD_GROUPS = 2
SSD_HPG = SSD_HEADS // SSD_GROUPS
SSD_STATE = 64
SSD_CONV_DIM = SSD_DINNER + 2 * SSD_GROUPS * SSD_STATE
GLA_HEADS = 4
GLA_KDIM = BRANCH_WIDTH // 2
GLA_VDIM = BRANCH_WIDTH
GLA_HEAD_K = GLA_KDIM // GLA_HEADS
GLA_HEAD_V = GLA_VDIM // GLA_HEADS
GLA_GATE_RANK = 16
GLA_GATE_NORMALIZER = 16.0
LRU_WIDTH = BRANCH_WIDTH
LRU_BLOCKS = 8
LRU_BLOCK = LRU_WIDTH // LRU_BLOCKS
LRU_C = 8.0
D_FF = ((8 * D_MODEL // 3 + 255) // 256) * 256

IN_SPLITS = (
    HGRN_FDIM, HGRN_FDIM, HGRN_VDIM, HGRN_VDIM,
    SSD_DINNER, SSD_CONV_DIM, SSD_HEADS,
    GLA_KDIM, GLA_KDIM, GLA_VDIM, GLA_VDIM, GLA_GATE_RANK,
    LRU_WIDTH, LRU_WIDTH,
    N_BRANCHES * D_MODEL,
)
D_IN = sum(IN_SPLITS)


F32 = jnp.float32

def rmsnorm(x, w):
    xf = x.astype(F32)
    y = xf * lax.rsqrt(jnp.mean(xf * xf, axis=-1, keepdims=True) + NORM_EPS)
    return (y * w.astype(F32)).astype(x.dtype)

def causal_dwconv(x, w, b):
    c = x.shape[-1]
    y = lax.conv_general_dilated(
        x, w[:, None, :].astype(x.dtype), window_strides=(1,),
        padding=[(w.shape[0] - 1, 0)], dimension_numbers=("NWC", "WIO", "NWC"),
        feature_group_count=c)
    return y + b.astype(x.dtype)

def chunk_gated_linear_attn(q, k, v, log_f):
    bsz, seqlen, nh, dk = q.shape
    dv = v.shape[-1]
    n = seqlen // CHUNK

    def to_chunks(t):
        return jnp.moveaxis(t.astype(F32).reshape(bsz, n, CHUNK, nh, t.shape[-1]), 1, 0)

    qc, kc, vc, gc = to_chunks(q), to_chunks(k), to_chunks(v), to_chunks(log_f)
    causal = jnp.tril(jnp.ones((CHUNK, CHUNK), bool))

    def step(state, inp):
        qi, ki, vi, gi = inp
        bcum = jnp.cumsum(gi, axis=1)
        rel = bcum[:, :, None] - bcum[:, None, :]
        rel = jnp.where(causal[None, :, :, None, None], rel, -jnp.inf)
        scores = jnp.einsum('bihd,bjhd,bijhd->bhij', qi, ki, jnp.exp(rel))
        o_intra = jnp.einsum('bhij,bjhv->bihv', scores, vi)
        o_inter = jnp.einsum('bihd,bhdv->bihv', qi * jnp.exp(bcum), state)
        b_last = bcum[:, -1:]
        k_dec = ki * jnp.exp(b_last - bcum)
        new_state = state * jnp.exp(b_last[:, 0])[..., None] + jnp.einsum('bjhd,bjhv->bhdv', k_dec, vi)
        return new_state, o_intra + o_inter

    s0 = jnp.zeros((bsz, nh, dk, dv), F32)
    _, o = lax.scan(step, s0, (qc, kc, vc, gc))
    return jnp.moveaxis(o, 0, 1).reshape(bsz, seqlen, nh, dv)

def hgrn2_branch(q, f_pre, i, g, lb, norm_w):
    bsz, seqlen, _ = q.shape
    lbf = lb.astype(F32)
    log_f = jnp.logaddexp(jnp.log(lbf), jnp.log1p(-lbf) + jax.nn.log_sigmoid(f_pre.astype(F32)))
    key = -jnp.expm1(log_f)
    qf = jax.nn.silu(q.astype(F32))
    hk = lambda t: t.reshape(bsz, seqlen, HGRN_HEADS, HGRN_EXPAND)
    hv = lambda t: t.reshape(bsz, seqlen, HGRN_HEADS, HGRN_VHEAD)
    o = chunk_gated_linear_attn(hk(qf), hk(key), hv(i.astype(F32)), hk(log_f))
    o = rmsnorm(o, norm_w) * jax.nn.silu(hv(g.astype(F32)))
    return o.reshape(bsz, seqlen, HGRN_VDIM)

def gla_branch(q, k, v, g, gate_lr, gate_w, gate_b, norm_w):
    bsz, seqlen, _ = q.shape
    log_a = jax.nn.log_sigmoid(gate_lr.astype(F32) @ gate_w.astype(F32) + gate_b.astype(F32)) / GLA_GATE_NORMALIZER
    hk = lambda t: t.astype(F32).reshape(bsz, seqlen, GLA_HEADS, GLA_HEAD_K)
    hv = lambda t: t.astype(F32).reshape(bsz, seqlen, GLA_HEADS, GLA_HEAD_V)
    o = chunk_gated_linear_attn(hk(q) * (GLA_HEAD_K ** -0.5), hk(k), hv(v), hk(log_a))
    o = rmsnorm(o, norm_w) * jax.nn.silu(hv(g))
    return o.reshape(bsz, seqlen, GLA_VDIM)

def ssd_branch(z, xbc, dt_raw, conv_w, conv_b, dt_bias, a_log, d_skip, norm_w):
    bsz, seqlen, _ = z.shape
    n = seqlen // CHUNK
    xbc = jax.nn.silu(causal_dwconv(xbc, conv_w, conv_b).astype(F32))
    xs, bm, cm = jnp.split(xbc, [SSD_DINNER, SSD_DINNER + SSD_GROUPS * SSD_STATE], axis=-1)
    dt = jax.nn.softplus(dt_raw.astype(F32) + dt_bias.astype(F32))
    a_neg = -jnp.exp(a_log.astype(F32)).reshape(SSD_GROUPS, SSD_HPG)
    x_c = xs.reshape(bsz, n, CHUNK, SSD_GROUPS, SSD_HPG, SSD_HEADDIM)
    dt_c = dt.reshape(bsz, n, CHUNK, SSD_GROUPS, SSD_HPG)
    b_c = bm.reshape(bsz, n, CHUNK, SSD_GROUPS, SSD_STATE)
    c_c = cm.reshape(bsz, n, CHUNK, SSD_GROUPS, SSD_STATE)
    a_cs = jnp.cumsum(dt_c * a_neg, axis=2)
    xdt = x_c * dt_c[..., None]
    causal = jnp.tril(jnp.ones((CHUNK, CHUNK), bool))
    seg = a_cs[:, :, :, None] - a_cs[:, :, None, :]
    lmat = jnp.exp(jnp.where(causal[None, None, :, :, None, None], seg, -jnp.inf))
    y_diag = jnp.einsum('bcigs,bcjgs,bcijgh,bcjghp->bcighp', c_c, b_c, lmat, xdt)
    decay_states = jnp.exp(a_cs[:, :, -1:] - a_cs)
    states = jnp.einsum('bcjgs,bcjgh,bcjghp->bcghps', b_c, decay_states, xdt)
    cs = jnp.cumsum(a_cs[:, :, -1], axis=1)
    rel = cs[:, :, None] - cs[:, None, :]
    ctril = jnp.tril(jnp.ones((n, n), bool))
    carried = jnp.einsum('bzcgh,bcghps->bzghps',
                         jnp.exp(jnp.where(ctril[None, :, :, None, None], rel, -jnp.inf)), states)
    prev = jnp.concatenate([jnp.zeros_like(carried[:, :1]), carried[:, :-1]], axis=1)
    y_off = jnp.einsum('bcigs,bcghps,bcigh->bcighp', c_c, prev, jnp.exp(a_cs))
    y = y_diag + y_off + x_c * d_skip.astype(F32).reshape(SSD_GROUPS, SSD_HPG)[..., None]
    y = y.reshape(bsz, seqlen, SSD_DINNER) * jax.nn.silu(z.astype(F32))
    yg = y.reshape(bsz, seqlen, SSD_GROUPS, SSD_DINNER // SSD_GROUPS)
    yg = yg * lax.rsqrt(jnp.mean(yg * yg, axis=-1, keepdims=True) + NORM_EPS)
    return yg.reshape(bsz, seqlen, SSD_DINNER) * norm_w.astype(F32)

def rglru_branch(xb, gate, conv_w, conv_b, wa, ba, wx, bx, lam):
    bsz, seqlen, _ = xb.shape
    u = causal_dwconv(xb, conv_w, conv_b).astype(F32)
    ub = u.reshape(bsz, seqlen, LRU_BLOCKS, LRU_BLOCK)
    r = jax.nn.sigmoid(jnp.einsum('blkd,kde->blke', ub, wa.astype(F32)).reshape(bsz, seqlen, LRU_WIDTH) + ba.astype(F32))
    i = jax.nn.sigmoid(jnp.einsum('blkd,kde->blke', ub, wx.astype(F32)).reshape(bsz, seqlen, LRU_WIDTH) + bx.astype(F32))
    log_a = -LRU_C * r * jax.nn.softplus(-lam.astype(F32))
    a = jnp.exp(log_a)
    bterm = jnp.sqrt(-jnp.expm1(2.0 * log_a)) * (i * u)

    def combine(e1, e2):
        a1, b1 = e1
        a2, b2 = e2
        return a1 * a2, a2 * b1 + b2

    _, h = lax.associative_scan(combine, (a, bterm), axis=1)
    return h * jax.nn.gelu(gate.astype(F32), approximate=True)

def first_inputs(seed: int = 0) -> dict:
    key = jax.random.key(seed)
    ks = jax.random.split(key, 32)
    nrm = lambda k, shape, scale: jax.random.normal(k, shape, F32) * scale
    gain = lambda k, shape: 1.0 + 0.02 * jax.random.normal(k, shape, F32)
    dt = jnp.exp(jax.random.uniform(ks[8], (DEPTH, SSD_HEADS), F32, math.log(1e-3), math.log(1e-1)))
    lam_u = jax.random.uniform(ks[19], (DEPTH, LRU_WIDTH), F32, 0.9, 0.999) ** (1.0 / LRU_C)
    return {
        "x": nrm(ks[0], (BATCH, SEQ, D_MODEL), 1.0),
        "norm_mix_w": gain(ks[1], (DEPTH, D_MODEL)),
        "w_in": nrm(ks[2], (DEPTH, D_MODEL, D_IN), D_MODEL ** -0.5),
        "hgrn_lower_bounds": nrm(ks[3], (DEPTH, HGRN_FDIM), 0.1),
        "hgrn_norm_w": gain(ks[4], (DEPTH, HGRN_VHEAD)),
        "ssd_conv_w": nrm(ks[5], (DEPTH, CONV_WIDTH, SSD_CONV_DIM), CONV_WIDTH ** -0.5),
        "ssd_conv_b": nrm(ks[6], (DEPTH, SSD_CONV_DIM), 0.01),
        "ssd_dt_bias": dt + jnp.log(-jnp.expm1(-dt)),
        "ssd_a_log": jnp.log(jax.random.uniform(ks[9], (DEPTH, SSD_HEADS), F32, 1.0, 16.0)),
        "ssd_d": gain(ks[10], (DEPTH, SSD_HEADS)),
        "ssd_norm_w": gain(ks[11], (DEPTH, SSD_DINNER)),
        "gla_gate_w": nrm(ks[12], (DEPTH, GLA_GATE_RANK, GLA_KDIM), GLA_GATE_RANK ** -0.5),
        "gla_gate_b": nrm(ks[13], (DEPTH, GLA_KDIM), 0.01),
        "gla_norm_w": gain(ks[14], (DEPTH, GLA_HEAD_V)),
        "lru_conv_w": nrm(ks[15], (DEPTH, CONV_WIDTH, LRU_WIDTH), CONV_WIDTH ** -0.5),
        "lru_conv_b": nrm(ks[16], (DEPTH, LRU_WIDTH), 0.01),
        "lru_wa": nrm(ks[17], (DEPTH, LRU_BLOCKS, LRU_BLOCK, LRU_BLOCK), LRU_BLOCK ** -0.5),
        "lru_ba": nrm(ks[18], (DEPTH, LRU_WIDTH), 0.01),
        "lru_wx": nrm(ks[20], (DEPTH, LRU_BLOCKS, LRU_BLOCK, LRU_BLOCK), LRU_BLOCK ** -0.5),
        "lru_bx": nrm(ks[21], (DEPTH, LRU_WIDTH), 0.01),
        "lru_lambda": jnp.log(lam_u) - jnp.log1p(-lam_u),
        "w_branch": nrm(ks[22], (DEPTH, N_BRANCHES, BRANCH_WIDTH, D_MODEL), BRANCH_WIDTH ** -0.5),
        "w_out": nrm(ks[23], (DEPTH, D_MODEL, D_MODEL), D_MODEL ** -0.5),
        "norm_ffn_w": gain(ks[24], (DEPTH, D_MODEL)),
        "w_ffn_in": nrm(ks[25], (DEPTH, D_MODEL, 2 * D_FF), D_MODEL ** -0.5),
        "w_ffn_out": nrm(ks[26], (DEPTH, D_FF, D_MODEL), D_FF ** -0.5),
        "norm_f_w": gain(ks[27], (D_MODEL,)),
    }

def first_block(x, norm_mix_w, w_in, hgrn_lower_bounds, hgrn_norm_w, ssd_conv_w, ssd_conv_b, ssd_dt_bias,
              ssd_a_log, ssd_d, ssd_norm_w, gla_gate_w, gla_gate_b, gla_norm_w, lru_conv_w, lru_conv_b,
              lru_wa, lru_ba, lru_wx, lru_bx, lru_lambda, w_branch, w_out, norm_ffn_w, w_ffn_in,
              w_ffn_out, norm_f_w):
    bsz, seqlen, _ = x.shape
    split_idx = np.cumsum(IN_SPLITS)[:-1].tolist()
    lb_all = jnp.cumsum(jax.nn.softmax(hgrn_lower_bounds.astype(F32), axis=0), axis=0)
    lb_all = lb_all - lb_all[0:1]
    h = x
    for l in range(DEPTH):
        xn = rmsnorm(h, norm_mix_w[l])
        proj = xn @ w_in[l]
        (hq, hf, hi, hg, sz, sxbc, sdt, gq, gk, gv, gg, glr, lx, lg, mg) = jnp.split(proj, split_idx, axis=-1)
        ya = hgrn2_branch(hq, hf, hi, hg, lb_all[l], hgrn_norm_w[l])
        yb = ssd_branch(sz, sxbc, sdt, ssd_conv_w[l], ssd_conv_b[l], ssd_dt_bias[l], ssd_a_log[l],
                        ssd_d[l], ssd_norm_w[l])
        yc = gla_branch(gq, gk, gv, gg, glr, gla_gate_w[l], gla_gate_b[l], gla_norm_w[l])
        yd = rglru_branch(lx, lg, lru_conv_w[l], lru_conv_b[l], lru_wa[l], lru_ba[l], lru_wx[l], lru_bx[l],
                          lru_lambda[l])
        ys = jnp.stack([ya, yb, yc, yd], axis=2).astype(h.dtype)
        branch_out = jnp.einsum('blnw,nwd->blnd', ys, w_branch[l])
        gates = jax.nn.sigmoid(mg.astype(F32)).reshape(bsz, seqlen, N_BRANCHES, D_MODEL)
        merged = jnp.sum(gates * branch_out.astype(F32), axis=2).astype(h.dtype)
        h = h + (merged @ w_out[l]).astype(h.dtype)
        xn = rmsnorm(h, norm_ffn_w[l])
        gate_up = xn @ w_ffn_in[l]
        g_ff, u_ff = jnp.split(gate_up, [D_FF], axis=-1)
        h = h + ((jax.nn.silu(g_ff) * u_ff) @ w_ffn_out[l]).astype(h.dtype)
    return rmsnorm(h, norm_f_w)


_first_inputs = first_inputs


def first_inputs(seed=0):
    import zlib

    import numpy as np

    out = dict(_first_inputs(seed))
    spreads = {}
    factors = {}
    for name, (base, spread) in spreads.items():
        noise = np.random.default_rng([zlib.crc32(name.encode()), seed]).standard_normal(out[name].shape)
        drawn = base * np.exp(spread * noise) if base else spread * noise
        out[name] = __import__('jax').numpy.asarray(drawn.astype(out[name].dtype))
    for name, factor in factors.items():
        out[name] = (out[name] * factor).astype(out[name].dtype)
    return out


_narrow_inputs = first_inputs


def first_inputs(seed=0):

    out = dict(_narrow_inputs(seed))
    wider = {'hgrn_norm_w': 11.03,
     'ssd_conv_b': 10.14,
     'ssd_d': 12.0,
     'ssd_norm_w': 6.61,
     'gla_gate_b': 12.0,
     'gla_norm_w': 11.38,
     'lru_conv_b': 3.99,
     'lru_ba': 12.0,
     'lru_bx': 12.0,
     'norm_ffn_w': 5.16,
     'norm_f_w': 3.51}
    for name, times in wider.items():
        mean = out[name].mean()
        out[name] = (mean + times * (out[name] - mean)).astype(out[name].dtype)
    return out


DEPTH_2 = 2

D_HEAD = 64
GRID_W = 64
Q_BLOCK = 128
RMS_EPS = 1e-6
H_A = D_MODEL // (2 * D_HEAD)
WIN_R = 8
WIN_C = 16
H_B = D_MODEL // (2 * D_HEAD)
H_B_KV = H_B // 4
AXIAL_THETA = 10000.0
H_C = D_MODEL // (2 * D_HEAD)
Q_LORA = D_MODEL // 4
KV_LORA = D_MODEL // 8
C_NOPE = 64
C_ROPE = 32
C_V = 64
MLA_THETA = 10000.0
H_D = D_MODEL // (4 * D_HEAD)
D_V = 2 * D_HEAD
ROPE_THETA = 500000.0
ROT_DIM = D_HEAD // 4
GATE_E = (H_A + H_B) * D_HEAD
SPLIT_E = [H_A * D_HEAD, H_A * D_HEAD, H_A * D_HEAD,
           H_B * D_HEAD, H_B_KV * D_HEAD, H_B_KV * D_HEAD, GATE_E]
GATE_O = H_C * C_V + H_D * D_V
SPLIT_O = [Q_LORA, KV_LORA, C_ROPE, 2 * H_D * D_HEAD, 2 * H_D * D_HEAD,
           H_D * D_V, GATE_O]
IN_E = sum(SPLIT_E)
IN_O = sum(SPLIT_O)
N_EVEN = (DEPTH_2 + 1) // 2
N_ODD = DEPTH_2 // 2


def _split(x, sizes):
    idx = [int(v) for v in np.cumsum(sizes)[:-1]]
    return jnp.split(x, idx, axis=-1)

def rmsnorm_2(x, g):
    xf = x.astype(jnp.float32)
    y = xf * lax.rsqrt(jnp.mean(xf * xf, axis=-1, keepdims=True) + RMS_EPS)
    return (y * g.astype(jnp.float32)).astype(x.dtype)

def rope_angles(pos, dim, theta):
    inv = jnp.power(theta, -jnp.arange(0, dim, 2, dtype=jnp.float32) / dim)
    return pos[:, None] * inv[None, :]

def rotate(x, ang):
    shp = (ang.shape[0],) + (1,) * (x.ndim - 3) + (ang.shape[1],)
    c = jnp.cos(ang).reshape(shp).astype(x.dtype)
    s = jnp.sin(ang).reshape(shp).astype(x.dtype)
    x1, x2 = jnp.split(x, 2, axis=-1)
    return jnp.concatenate([x1 * c - x2 * s, x2 * c + x1 * s], axis=-1)

def attend_blocks(q, k, v, scale):
    B, S, Hq, dq = q.shape
    Hk, dv = k.shape[2], v.shape[3]
    G = Hq // Hk
    nb = S // Q_BLOCK
    qb = q.reshape(B, nb, Q_BLOCK, Hk, G, dq).transpose(1, 0, 2, 3, 4, 5)

    def one(qi):
        s = jnp.einsum('bqhgd,bkhd->bhgqk', qi, k).astype(jnp.float32) * scale
        p = jax.nn.softmax(s, axis=-1).astype(v.dtype)
        return jnp.einsum('bhgqk,bkhd->bqhgd', p, v)

    o = lax.map(one, qb)
    return o.transpose(1, 0, 2, 3, 4, 5).reshape(B, S, Hq, dv)

def diff_attend_blocks(q1, q2, k1, k2, v, lam, scale):
    B, S, H, d = q1.shape
    nb = S // Q_BLOCK
    q1b = q1.reshape(B, nb, Q_BLOCK, H, d).transpose(1, 0, 2, 3, 4)
    q2b = q2.reshape(B, nb, Q_BLOCK, H, d).transpose(1, 0, 2, 3, 4)

    def one(args):
        a, b = args
        s1 = jnp.einsum('bqhd,bkhd->bhqk', a, k1).astype(jnp.float32) * scale
        s2 = jnp.einsum('bqhd,bkhd->bhqk', b, k2).astype(jnp.float32) * scale
        p = jax.nn.softmax(s1, axis=-1) - lam * jax.nn.softmax(s2, axis=-1)
        return jnp.einsum('bhqk,bkhd->bqhd', p.astype(v.dtype), v)

    o = lax.map(one, (q1b, q2b))
    return o.transpose(1, 0, 2, 3, 4).reshape(B, S, H, v.shape[-1])

def neighbourhood_attention(q, k, v, rpb):
    B, S, H, d = q.shape
    rows = S // GRID_W
    wr = min(WIN_R, rows)
    wc = WIN_C
    qg = q.reshape(B, rows, GRID_W, H, d)
    kg = k.reshape(B, rows, GRID_W, H, d)
    vg = v.reshape(B, rows, GRID_W, H, d)
    col = jnp.arange(GRID_W)
    c0 = jnp.clip(col - wc // 2, 0, GRID_W - wc)
    cidx = c0[:, None] + jnp.arange(wc)[None, :]
    cb = (cidx - col[:, None] + (WIN_C - 1))[:, None, :]
    scale = d ** -0.5

    def one(r):
        r0 = jnp.clip(r - wr // 2, 0, rows - wr)
        kr = lax.dynamic_slice_in_dim(kg, r0, wr, axis=1)
        vr = lax.dynamic_slice_in_dim(vg, r0, wr, axis=1)
        kw = kr[:, :, cidx]
        vw = vr[:, :, cidx]
        qr = lax.dynamic_index_in_dim(qg, r, axis=1, keepdims=False)
        s = jnp.einsum('bqhd,biqjhd->bhqij', qr, kw).astype(jnp.float32) * scale
        rb = (r0 + jnp.arange(wr) - r + (WIN_R - 1))[None, :, None]
        bias = rpb[:, rb, cb].astype(jnp.float32)
        s = (s + bias[None]).reshape(B, H, GRID_W, wr * wc)
        p = jax.nn.softmax(s, axis=-1).reshape(B, H, GRID_W, wr, wc).astype(v.dtype)
        return jnp.einsum('bhqij,biqjhd->bqhd', p, vw)

    o = lax.map(one, jnp.arange(rows))
    return o.transpose(1, 0, 2, 3, 4).reshape(B, S, H, d)

def even_layer(x, norm, w_in, gq_a, gk_a, rpb, gq_b, gk_b, w_out, ang_row, ang_col):
    B, S, _ = x.shape
    h = rmsnorm_2(x, norm)
    qa, ka, va, qb, kb, vb, gate = _split(h @ w_in, SPLIT_E)
    qa = rmsnorm_2(qa.reshape(B, S, H_A, D_HEAD), gq_a)
    ka = rmsnorm_2(ka.reshape(B, S, H_A, D_HEAD), gk_a)
    va = va.reshape(B, S, H_A, D_HEAD)
    oa = neighbourhood_attention(qa, ka, va, rpb)
    half = D_HEAD // 2
    qb = rmsnorm_2(qb.reshape(B, S, H_B, D_HEAD), gq_b)
    kb = rmsnorm_2(kb.reshape(B, S, H_B_KV, D_HEAD), gk_b)
    qb = jnp.concatenate([rotate(qb[..., :half], ang_row), rotate(qb[..., half:], ang_col)], -1)
    kb = jnp.concatenate([rotate(kb[..., :half], ang_row), rotate(kb[..., half:], ang_col)], -1)
    vb = vb.reshape(B, S, H_B_KV, D_HEAD)
    ob = attend_blocks(qb, kb, vb, D_HEAD ** -0.5)
    o = jnp.concatenate([oa.reshape(B, S, -1), ob.reshape(B, S, -1)], -1) * jax.nn.silu(gate)
    return o @ w_out

def odd_layer(x, norm, w_in, g_cq, w_cq_b, g_ckv, w_ckv_b, gq_c, gk_c, gq_d, gk_d,
              lam_q1, lam_k1, lam_q2, lam_k2, g_sub_d, w_out, ang_mla, ang_part, lam_init):
    B, S, _ = x.shape
    h = rmsnorm_2(x, norm)
    cq, ckv, kpe, qd, kd, vd, gate = _split(h @ w_in, SPLIT_O)
    q = (rmsnorm_2(cq, g_cq) @ w_cq_b).reshape(B, S, H_C, C_NOPE + C_ROPE)
    kv = (rmsnorm_2(ckv, g_ckv) @ w_ckv_b).reshape(B, S, H_C, C_NOPE + C_V)
    k_nope, v_c = kv[..., :C_NOPE], kv[..., C_NOPE:]
    k_pe = jnp.broadcast_to(kpe[:, :, None, :], (B, S, H_C, C_ROPE))
    qc = rmsnorm_2(q, gq_c)
    kc = rmsnorm_2(jnp.concatenate([k_nope, k_pe], -1), gk_c)
    qc = jnp.concatenate([qc[..., :C_NOPE], rotate(qc[..., C_NOPE:], ang_mla)], -1)
    kc = jnp.concatenate([kc[..., :C_NOPE], rotate(kc[..., C_NOPE:], ang_mla)], -1)
    oc = attend_blocks(qc, kc, v_c, (C_NOPE + C_ROPE) ** -0.5)
    qd = rmsnorm_2(qd.reshape(B, S, H_D, 2, D_HEAD), gq_d)
    kd = rmsnorm_2(kd.reshape(B, S, H_D, 2, D_HEAD), gk_d)
    qd = jnp.concatenate([rotate(qd[..., :ROT_DIM], ang_part), qd[..., ROT_DIM:]], -1)
    kd = jnp.concatenate([rotate(kd[..., :ROT_DIM], ang_part), kd[..., ROT_DIM:]], -1)
    vd = vd.reshape(B, S, H_D, D_V)
    f32 = jnp.float32
    lam = (jnp.exp(jnp.sum(lam_q1.astype(f32) * lam_k1.astype(f32)))
           - jnp.exp(jnp.sum(lam_q2.astype(f32) * lam_k2.astype(f32))) + lam_init)
    od = diff_attend_blocks(qd[:, :, :, 0], qd[:, :, :, 1], kd[:, :, :, 0], kd[:, :, :, 1],
                            vd, lam, D_HEAD ** -0.5)
    od = rmsnorm_2(od, g_sub_d) * (1.0 - lam_init)
    o = jnp.concatenate([oc.reshape(B, S, -1), od.reshape(B, S, -1)], -1) * jax.nn.silu(gate)
    return o @ w_out

def second_inputs(seed: int = 0) -> dict:
    key = jax.random.key(seed)
    ks = iter(jax.random.split(key, 32))
    f32 = jnp.float32

    def w(shape, fan_in):
        return jax.random.normal(next(ks), shape, f32) * (fan_in ** -0.5)

    def gain(shape):
        return 1.0 + 0.1 * jax.random.normal(next(ks), shape, f32)

    def small(shape, s):
        return s * jax.random.normal(next(ks), shape, f32)

    NE, NO = N_EVEN, N_ODD
    return {
        "x": jax.random.normal(next(ks), (BATCH, SEQ, D_MODEL), f32),
        "norm_e": gain((NE, D_MODEL)),
        "w_in_e": w((NE, D_MODEL, IN_E), D_MODEL),
        "gq_a": gain((NE, D_HEAD)),
        "gk_a": gain((NE, D_HEAD)),
        "rpb_a": small((NE, H_A, 2 * WIN_R - 1, 2 * WIN_C - 1), 0.2),
        "gq_b": gain((NE, D_HEAD)),
        "gk_b": gain((NE, D_HEAD)),
        "w_out_e": w((NE, GATE_E, D_MODEL), GATE_E),
        "norm_o": gain((NO, D_MODEL)),
        "w_in_o": w((NO, D_MODEL, IN_O), D_MODEL),
        "g_cq": gain((NO, Q_LORA)),
        "w_cq_b": w((NO, Q_LORA, H_C * (C_NOPE + C_ROPE)), Q_LORA),
        "g_ckv": gain((NO, KV_LORA)),
        "w_ckv_b": w((NO, KV_LORA, H_C * (C_NOPE + C_V)), KV_LORA),
        "gq_c": gain((NO, C_NOPE + C_ROPE)),
        "gk_c": gain((NO, C_NOPE + C_ROPE)),
        "gq_d": gain((NO, D_HEAD)),
        "gk_d": gain((NO, D_HEAD)),
        "lam_q1": small((NO, D_HEAD), 0.1),
        "lam_k1": small((NO, D_HEAD), 0.1),
        "lam_q2": small((NO, D_HEAD), 0.1),
        "lam_k2": small((NO, D_HEAD), 0.1),
        "g_sub_d": gain((NO, D_V)),
        "w_out_o": w((NO, GATE_O, D_MODEL), GATE_O),
    }

def second_block(x, norm_e, w_in_e, gq_a, gk_a, rpb_a, gq_b, gk_b, w_out_e,
              norm_o, w_in_o, g_cq, w_cq_b, g_ckv, w_ckv_b, gq_c, gk_c, gq_d, gk_d,
              lam_q1, lam_k1, lam_q2, lam_k2, g_sub_d, w_out_o):
    S = x.shape[1]
    t = jnp.arange(S)
    pos = t.astype(jnp.float32)
    row = (t // GRID_W).astype(jnp.float32)
    col = (t % GRID_W).astype(jnp.float32)
    half = D_HEAD // 2
    ang_row = rope_angles(row, half, AXIAL_THETA)
    ang_col = rope_angles(col, half, AXIAL_THETA)
    ang_mla = rope_angles(pos, C_ROPE, MLA_THETA)
    ang_part = rope_angles(pos, ROT_DIM, ROPE_THETA)
    for l in range(DEPTH_2):
        i = l // 2
        if l % 2 == 0:
            x = x + even_layer(x, norm_e[i], w_in_e[i], gq_a[i], gk_a[i], rpb_a[i],
                               gq_b[i], gk_b[i], w_out_e[i], ang_row, ang_col)
        else:
            lam_init = 0.8 - 0.6 * math.exp(-0.3 * l)
            x = x + odd_layer(x, norm_o[i], w_in_o[i], g_cq[i], w_cq_b[i], g_ckv[i],
                              w_ckv_b[i], gq_c[i], gk_c[i], gq_d[i], gk_d[i],
                              lam_q1[i], lam_k1[i], lam_q2[i], lam_k2[i], g_sub_d[i],
                              w_out_o[i], ang_mla, ang_part, lam_init)
    return x


def setup_inputs(seed=0):
    out = dict(first_inputs(seed))
    for name, value in second_inputs(seed + 1).items():
        if name != "x":
            out[name + "_2"] = value
    return out


def reference(
    x, norm_mix_w, w_in, hgrn_lower_bounds, hgrn_norm_w, ssd_conv_w, ssd_conv_b, ssd_dt_bias,
    ssd_a_log, ssd_d, ssd_norm_w, gla_gate_w, gla_gate_b, gla_norm_w, lru_conv_w, lru_conv_b,
    lru_wa, lru_ba, lru_wx, lru_bx, lru_lambda, w_branch, w_out, norm_ffn_w, w_ffn_in,
    w_ffn_out, norm_f_w, norm_e_2, w_in_e_2, gq_a_2, gk_a_2, rpb_a_2, gq_b_2, gk_b_2, w_out_e_2,
    norm_o_2, w_in_o_2, g_cq_2, w_cq_b_2, g_ckv_2, w_ckv_b_2, gq_c_2, gk_c_2, gq_d_2, gk_d_2,
    lam_q1_2, lam_k1_2, lam_q2_2, lam_k2_2, g_sub_d_2, w_out_o_2,
):
    x = first_block(
        x, norm_mix_w, w_in, hgrn_lower_bounds, hgrn_norm_w, ssd_conv_w, ssd_conv_b,
        ssd_dt_bias, ssd_a_log, ssd_d, ssd_norm_w, gla_gate_w, gla_gate_b, gla_norm_w,
        lru_conv_w, lru_conv_b, lru_wa, lru_ba, lru_wx, lru_bx, lru_lambda, w_branch, w_out,
        norm_ffn_w, w_ffn_in, w_ffn_out, norm_f_w,
    )
    return second_block(
        x, norm_e_2, w_in_e_2, gq_a_2, gk_a_2, rpb_a_2, gq_b_2, gk_b_2, w_out_e_2, norm_o_2,
        w_in_o_2, g_cq_2, w_cq_b_2, g_ckv_2, w_ckv_b_2, gq_c_2, gk_c_2, gq_d_2, gk_d_2,
        lam_q1_2, lam_k1_2, lam_q2_2, lam_k2_2, g_sub_d_2, w_out_o_2,
    )


_drawn_inputs = setup_inputs


def setup_inputs(seed=0):
    import zlib

    import numpy as np

    out = dict(_drawn_inputs(seed))
    spreads = {}
    factors = {'gla_gate_b': 3.336,
     'lru_ba': 8.0,
     'lru_bx': 5.877,
     'norm_e_2': 3.571,
     'gq_a_2': 8.0,
     'gk_a_2': 8.0,
     'rpb_a_2': 4.7,
     'gq_b_2': 8.0,
     'gk_b_2': 8.0,
     'g_cq_2': 8.0,
     'g_ckv_2': 7.996,
     'gq_c_2': 8.0,
     'gk_c_2': 8.0,
     'gq_d_2': 21.64,
     'lam_q1_2': 16.159,
     'lam_k1_2': 34.712,
     'lam_k2_2': 42.564,
     'gk_d_2': 8.0,
     'g_sub_d_2': 8.0}
    for name, (base, spread) in spreads.items():
        noise = np.random.default_rng([zlib.crc32(name.encode()), seed]).standard_normal(out[name].shape)
        drawn = base * np.exp(spread * noise) if base else spread * noise
        out[name] = __import__('jax').numpy.asarray(drawn.astype(out[name].dtype))
    for name, factor in factors.items():
        out[name] = (out[name] * factor).astype(out[name].dtype)
    return out
```

```python
from contextlib import ExitStack
import math
import numpy as np
import concourse.bass as bass
from concourse import mybir

F32 = mybir.dt.float32
I32 = mybir.dt.int32
ALU = mybir.AluOpType
ACT = mybir.ActivationFunctionType
AX = mybir.AxisListType

P = 128
D = 1024
L = 1024
KD = D // P
NT = L // P
EPS = 1e-6

HQ, HF, HI, HG = 0, 512, 1024, 1536
SZ, SX, SDT = 2048, 2560, 3328
GQ, GK, GV, GG, GLR = 3336, 3592, 3848, 4360, 4872
LX, LG, MG = 4888, 5400, 5912
DFF = 2816
NF = DFF // P
EQA, EKA, EVA, EQB, EKB, EVB, EG = 0, 512, 1024, 1536, 2048, 2176, 2304
OCQ, OCKV, OKPE, OQD, OKD, OVD, OG = 0, 256, 384, 416, 928, 1440, 1952
LAM_INIT = 0.8 - 0.6 * math.exp(-0.3)
LAG = 2
POST = 5
NLEV = 7

PC = {}
_at = 0
for _name, _n in [("nmix", 8), ("nffn", 8), ("nf", 8), ("ne", 8), ("no", 8), ("hnw", 1), ("gnw", 1),
                  ("scw", 24), ("scb", 6), ("lcw", 16), ("lcb", 4), ("ba", 4), ("bx", 4), ("lam", 4),
                  ("gb", 2), ("sd", 4), ("snw", 4), ("dtb", 1), ("alog", 1), ("gqa", 1), ("gka", 1),
                  ("gqb", 1), ("gkb", 1), ("gcq", 2), ("gckv", 1), ("gqc", 1), ("gkc", 1), ("gqd", 1),
                  ("gkd", 1), ("gsub", 1), ("lq1", 1), ("lk1", 1), ("lq2", 1), ("lk2", 1)]:
    PC[_name] = _at
    _at += _n
NPAR = _at
CM = {n: i * P for i, n in enumerate(["ident", "tri", "neg", "blk64", "o1024", "o128", "o256", "o96",
                                      "one", "pB", "pC", "pD"])}
CNB = len(CM) * P
CEPS = CNB + 64
CONE = CEPS + 1
NCST = CONE + 1



def build(nc, a):
    with ExitStack() as ctx:
        def sb(name, shape, dt=F32):
            return ctx.enter_context(nc.sbuf_tensor(name, shape, dt))

        H = sb("H", [P, KD, L])
        XN = sb("XN", [P, KD, L])
        AR = sb("AR", [P, 29, L])
        WR = sb("WR", [P, 4, 8, P])
        CST = sb("CST", [P, NCST])
        MSK = sb("MSK", [P, NLEV + 1, P], I32)
        PAR = sb("PAR", [P, NPAR])
        SM = sb("SM", [P, 40])
        PS = [ctx.enter_context(nc.psum_tensor(f"ps{i}", [P, L], F32)) for i in range(4)]
        def sem(name):
            return ctx.enter_context(nc.semaphore(name))

        s_cst_in = sem("cst_in")
        s_dve_step = sem("dve_step")
        s_act_step = sem("act_step")
        s_nsq = sem("nsq")
        s_nsq_used = sem("nsq_used")
        s_normed = sem("normed")
        s_conv = sem("conv")
        s_ssd_silu = sem("ssd_silu")
        s_dt_ln = sem("dt_ln")
        s_dt_done = sem("dt_done")
        s_nega = sem("nega")
        s_dec_in = sem("dec_in")
        s_dec_ready = sem("dec_ready")
        s_xdt = sem("xdt")
        s_ea = sem("ea")
        s_segm = sem("segm")
        s_lmat = sem("lmat")
        s_mc = sem("mc")
        s_yz = sem("yz")
        s_ysq = sem("ysq")
        s_ys = sem("ys")
        s_ssd_state = sem("ssd_state")
        s_lnr = sem("lnr")
        s_expo = sem("expo")
        s_expd = sem("expd")
        s_xlev = sem("xlev")
        s_kdec = sem("kdec")
        s_qdec = sem("qdec")
        s_a_done = sem("a_done")
        s_g_state = sem("g_state")
        s_osq = sem("osq")
        s_bd_zero = sem("bd_zero")
        s_bd_in = sem("bd_in")
        s_lru_t = sem("lru_t")
        s_lru_q = sem("lru_q")
        s_lru_b = sem("lru_b")
        s_lsp_in = sem("lsp_in")
        s_merge_add = sem("merge_add")
        s_hn_done = sem("hn_done")
        s_rope_tmp = sem("rope_tmp")
        s_tab_in = sem("tab_in")
        s_vs_in = sem("vs_in")
        s_bias_in = sem("bias_in")
        s_negmax = sem("negmax")
        s_pexp = sem("pexp")
        s_probs = sem("probs")
        s_qbd = sem("qbd")
        s_kz = sem("kz")
        s_lam_e = sem("lam_e")
        s_out_in = sem("out_in")
        s_pre_f = sem("pre_f")
        s_kraw = sem("kraw")
        s_od_done = sem("od_done")
        s_lamv = sem("lamv")
        filled = [ctx.enter_context(nc.semaphore(f"filled{i}")) for i in range(4)]
        freed = [ctx.enter_context(nc.semaphore(f"freed{i}")) for i in range(4)]
        w_in = [ctx.enter_context(nc.semaphore(f"w_in{i}")) for i in range(4)]

        def A(i):
            return AR[:, i, :]

        def par(name, j=0, p=P):
            c = PC[name] + j
            return PAR[0:p, c:c + 1]

        def cm(name, p=P, q=P):
            return CST[0:p, CM[name]:CM[name] + q]

        IDENT = cm("ident")
        QBD = AR[:, 4:6, :].rearrange("p a (r c) -> p (a r) c", c=P)
        MSKF = MSK[:, :, :].rearrange("p a b -> p (a b)").bitcast(F32)
        epsc = CST[:, CEPS:CEPS + 1]

        def tt(ap):
            return ap.rearrange("p (t i) -> p t i", i=P)

        J = {}
        njobs = [0]
        WL = []
        nw = [0]

        def bank(name):
            return J[name] % 4

        def turn(name):
            return J[name] // 4 + 1

        block = ctx.enter_context(nc.Block())

        def weave(main, side):
            main, side = iter(main), iter(side)
            for _ in main:
                next(side, None)
            for _ in side:
                pass

        def chain(steps, *preps):
            for prep in preps:
                n = 0
                for _ in prep:
                    n += 1
                    yield
                assert n <= steps
                for _ in range(steps - n):
                    yield

        win, wbr, wout, wfi, wfo = a["w_in"][0], a["w_branch"][0], a["w_out"][0], a["w_ffn_in"][0], a["w_ffn_out"][0]
        wie, woe, wio, woo = a["w_in_e_2"][0], a["w_out_e_2"][0], a["w_in_o_2"][0], a["w_out_o_2"][0]
        wcq, wckv = a["w_cq_b_2"][0], a["w_ckv_b_2"][0]

        def cols(w, c0, m=P, k0=0, nk=8):
            return w[k0 * P:(k0 + nk) * P, c0:c0 + m].rearrange("(k p) c -> p k c", p=P)

        @block.tensor
        def _(pe):
            def opn(name):
                n = njobs[0]
                njobs[0] += 1
                assert name not in J, name
                J[name] = n
                return PS[n % 4], n

            def weight(src, n, m=P, kp=P, nk=8, dup=False):
                w = nw[0]
                nw[0] += 1
                WL.append((src, n, m, kp, nk, dup))
                pe.wait_ge(w_in[w % 4], 16 * (1 + dup) * 0 + 16 * (w // 4 + 1))
                return WR[:, w % 4]

            def gemm(name, src, rhs=None, m=P, kp=P, nk=8, dup=False, o0=0, ps=None):
                rhs = rhs or (lambda k: XN[:, k, :])
                if ps is None:
                    pt, n = opn(name)
                    pe.wait_ge(freed[n % 4], n // 4)
                else:
                    pt, n = ps
                wt = weight(src, n, m, kp, nk, dup)
                for h in range(2):
                    for k in range(nk):
                        mm = pe.matmul(pt[o0:o0 + m, h * 512:h * 512 + 512], wt[0:kp, k, 0:m],
                                       rhs(k)[0:kp, h * 512:h * 512 + 512], start=k == 0, stop=k == nk - 1)
                if ps is None:
                    mm.then_inc(filled[n % 4], 1)

            def transposes(name, src, p=P, m=P):
                pt, n = opn(name)
                pe.wait_ge(freed[n % 4], n // 4)
                for t in range(NT):
                    mm = pe.transpose(pt[:, t * P:t * P + P], src[:, t * P:t * P + P], IDENT)
                mm.then_inc(filled[n % 4], 1)

            def reduce_job(name, mat, srcs, m=P):
                pt, n = opn(name)
                pe.wait_ge(freed[n % 4], n // 4)
                for h in range(2):
                    for i, s in enumerate(srcs):
                        mm = pe.matmul(pt[0:m, h * 512:h * 512 + 512], mat, s[0:m, h * 512:h * 512 + 512],
                                       start=i == 0, stop=i == len(srcs) - 1)
                mm.then_inc(filled[n % 4], 1)

            def norm(i):
                pt, n = opn(("norm", i))
                pe.wait_ge(freed[n % 4], n // 4)
                for k in range(KD):
                    pe.wait_ge(s_nsq, i * KD + k + 1)
                    for h in range(2):
                        mm = pe.matmul(pt[:, h * 512:h * 512 + 512], cm("o1024"),
                                       A(26 + k % 2)[:, h * 512:h * 512 + 512], start=k == 0, stop=k == KD - 1)
                    if k < KD - 1:
                        mm.then_inc(s_nsq_used, 1)
                mm.then_inc(filled[n % 4], 1)

            pe.wait_ge(s_cst_in, 16 * 11)
            for f in range(KD):
                pt, n = opn(("x", f))
                if n >= 4:
                    pe.wait_ge(freed[n % 4], n // 4)
                for t in range(NT):
                    mm = pe.transpose(pt[:, t * P:t * P + P], AR[:, t, f * P:f * P + P], IDENT)
                mm.then_inc(filled[n % 4], 1)
            norm(0)
            pe.wait_ge(s_normed, KD)

            for f in range(4):
                gemm(("z", f), cols(win, SZ + f * P))
            for f in range(6):
                gemm(("sx", f), cols(win, SX + f * P))
            gemm(("dt",), cols(win, SDT, 8), m=8)
            for f in range(4):
                pe.wait_ge(s_ssd_silu, f + 1)
                if f == 0:
                    pe.wait_ge(s_dt_done, 1)
                    pt, n = opn(("dtt",))
                    pe.wait_ge(freed[n % 4], n // 4)
                    for i, src in enumerate((A(0), A(2))):
                        for t in range(NT):
                            mm = pe.matmul(pt[:, i * 64 + t * 8:i * 64 + t * 8 + 8], src[0:8, t * P:t * P + P],
                                           IDENT[0:8, 0:8], start=True, stop=True)
                    mm.then_inc(filled[n % 4], 1)
                    pe.wait_ge(freed[bank(("dtt",))], turn(("dtt",)))
                    pt, n = opn(("acs",))
                    pe.wait_ge(freed[n % 4], n // 4)
                    pe.matmul(pt[:, 0:64], cm("tri"), A(27)[:, 64:128], start=True, stop=True)
                    mm = pe.matmul(pt[:, 64:128], cm("one"), A(27)[:, 64:128], start=True, stop=True)
                    mm.then_inc(filled[n % 4], 1)
                transposes(("xt", f), A(8 + f))
            pe.wait_ge(s_ssd_silu, 6)
            transposes(("Bt",), A(12))
            for g in range(2):
                pt, n = opn(("CB", g))
                pe.wait_ge(freed[n % 4], n // 4)
                q = slice(g * 64, g * 64 + 64)
                for t in range(NT):
                    mm = pe.matmul(pt[:, t * P:t * P + P], A(12)[q, t * P:t * P + P], A(13)[q, t * P:t * P + P],
                                   start=True, stop=True)
                mm.then_inc(filled[n % 4], 1)
            pe.wait_ge(freed[bank(("Bt",))], turn(("Bt",)))
            pe.wait_ge(s_xdt, 4)
            xdt = AR[:, 17:21, :].rearrange("p a (b c) -> p (a b) c", c=512)
            xdd = AR[:, 21:25, :].rearrange("p a (b c) -> p (a b) c", c=512)
            sst = AR[:, 0:4, :].rearrange("p a (b c) -> p (a b) c", c=512)
            for j in range(4):
                pt, n = opn(("sU", j))
                pe.wait_ge(freed[n % 4], n // 4)
                for i in range(2 if j < 3 else 1):
                    t = 2 * j + i
                    mm = pe.matmul(pt[:, i * 512:i * 512 + 512], A(14)[:, t * P:t * P + P], xdd[:, t, :],
                                   start=True, stop=True)
                mm.then_inc(filled[n % 4], 1)

            def seg(h):
                pt, n = opn(("seg", h))
                pe.wait_ge(freed[n % 4], n // 4)
                for t in range(NT):
                    c = 64 + t * 8 + h
                    mm = pe.matmul(pt[:, t * P:t * P + P], A(27)[:, c:c + 1].to_broadcast([P, P]), cm("tri"),
                                   start=True, stop=True)
                mm.then_inc(filled[n % 4], 1)
            seg(0)
            seg(1)
            for f in range(4):
                if f < 3:
                    seg(2 * f + 2)
                pe.wait_ge(s_mc, 2 * f + 2)
                pe.wait_ge(s_ssd_state, 7)
                pt, n = opn(("y", f))
                pe.wait_ge(freed[n % 4], n // 4)
                for hh in range(2):
                    h = 2 * f + hh
                    g = slice((h // 4) * 64, (h // 4) * 64 + 64)
                    o = slice(hh * 64, hh * 64 + 64)
                    for t in range(NT):
                        c = slice(t * P, t * P + P)
                        mm = pe.matmul(pt[o, c], xdt[:, t, h * 64:h * 64 + 64], A(21 + hh)[:, c],
                                       start=True, stop=t == 0)
                        if t:
                            mm = pe.matmul(pt[o, c], sst[g, t, h * 64:h * 64 + 64], A(23 + hh)[g, c],
                                           start=False, stop=True)
                mm.then_inc(filled[n % 4], 1)
                if f < 3:
                    seg(2 * f + 3)
                if f % 2:
                    pe.wait_ge(s_ysq, f + 1)
                    reduce_job(("yn", f // 2), cm("o256"), [A(12), A(14)])

            for u in range(6):
                nh = 1 if u < 4 else 2
                if u < 4:
                    gemm(("q", u), cols(win, HQ + u * P))
                    gemm(("k", u), cols(win, HF + u * P))
                    vc, gc = [HI + u * P], [HG + u * P]
                else:
                    w = u - 4
                    if w == 0:
                        gemm(("glr",), cols(win, GLR, 16), m=16)
                    gemm(("q", u), cols(win, GQ + w * P))
                    gemm(("k", u), cols(win, GK + w * P))
                    pe.wait_ge(freed[bank(("glr",))], turn(("glr",)))
                    gemm(("gz", u), a["gla_gate_w"][0][:, w * P:w * P + P], rhs=lambda k: A(11), kp=16, nk=1)
                    vc = [GV + (2 * w + hh) * P for hh in range(2)]
                    gc = [GG + (2 * w + hh) * P for hh in range(2)]
                for hh in range(nh):
                    gemm(("g", u, hh), cols(win, gc[hh]))
                for hh in range(nh):
                    gemm(("v", u, hh), cols(win, vc[hh]))
                    pe.wait_ge(freed[bank(("v", u, hh))], turn(("v", u, hh)))
                    transposes(("vt", u, hh), A(24))
                dk = P // nh
                pe.wait_ge(freed[bank(("q", u))], turn(("q", u)))
                pe.wait_ge(freed[bank(("k", u))], turn(("k", u)))
                for l in range(-1, NLEV):
                    if l >= 0:
                        pe.wait_ge(s_xlev, u * NLEV + l + 1)
                    x1, x2 = (A(17), A(16)) if l < 0 else (A(21 + l % 2),) * 2
                    for hh in range(nh):
                        pt, n = opn(("P", u, l, hh))
                        pe.wait_ge(freed[n % 4], n // 4)
                        r = slice(hh * dk, hh * dk + dk)
                        for t in range(NT):
                            c = slice(t * P, t * P + P)
                            mm = pe.matmul(pt[:, c], x1[r, c], x2[r, c], start=True, stop=True)
                        mm.then_inc(filled[n % 4], 1)
                pe.wait_ge(s_kdec, u + 1)
                transposes(("kdt", u), A(15))
                pe.wait_ge(freed[bank(("kdt", u))], turn(("kdt", u)))
                vtok = [A(25), A(13)]
                for hh in range(nh):
                    pe.wait_ge(freed[bank(("vt", u, hh))], turn(("vt", u, hh)))
                pt, n = opn(("U", u))
                pe.wait_ge(freed[n % 4], n // 4)
                for hh in range(nh):
                    for t in range(NT - 1):
                        c = slice(t * P, t * P + P)
                        mm = pe.matmul(pt[hh * dk:hh * dk + dk, c], A(27)[:, t * P + hh * dk:t * P + hh * dk + dk],
                                       vtok[hh][:, c], start=True, stop=True)
                mm.then_inc(filled[n % 4], 1)
                pe.wait_ge(s_a_done, u + 1)
                pe.wait_ge(s_g_state, u + 1)
                for hh in range(nh):
                    am = [A(23), A(12)][hh]
                    r = slice(hh * dk, hh * dk + dk)
                    pt, n = opn(("o", u, hh))
                    pe.wait_ge(freed[n % 4], n // 4)
                    for t in range(NT):
                        c = slice(t * P, t * P + P)
                        mm = pe.matmul(pt[:, c], vtok[hh][:, c], am[:, c], start=True, stop=t == 0)
                        if t:
                            mm = pe.matmul(pt[:, c], A(19)[r, c], A(16)[r, c], start=False, stop=True)
                    mm.then_inc(filled[n % 4], 1)
                    pe.wait_ge(freed[bank(("o", u, hh))], turn(("o", u, hh)))
                    reduce_job(("on", u, hh), cm("o128"), [A(21)])

            for f in range(4):
                gemm(("lx", f), cols(win, LX + f * P))
                gemm(("lg", f), cols(win, LG + f * P))
                pe.wait_ge(s_conv, 6 + f + 1)
                pe.wait_ge(s_bd_in, 64)
                for i, nm in enumerate(("lr", "li")):
                    pt, n = opn((nm, f))
                    pe.wait_ge(freed[n % 4], n // 4)
                    for h in range(2):
                        mm = pe.matmul(pt[:, h * 512:h * 512 + 512], A(20)[:, (i * 4 + f) * P:(i * 4 + f) * P + P],
                                       A(17)[:, h * 512:h * 512 + 512], start=True, stop=True)
                    mm.then_inc(filled[n % 4], 1)
            pe.wait_ge(s_ys, 16)

            def run(name, iters, jobs):
                n0, w0 = njobs[0], nw[0]
                nj = len(jobs)
                nwt = sum(len(ws) for ws, _ in jobs)
                assert nj % 4 == 0 and nwt % 4 == 0
                J[name] = n0
                body = []
                for k, (ws, _) in enumerate(jobs):
                    for src, nk in ws:
                        body.append((src, n0 + k, nk))
                WL.append(("run", iters, nj, body))
                njobs[0] += nj * iters
                nw[0] += nwt * iters
                with pe.Fori(0, iters) as i:
                    w = w0
                    for k, (ws, rhs) in enumerate(jobs):
                        n = n0 + k
                        pe.wait_ge(freed[n % 4], i * (nj // 4) + n // 4)
                        pt = PS[n % 4]
                        tot = sum(nk for _, nk in ws)
                        at = 0
                        for src, nk in ws:
                            pe.wait_ge(w_in[w % 4], i * (nwt // 4 * 16) + 16 * (w // 4 + 1))
                            wt = WR[:, w % 4]
                            for h in range(2):
                                for kk in range(nk):
                                    c = at + kk
                                    mm = pe.matmul(pt[:, h * 512:h * 512 + 512], wt[:, kk, :],
                                                   rhs(c)[:, h * 512:h * 512 + 512],
                                                   start=c == 0, stop=c == tot - 1)
                            at += nk
                            w += 1
                        mm.then_inc(filled[n % 4], 1)

            xn = lambda k: XN[:, k, :]
            jobs = []
            for b in range(4):
                jobs.append(([(lambda i, b=b: (win, MG + b * D, i, 1, 0), 8)], xn))
                jobs.append(([(lambda i, b=b: (wbr[b], 0, i, 1, 0), 4)], lambda k, b=b: A(4 * b + k)))
            run("merge", KD, jobs)

            def proj(name, w, rhs, chunks):
                run(name, 2, [([(lambda i, j=j, k0=k0: (w, j * P, i, 4, k0), nk) for k0, nk in chunks], rhs)
                              for j in range(4)])
            n = J["merge"] + 8 * KD - 1
            pe.wait_ge(s_merge_add, 3 * KD)
            proj("wout", wout, lambda k: A(16 + k), [(0, 8)])
            norm(1)
            pe.wait_ge(s_normed, 2 * KD)
            run("ffn_in", NF // 2, [([(lambda i, j=j, s=s: (wfi, s * DFF + j * P, i, 2, 0), 8)], xn)
                                    for j in range(2) for s in range(2)])
            for k in range(4):
                n = J["ffn_in"] + 2 * NF - 4 + k
                pe.wait_ge(freed[n % 4], n // 4 + 1)
            proj("ffn_out", wfo, lambda k: A(k), [(0, 8), (8, 8), (16, 6)])
            norm(2)

            def headnorm(i, name, mat, src, m=P):
                reduce_job(("hn", i), mat, [src], m)

            def rope(i, mat, x, m=P):
                pe.wait_ge(s_hn_done, i + 1)
                pt, n = opn(("rope", i))
                pe.wait_ge(freed[n % 4], n // 4)
                for h in range(2):
                    mm = pe.matmul(pt[0:m, h * 512:h * 512 + 512], mat, x[0:m, h * 512:h * 512 + 512],
                                   start=True, stop=True)
                mm.then_inc(filled[n % 4], 1)

            cnt = {"hn": 0, "s": 0, "unit": 0}

            def hn(name, mat, m=P):
                pe.wait_ge(freed[bank(name)], turn(name))
                reduce_job(("hn", cnt["hn"]), mat, [A(22)], m)
                cnt["hn"] += 1

            def prep_a(p):
                gemm(("qa", p), cols(wie, EQA + p * P))
                yield
                hn(("qa", p), cm("blk64"))
                gemm(("ka", p), cols(wie, EKA + p * P))
                yield
                hn(("ka", p), cm("blk64"))
                gemm(("va", p), cols(wie, EVA + p * P))
                yield
                pe.wait_ge(freed[bank(("va", p))], turn(("va", p)))
                transposes(("vat", p), A(27))
                yield
                gemm(("ga", p), cols(wie, EG + p * P))
                yield

            def prep_bkv():
                for j in range(2):
                    gemm(("kb", j), cols(wie, EKB + j * 64, 64), dup=True)
                    hn(("kb", j), cm("blk64"))
                    rope(cnt["hn"] - 1, cm("pB"), A(10 + j))
                gemm(("vb",), cols(wie, EVB))
                pe.wait_ge(freed[bank(("vb",))], turn(("vb",)))
                transposes(("vbt",), A(27))
                yield

            def prep_b(p):
                gemm(("qb", p), cols(wie, EQB + p * P))
                yield
                hn(("qb", p), cm("blk64"))
                gemm(("gb", p), cols(wie, EG + 512 + p * P))
                yield
                rope(cnt["hn"] - 1, cm("pB"), A(8 + p % 2))
                yield

            def prep_c0():
                gemm(("cq", 0), cols(wio, OCQ))
                gemm(("cq", 1), cols(wio, OCQ + P))
                pe.wait_ge(freed[bank(("cq", 0))], turn(("cq", 0)))
                pe.wait_ge(freed[bank(("cq", 1))], turn(("cq", 1)))
                reduce_job(("hn", cnt["hn"]), cm("o256"), [A(22), A(24)])
                cnt["hn"] += 1
                gemm(("ckv",), cols(wio, OCKV))
                hn(("ckv",), cm("o128"))
                gemm(("kpe",), cols(wio, OKPE, 32), m=32, o0=64)
                pe.wait_ge(s_hn_done, cnt["hn"])
                yield

            def prep_c(h):
                gemm(("qc", h), cols(wcq, h * 96, 96, nk=2), rhs=lambda k: A(18 + k), m=96, nk=2)
                yield
                hn(("qc", h), cm("o96", 96, 96), 96)
                if h % 2 == 0:
                    gemm(("gc", h // 2), cols(wio, OG + h // 2 * P))
                yield
                rope(cnt["hn"] - 1, cm("pC", 96, 96), A(8 + h % 2), 96)
                gemm(("kc", h), cols(wckv, h * 128, 64, nk=1), rhs=lambda k: A(28), m=64, nk=1)
                yield
                pe.wait_ge(s_kraw, h + 1)
                reduce_job(("hn", cnt["hn"]), cm("o96", 96, 96), [A(22)], 96)
                cnt["hn"] += 1
                yield
                rope(cnt["hn"] - 1, cm("pC", 96, 96), A(10 + h % 2), 96)
                yield
                if h % 2 == 0:
                    p = h // 2
                    src = wckv.rearrange("k (h c) -> k h c", c=128)[:, 2 * p:2 * p + 2, 64:128]
                    gemm(("vc", p), src, rhs=lambda k: A(28), nk=1)
                yield
                if h % 2 == 0:
                    pe.wait_ge(freed[bank(("vc", p))], turn(("vc", p)))
                    transposes(("vct", p), A(27))
                yield
                yield

            def prep_d(h):
                gemm(("qd", h), cols(wio, OQD + h * P))
                yield
                hn(("qd", h), cm("blk64"))
                gemm(("kd", h), cols(wio, OKD + h * P))
                yield
                rope(cnt["hn"] - 1, cm("pD"), A(8 + h % 2))
                yield
                hn(("kd", h), cm("blk64"))
                yield
                rope(cnt["hn"] - 1, cm("pD"), A(10 + h % 2))
                gemm(("vd", h), cols(wio, OVD + h * P))
                yield
                pe.wait_ge(freed[bank(("vd", h))], turn(("vd", h)))
                transposes(("vdt", h), A(27))
                yield
                gemm(("gd", h), cols(wio, OG + 512 + h * P))
                yield
                yield

            def attend(kind, units, q, k, v, dk, ready, o0, dv):
                nu = len(units)
                base = cnt["unit"]
                nm = 2 if kind == "D" else 1
                for s in range(nu + LAG + 1 + (3 if kind == "D" else 0)):
                    if s < nu:
                        un = units[s]
                        if un[2] == 0:
                            ready(un[1])
                        for m in range(nm):
                            pt, n = opn(("S", base + s, m))
                            pe.wait_ge(freed[n % 4], n // 4)
                            if kind == "A":
                                for rr in range(2):
                                    r = 2 * un[2] + rr
                                    r0 = min(max(r - 4, 0), 8)
                                    mm = pe.matmul(pt[:, rr * 512:rr * 512 + 512], QBD[:, r, :],
                                                   k(un)[:, r0 * 64:r0 * 64 + 512], start=True, stop=True)
                            else:
                                for h in range(2):
                                    mm = pe.matmul(pt[:, h * 512:h * 512 + 512],
                                                   q(un)[0:dk, un[2] * P:un[2] * P + P],
                                                   k(un, m)[0:dk, h * 512:h * 512 + 512], start=True, stop=True)
                            mm.then_inc(filled[n % 4], 1)
                    if LAG <= s < nu + LAG:
                        b = base + s - LAG
                        pe.wait_ge(s_probs, b + 1)
                        pt, n = opn(("T", b))
                        pe.wait_ge(freed[n % 4], n // 4)
                        pr = A(16 + (b % 2) * nm)
                        for c in range(NT):
                            mm = pe.transpose(pt[:, c * P:c * P + P], pr[:, c * P:c * P + P], IDENT)
                        mm.then_inc(filled[n % 4], 1)
                    if LAG + 1 <= s < nu + LAG + 1:
                        b = base + s - LAG - 1
                        un = units[s - LAG - 1]
                        pe.wait_ge(freed[bank(("T", b))], turn(("T", b)))
                        pt, n = opn(("O", b))
                        pe.wait_ge(freed[n % 4], n // 4)
                        pT = A(20 + b % 2)
                        if kind == "A":
                            for rr in range(2):
                                r = 2 * un[2] + rr
                                r0 = min(max(r - 4, 0), 8)
                                vt = (A(12 + un[1] % 2) if r0 % 2 == 0 else A(18 + un[1] % 2))
                                for c in range(4):
                                    x0 = (r0 // 2 + c) * P
                                    y0 = (rr * 4 + c) * P
                                    mm = pe.matmul(pt[:, rr * P:rr * P + P], vt[:, x0:x0 + P],
                                                   pT[:, y0:y0 + P], start=c == 0, stop=c == 3)
                        else:
                            oo = o0(un)
                            for c in range(NT):
                                mm = pe.matmul(pt[oo:oo + dv, 0:P], v(un, c), pT[:, c * P:c * P + P],
                                               start=c == 0, stop=c == NT - 1)
                        mm.then_inc(filled[n % 4], 1)
                    yield
                cnt["unit"] += nu

            def att_a():
                def ready(p):
                    pe.wait_ge(s_qbd, p + 1)
                    pe.wait_ge(s_vs_in, 32 * (p + 1))
                return attend("A", [("A", p, u) for p in range(4) for u in range(8)], None,
                              lambda un: A(10 + un[1] % 2), None, None, ready, None, P)

            def att_b():
                def ready(h):
                    pe.wait_ge(s_rope_tmp, 2 + h // 2 + 1)
                    pe.wait_ge(s_kz, 2)
                return attend("B", [("B", h, u) for h in range(8) for u in range(8)],
                              lambda un: A(8 + un[1] // 2 % 2), lambda un, m: A([10, 18][un[1] % 2] + un[1] // 4),
                              lambda un, c: A(12)[:, c * P + un[1] // 4 * 64:c * P + un[1] // 4 * 64 + 64],
                              P, ready, lambda un: (un[1] % 2) * 64, 64)

            def att_c():
                def ready(h):
                    pe.wait_ge(s_rope_tmp, 6 + 2 * h + 2)
                    pe.wait_ge(freed[bank(("vct", h // 2))], turn(("vct", h // 2)))
                return attend("C", [("C", h, u) for h in range(8) for u in range(8)],
                              lambda un: A(8 + un[1] % 2), lambda un, m: A(10 + un[1] % 2),
                              lambda un, c: A(12 + un[1] // 2 % 2)[:, c * P + un[1] % 2 * 64:c * P + un[1] % 2 * 64 + 64],
                              96, ready, lambda un: (un[1] % 2) * 64, 64)

            def att_d():
                def ready(h):
                    pe.wait_ge(s_kz, 2 + h + 1)
                    pe.wait_ge(freed[bank(("vdt", h))], turn(("vdt", h)))
                steps = attend("D", [("D", h, u) for h in range(4) for u in range(8)], lambda un: A(8 + un[1] % 2),
                               lambda un, m: (A(10 + un[1] % 2), (A(24), MSKF)[un[1] % 2])[m],
                               lambda un, c: A(12 + un[1] % 2)[:, c * P:c * P + P], P, ready, lambda un: 0, 128)
                for s, _ in enumerate(steps):
                    yield
                    if s >= 8 and s % 8 == POST:
                        h = s // 8 - 1
                        pe.wait_ge(s_osq, h + 1)
                        reduce_job(("odn", h), cm("o128"), [A(22)])

            norm(3)
            pe.wait_ge(s_normed, 4 * KD)
            weave(prep_a(0), ())
            weave(att_a(), chain(8, prep_a(1), prep_a(2), prep_a(3)))
            weave(prep_bkv(), ())
            weave(prep_b(0), ())
            weave(att_b(), chain(16, prep_b(1), prep_b(2), prep_b(3)))
            pe.wait_ge(s_od_done, 32 + 64)
            proj("wout_e", woe, lambda k: A(k), [(0, 8)])
            norm(4)
            pe.wait_ge(s_normed, 5 * KD)
            pe.wait_ge(s_lam_e, 1)
            pt, n = opn(("lam",))
            pe.wait_ge(freed[n % 4], n // 4)
            mm = pe.matmul(pt[:, 0:2], cm("one", 64), SM[0:64, 30:32], start=True, stop=True)
            mm.then_inc(filled[n % 4], 1)
            weave(prep_c0(), ())
            weave(prep_c(0), ())
            weave(att_c(), chain(8, *[prep_c(h) for h in range(1, 8)]))
            weave(prep_d(0), ())
            weave(att_d(), chain(8, *[prep_d(h) for h in range(1, 4)]))
            pe.wait_ge(s_od_done, 32 + 64 + 64 + 4)
            proj("wout_o", woo, lambda k: A(k), [(0, 8)])
            for k in range(4):
                n = J["wout_o"] + 4 + k
                pe.wait_ge(freed[n % 4], n // 4 + 1)
            for t in range(NT):
                pt, n = opn(("out", t))
                pe.wait_ge(freed[n % 4], n // 4)
                for f in range(KD):
                    mm = pe.transpose(pt[:, f * P:f * P + P], H[:, f, t * P:t * P + P], IDENT)
                mm.then_inc(filled[n % 4], 1)

        @block.sync
        def _(sp):
            sp.dma_start(CST[:, :], a["cst"]).then_inc(s_cst_in, 16)
            sp.dma_start(PAR[:, :], a["par"]).then_inc(s_cst_in, 16)
            sp.dma_start(MSK[:, :, :].rearrange("p a b -> p (a b)"), a["msk"]).then_inc(s_cst_in, 16)
            for t in range(NT):
                sp.dma_start(AR[:, t, :], a["x"][0, t * P:t * P + P, :]).then_inc(s_cst_in, 16)
            users = []

            def load(w, src, m, kp, nk, dup):
                dst = WR[:, w % 4]
                if len(src.shape) == 2:
                    dst = dst[0:kp, 0, 0:m]
                elif src.shape[1] == 2 and src.shape[2] == 64:
                    dst = dst[:, 0, :].rearrange("p (h c) -> p h c", h=2)
                elif dup:
                    dst = dst.rearrange("p k (two c) -> p k two c", two=2)[:, 0:nk, 0, :]
                    sp.dma_start(dst, src).then_inc(w_dup, 16)
                    dst = WR[:, w % 4].rearrange("p k (two c) -> p k two c", two=2)[:, 0:nk, 1, :]
                    sp.wait_ge(w_dup, 16 * (dups[0] + 1))
                    dups[0] += 1
                else:
                    dst = dst[:, 0:nk, 0:m]
                sp.dma_start(dst, src).then_inc(w_in[w % 4], 16)

            dups = [0]
            w_dup = s_pre_f
            w = 0
            for e in WL:
                if e[0] == "run":
                    _, iters, nj, body = e
                    nb = len(body)

                    def issue(i, kk, prev):
                        src, _, nk = body[kk]
                        wm, c0, ii, step, k0 = src(i)
                        if isinstance(ii, int):
                            col = slice(c0 + ii * step * P, c0 + ii * step * P + P)
                        else:
                            col = bass.ds(sp.snap(ii * (step * P) + c0 if c0 else ii * (step * P // 2) * 2), P)
                        ap = wm[k0 * P:(k0 + nk) * P, col].rearrange("(k p) c -> p k c", p=P)
                        n, di = prev
                        sp.wait_ge(filled[n % 4], di + (n // 4 + 1))
                        sp.dma_start(WR[:, (w + kk) % 4, 0:nk, :], ap).then_inc(w_in[(w + kk) % 4], 16)

                    for kk in range(nb):
                        n = users[w + kk - 4] if kk < 4 else body[kk - 4][1]
                        issue(0, kk, (n, 0))
                    with sp.Fori(1, iters) as i:
                        for kk in range(nb):
                            if kk >= 4:
                                issue(i, kk, (body[kk - 4][1], i * (nj // 4)))
                            else:
                                issue(i, kk, (body[kk - 4 + nb][1], (i - 1) * (nj // 4)))
                    for i in range(iters):
                        users += [n + i * nj for _, n, _ in body]
                    w += nb * iters
                else:
                    src, n, m, kp, nk, dup = e
                    if w >= 4:
                        u = users[w - 4]
                        sp.wait_ge(filled[u % 4], u // 4 + 1)
                    load(w, src, m, kp, nk, dup)
                    users.append(n)
                    w += 1

        @block.scalar
        def _(act):
            done = {}

            def tick(sem):
                done[sem.name] = done.get(sem.name, 0) + 1
                return done[sem.name]

            def norm(i):
                for k in range(KD):
                    if k >= 2:
                        act.wait_ge(s_nsq_used, i * (KD - 1) + k - 1)
                    act.activation(A(26 + k % 2), H[:, k, :], ACT.Square).then_inc(s_nsq, 1)
                    act.wait_ge(s_nsq, tick(s_nsq))
                act.wait_ge(filled[bank(("norm", i))], turn(("norm", i)))
                t = PS[bank(("norm", i))]
                act.activation(A(25), t[:, :], ACT.Sqrt, bias=epsc)\
                    .then_inc(freed[bank(("norm", i))], 1)
                act.wait_ge(freed[bank(("norm", i))], turn(("norm", i)))

            act.wait_ge(s_cst_in, 16 * 11)
            for k in range(KD):
                act.wait_ge(filled[bank(("x", k))], turn(("x", k)))
                act.activation(H[:, k, :], PS[bank(("x", k))][:, :], ACT.Copy)\
                    .then_inc(freed[bank(("x", k))], 1)
                act.wait_ge(freed[bank(("x", k))], turn(("x", k)))
            norm(0)
            act.activation(SM[0:8, 0:1], par("alog", 0, 8), ACT.Exp).then_inc(s_nega, 1)
            act.wait_ge(s_nega, tick(s_nega))
            for k in range(4):
                act.wait_ge(filled[bank(("z", k))], turn(("z", k)))
                act.activation(A(4 + k), PS[bank(("z", k))][:, :], ACT.Silu)\
                    .then_inc(freed[bank(("z", k))], 1)
                act.wait_ge(freed[bank(("z", k))], turn(("z", k)))

            def ssd_silu(k):
                act.wait_ge(s_conv, k + 1)
                act.activation(A(8 + k), A(8 + k), ACT.Silu).then_inc(s_ssd_silu, 1)
                act.wait_ge(s_ssd_silu, tick(s_ssd_silu))
            for k in range(6):
                if k >= 2:
                    act.wait_ge(s_conv, k - 1)
                if k == 0:
                    act.wait_ge(s_normed, KD)
                act.wait_ge(filled[bank(("sx", k))], turn(("sx", k)))
                act.activation(A(25 + k % 2), PS[bank(("sx", k))][:, :], ACT.Copy)\
                    .then_inc(freed[bank(("sx", k))], 1)
                act.wait_ge(freed[bank(("sx", k))], turn(("sx", k)))
                if k >= 1:
                    ssd_silu(k - 1)
            act.wait_ge(filled[bank(("dt",))], turn(("dt",)))
            act.activation(A(0)[0:8, :], PS[bank(("dt",))][0:8, :], ACT.Identity, bias=par("dtb", 0, 8))\
                .then_inc(freed[bank(("dt",))], 1)
            act.wait_ge(freed[bank(("dt",))], turn(("dt",)))
            act.activation(A(1)[0:8, :], A(0)[0:8, :], ACT.Abs).then_inc(s_act_step, 1)
            act.wait_ge(s_act_step, tick(s_act_step))
            act.activation(A(1)[0:8, :], A(1)[0:8, :], ACT.Exp, scale=-1.0).then_inc(s_act_step, 1)
            act.wait_ge(s_act_step, tick(s_act_step))
            act.activation(A(1)[0:8, :], A(1)[0:8, :], ACT.Ln, bias=1.0).then_inc(s_dt_ln, 1)
            act.wait_ge(s_dt_ln, tick(s_dt_ln))
            ssd_silu(5)
            act.wait_ge(s_dec_in, 1)
            act.activation(A(27)[:, 256:384], A(27)[:, 256:384], ACT.Exp).then_inc(s_dec_ready, 1)
            act.wait_ge(s_dec_ready, tick(s_dec_ready))
            act.wait_ge(filled[bank(("Bt",))], turn(("Bt",)))
            act.activation(A(14), PS[bank(("Bt",))][:, :], ACT.Copy)\
                .then_inc(freed[bank(("Bt",))], 1)
            act.wait_ge(freed[bank(("Bt",))], turn(("Bt",)))
            for g in range(2):
                act.wait_ge(filled[bank(("CB", g))], turn(("CB", g)))
                act.activation(A(15 + g), PS[bank(("CB", g))][:, :], ACT.Copy)\
                    .then_inc(freed[bank(("CB", g))], 1)
                act.wait_ge(freed[bank(("CB", g))], turn(("CB", g)))

            def ssd_head(h):
                if h:
                    act.wait_ge(s_mc, h)
                act.wait_ge(filled[bank(("seg", h))], turn(("seg", h)))
                act.activation(A(26), PS[bank(("seg", h))][:, :], ACT.Exp).then_inc(s_ea, 1)
                act.wait_ge(s_ea, tick(s_ea))
                act.wait_ge(s_segm, h + 1)
                act.activation(A(25), A(25), ACT.Exp).then_inc(s_lmat, 1)
                act.wait_ge(s_lmat, tick(s_lmat))
            for fz in range(4):
                ssd_head(2 * fz)
                ssd_head(2 * fz + 1)
                act.wait_ge(s_yz, fz + 1)
                if fz == 2:
                    act.wait_ge(s_ys, 2)
                act.activation(A(12 + 2 * (fz % 2)), A(8 + fz), ACT.Square).then_inc(s_ysq, 1)
                act.wait_ge(s_ysq, tick(s_ysq))
                if fz % 2:
                    g = fz // 2
                    act.wait_ge(filled[bank(("yn", g))], turn(("yn", g)))
                    act.activation(A(28), PS[bank(("yn", g))][:, :], ACT.Sqrt, bias=epsc)\
                        .then_inc(freed[bank(("yn", g))], 1)
                    act.wait_ge(freed[bank(("yn", g))], turn(("yn", g)))
            for u in range(6):
                nh = 1 if u < 4 else 2
                act.wait_ge(s_ys, 4 + u if u < 4 else 8 + 2 * (u - 4))
                if u < 4:
                    act.wait_ge(filled[bank(("q", u))], turn(("q", u)))
                    act.activation(A(16), PS[bank(("q", u))][:, :], ACT.Silu)\
                        .then_inc(freed[bank(("q", u))], 1)
                    act.wait_ge(freed[bank(("q", u))], turn(("q", u)))
                    act.wait_ge(filled[bank(("k", u))], turn(("k", u)))
                    t = PS[bank(("k", u))]
                    act.activation(A(17), t[:, :], ACT.Sigmoid, scale=-1.0).then_inc(s_act_step, 1)
                    act.wait_ge(s_act_step, tick(s_act_step))
                    act.activation(A(18), t[:, :], ACT.Copy)\
                        .then_inc(freed[bank(("k", u))], 1)
                    act.wait_ge(freed[bank(("k", u))], turn(("k", u)))
                else:
                    if u == 4:
                        act.wait_ge(filled[bank(("glr",))], turn(("glr",)))
                        act.activation(A(11)[0:16, :], PS[bank(("glr",))][0:16, :], ACT.Copy)\
                            .then_inc(freed[bank(("glr",))], 1)
                        act.wait_ge(freed[bank(("glr",))], turn(("glr",)))
                    act.wait_ge(filled[bank(("q", u))], turn(("q", u)))
                    act.activation(A(16), PS[bank(("q", u))][:, :], ACT.Copy, scale=0.125)\
                        .then_inc(freed[bank(("q", u))], 1)
                    act.wait_ge(freed[bank(("q", u))], turn(("q", u)))
                    act.wait_ge(filled[bank(("k", u))], turn(("k", u)))
                    act.activation(A(17), PS[bank(("k", u))][:, :], ACT.Copy)\
                        .then_inc(freed[bank(("k", u))], 1)
                    act.wait_ge(freed[bank(("k", u))], turn(("k", u)))
                    act.wait_ge(filled[bank(("gz", u))], turn(("gz", u)))
                    act.activation(A(18), PS[bank(("gz", u))][:, :], ACT.Identity, bias=par("gb", u - 4))\
                        .then_inc(freed[bank(("gz", u))], 1)
                    act.wait_ge(freed[bank(("gz", u))], turn(("gz", u)))
                act.activation(A(19), A(18), ACT.Abs).then_inc(s_act_step, 1)
                act.wait_ge(s_act_step, tick(s_act_step))
                act.activation(A(19), A(19), ACT.Exp, scale=-1.0).then_inc(s_act_step, 1)
                act.wait_ge(s_act_step, tick(s_act_step))
                act.activation(A(19), A(19), ACT.Ln, bias=1.0).then_inc(s_lnr, 1)
                act.wait_ge(s_lnr, tick(s_lnr))
                for hh in range(nh):
                    act.wait_ge(filled[bank(("g", u, hh))], turn(("g", u, hh)))
                    act.activation([A(26), A(14)][hh], PS[bank(("g", u, hh))][:, :], ACT.Silu)\
                        .then_inc(freed[bank(("g", u, hh))], 1)
                    act.wait_ge(freed[bank(("g", u, hh))], turn(("g", u, hh)))
                for hh in range(nh):
                    act.wait_ge(filled[bank(("v", u, hh))], turn(("v", u, hh)))
                    act.activation(A(24), PS[bank(("v", u, hh))][:, :], ACT.Copy)\
                        .then_inc(freed[bank(("v", u, hh))], 1)
                    act.wait_ge(freed[bank(("v", u, hh))], turn(("v", u, hh)))
                    act.wait_ge(filled[bank(("vt", u, hh))], turn(("vt", u, hh)))
                    act.activation([A(25), A(13)][hh], PS[bank(("vt", u, hh))][:, :], ACT.Copy)\
                        .then_inc(freed[bank(("vt", u, hh))], 1)
                    act.wait_ge(freed[bank(("vt", u, hh))], turn(("vt", u, hh)))
                for l in range(NLEV):
                    act.wait_ge(s_expo, u * NLEV + l + 1)
                    act.activation(A(21 + l % 2), A(21 + l % 2), ACT.Exp).then_inc(s_expd, 1)
                    act.wait_ge(s_expd, tick(s_expd))
                act.wait_ge(s_qdec, 2 * u + 1)
                act.activation(A(15), A(15), ACT.Exp).then_inc(s_lru_t, 1)
                act.wait_ge(s_lru_t, tick(s_lru_t))
                act.activation(A(18), A(20), ACT.Exp).then_inc(s_lru_t, 1)
                act.wait_ge(s_lru_t, tick(s_lru_t))
                act.wait_ge(filled[bank(("kdt", u))], turn(("kdt", u)))
                act.activation(A(27), PS[bank(("kdt", u))][:, :], ACT.Copy)\
                    .then_inc(freed[bank(("kdt", u))], 1)
                act.wait_ge(freed[bank(("kdt", u))], turn(("kdt", u)))
                for hh in range(nh):
                    if hh:
                        act.wait_ge(s_ys, 8 + 2 * (u - 4) + 1)
                    act.wait_ge(filled[bank(("o", u, hh))], turn(("o", u, hh)))
                    t = PS[bank(("o", u, hh))]
                    act.activation(A(24), t[:, :], ACT.Copy).then_inc(s_act_step, 1)
                    act.wait_ge(s_act_step, tick(s_act_step))
                    act.activation(A(21), t[:, :], ACT.Square)\
                        .then_inc(freed[bank(("o", u, hh))], 1)
                    act.wait_ge(freed[bank(("o", u, hh))], turn(("o", u, hh)))
                    act.wait_ge(filled[bank(("on", u, hh))], turn(("on", u, hh)))
                    act.activation(A(22), PS[bank(("on", u, hh))][:, :], ACT.Sqrt, bias=epsc)\
                        .then_inc(freed[bank(("on", u, hh))], 1)
                    act.wait_ge(freed[bank(("on", u, hh))], turn(("on", u, hh)))
            base = 12
            act.activation(SM[:, 4:8], PAR[:, PC["lam"]:PC["lam"] + 4], ACT.Abs).then_inc(s_act_step, 1)
            act.wait_ge(s_act_step, tick(s_act_step))
            act.activation(SM[:, 4:8], SM[:, 4:8], ACT.Exp, scale=-1.0).then_inc(s_lsp_in, 1)
            act.wait_ge(s_lsp_in, tick(s_lsp_in))
            act.wait_ge(s_lsp_in, 1)
            for k in range(4):
                act.wait_ge(s_ys, 12 + k)
                act.wait_ge(filled[bank(("lx", k))], turn(("lx", k)))
                act.activation(A(16), PS[bank(("lx", k))][:, :], ACT.Copy)\
                    .then_inc(freed[bank(("lx", k))], 1)
                act.wait_ge(freed[bank(("lx", k))], turn(("lx", k)))
                act.wait_ge(filled[bank(("lg", k))], turn(("lg", k)))
                act.activation(A(23), PS[bank(("lg", k))][:, :], ACT.Gelu_apprx_tanh)\
                    .then_inc(freed[bank(("lg", k))], 1)
                act.wait_ge(freed[bank(("lg", k))], turn(("lg", k)))
                act.wait_ge(filled[bank(("lr", k))], turn(("lr", k)))
                act.activation(A(18), PS[bank(("lr", k))][:, :], ACT.Sigmoid, bias=par("ba", k))\
                    .then_inc(freed[bank(("lr", k))], 1)
                act.wait_ge(freed[bank(("lr", k))], turn(("lr", k)))
                act.wait_ge(filled[bank(("li", k))], turn(("li", k)))
                act.activation(A(19), PS[bank(("li", k))][:, :], ACT.Sigmoid, bias=par("bx", k))\
                    .then_inc(freed[bank(("li", k))], 1)
                act.wait_ge(freed[bank(("li", k))], turn(("li", k)))
                act.wait_ge(s_lamv, 1)
                act.activation(A(21), A(18), ACT.Tanh, scale=SM[:, 8 + k:9 + k]).then_inc(s_lru_q, 1)
                act.wait_ge(s_lru_q, tick(s_lru_q))
                act.activation(A(18), A(18), ACT.Exp, scale=SM[:, 12 + k:13 + k]).then_inc(s_lru_q, 1)
                act.wait_ge(s_lru_q, tick(s_lru_q))
                act.wait_ge(s_lru_b, k + 1)
                act.activation(A(21), A(21), ACT.Sqrt, scale=2.0).then_inc(s_lru_q, 1)
                act.wait_ge(s_lru_q, tick(s_lru_q))

            n0 = J["merge"]

            def merge(i):
                for b in range(4):
                    nm, nb = n0 + 2 * b, n0 + 2 * b + 1
                    if not isinstance(i, int) or i > 0 or b >= 2:
                        np_ = nb - 4
                        act.wait_ge(freed[np_ % 4], i * 2 + (np_ // 4 + 1))
                    act.wait_ge(filled[nm % 4], i * 2 + (nm // 4 + 1))
                    act.activation(A(24 + b % 2), PS[nm % 4][:, :], ACT.Sigmoid).then_inc(freed[nm % 4], 1)
            act.wait_ge(s_ys, 16)
            merge(0)
            with act.Fori(1, KD) as i:
                merge(i)
            for k in range(4):
                n = J["wout"] + 4 + k
                act.wait_ge(freed[n % 4], n // 4 + 1)
            norm(1)
            n1 = J["ffn_in"]
            act.wait_ge(s_normed, 2 * KD)

            def ffn(i):
                for j in range(2):
                    ng, nu = n1 + 2 * j, n1 + 2 * j + 1
                    if not isinstance(i, int):
                        act.wait_ge(freed[nu % 4], i + nu // 4)
                    act.wait_ge(filled[ng % 4], i + (ng // 4 + 1))
                    act.activation(A(24 + j), PS[ng % 4][:, :], ACT.Silu).then_inc(freed[ng % 4], 1)
            ffn(0)
            with act.Fori(1, NF // 2) as i:
                ffn(i)
            for k in range(4):
                n = J["ffn_out"] + 4 + k
                act.wait_ge(freed[n % 4], n // 4 + 1)
            norm(2)
            act.wait_ge(s_normed, 3 * KD)
            norm(3)

            act.wait_ge(s_normed, 4 * KD)
            cnt = {"hn": 0, "unit": 0, "s": 0, "vs": 0}

            def raw(name, dst, sq, m=P):
                if cnt["hn"]:
                    act.wait_ge(s_hn_done, cnt["hn"])
                act.wait_ge(filled[bank(name)], turn(name))
                t = PS[bank(name)]
                act.activation(dst[0:m, :], t[0:m, :], ACT.Copy).then_inc(s_act_step, 1)
                act.wait_ge(s_act_step, tick(s_act_step))
                act.activation(sq[0:m, :], t[0:m, :], ACT.Square)\
                    .then_inc(freed[bank(name)], 1)
                act.wait_ge(freed[bank(name)], turn(name))

            def root(m=P):
                i = cnt["hn"]
                act.wait_ge(filled[bank(("hn", i))], turn(("hn", i)))
                act.activation(A(23)[0:m, :], PS[bank(("hn", i))][0:m, :], ACT.Sqrt, bias=epsc[0:m])\
                    .then_inc(freed[bank(("hn", i))], 1)
                act.wait_ge(freed[bank(("hn", i))], turn(("hn", i)))
                cnt["hn"] += 1

            def to_sbuf(name):
                act.wait_ge(filled[bank(name)], turn(name))
                act.activation(A(27), PS[bank(name)][:, :], ACT.Copy).then_inc(freed[bank(name)], 1)
                act.wait_ge(freed[bank(name)], turn(name))

            def to_tokens(name, dst):
                act.wait_ge(filled[bank(name)], turn(name))
                act.activation(dst, PS[bank(name)][:, :], ACT.Copy).then_inc(freed[bank(name)], 1)
                act.wait_ge(freed[bank(name)], turn(name))

            def prep_a(p):
                if p >= 2:
                    act.wait_ge(s_negmax, 8 * (p - 1))
                act.dma_start(A(25 + p % 2)[:, 0:960], a["rpb"][p]).then_inc(s_bias_in, 16)
                raw(("qa", p), A(8 + p % 2), A(22))
                yield
                root()
                raw(("ka", p), A(10 + p % 2), A(22))
                yield
                root()
                to_sbuf(("va", p))
                yield
                to_tokens(("vat", p), A(12 + p % 2))
                v, vs = tt(A(12 + p % 2)), tt(A(18 + p % 2))
                act.dma_start(vs[0:64, 0:7, :], v[64:128, 0:7, :]).then_inc(s_vs_in, 16)
                act.dma_start(vs[64:128, 0:7, :], v[0:64, 1:8, :]).then_inc(s_vs_in, 16)
                yield
                if p >= 2:
                    act.wait_ge(s_od_done, 8 * (p - 1))
                act.wait_ge(filled[bank(("ga", p))], turn(("ga", p)))
                act.activation(A(14 + p % 2), PS[bank(("ga", p))][:, :], ACT.Silu)\
                    .then_inc(freed[bank(("ga", p))], 1)
                act.wait_ge(freed[bank(("ga", p))], turn(("ga", p)))
                yield

            def tables(which):
                act.dma_start(A(25), a["rope"][2 * which]).then_inc(s_tab_in, 16)
                act.dma_start(A(26), a["rope"][2 * which + 1]).then_inc(s_tab_in, 16)

            def gate(name, dst):
                act.wait_ge(filled[bank(name)], turn(name))
                act.activation(dst, PS[bank(name)][:, :], ACT.Silu).then_inc(freed[bank(name)], 1)
                act.wait_ge(freed[bank(name)], turn(name))

            def prep_bkv():
                act.wait_ge(s_od_done, 32)
                tables(0)
                for j in range(2):
                    raw(("kb", j), A(10 + j), A(22))
                    root()
                act.wait_ge(s_rope_tmp, 2)
                to_sbuf(("vb",))
                to_tokens(("vbt",), A(12))
                yield

            def prep_b(p):
                raw(("qb", p), A(8 + p % 2), A(22))
                yield
                root()
                if p >= 2:
                    act.wait_ge(s_od_done, 32 + 16 * (p - 1))
                gate(("gb", p), A(14 + p % 2))
                yield
                yield

            def prep_c0():
                tables(1)
                act.wait_ge(s_hn_done, cnt["hn"])
                for j in range(2):
                    act.wait_ge(filled[bank(("cq", j))], turn(("cq", j)))
                    t = PS[bank(("cq", j))]
                    act.activation(A(18 + j), t[:, :], ACT.Copy).then_inc(s_act_step, 1)
                    act.wait_ge(s_act_step, tick(s_act_step))
                    act.activation(A(22 + 2 * j), t[:, :], ACT.Square)\
                        .then_inc(freed[bank(("cq", j))], 1)
                    act.wait_ge(freed[bank(("cq", j))], turn(("cq", j)))
                root()
                raw(("ckv",), A(28), A(22))
                root()
                act.wait_ge(filled[bank(("kpe",))], turn(("kpe",)))
                act.activation(MSKF[64:96, :], PS[bank(("kpe",))][64:96, :], ACT.Copy)\
                    .then_inc(freed[bank(("kpe",))], 1)
                act.wait_ge(freed[bank(("kpe",))], turn(("kpe",)))
                yield

            def prep_c(h):
                p = h // 2
                raw(("qc", h), A(8 + h % 2), A(22), 96)
                yield
                root(96)
                if h % 2 == 0:
                    if p >= 2:
                        act.wait_ge(s_od_done, 96 + 16 * (p - 1))
                    gate(("gc", p), A(14 + p % 2))
                yield
                act.wait_ge(s_hn_done, cnt["hn"])
                act.wait_ge(filled[bank(("kc", h))], turn(("kc", h)))
                t = PS[bank(("kc", h))]
                kt = A(10 + h % 2)
                act.activation(kt[0:64, :], t[0:64, :], ACT.Copy).then_inc(s_act_step, 1)
                act.wait_ge(s_act_step, tick(s_act_step))
                act.activation(A(22)[0:64, :], t[0:64, :], ACT.Square)\
                    .then_inc(freed[bank(("kc", h))], 1)
                act.wait_ge(freed[bank(("kc", h))], turn(("kc", h)))
                act.activation(kt[64:96, :], MSKF[64:96, :], ACT.Copy).then_inc(s_act_step, 1)
                act.wait_ge(s_act_step, tick(s_act_step))
                act.activation(A(22)[64:96, :], MSKF[64:96, :], ACT.Square).then_inc(s_kraw, 1)
                act.wait_ge(s_kraw, tick(s_kraw))
                yield
                root(96)
                yield
                yield
                if h % 2 == 0:
                    act.wait_ge(s_rope_tmp, 6 + 2 * h + 2)
                    to_sbuf(("vc", p))
                yield
                if h % 2 == 0:
                    to_tokens(("vct", p), A(12 + p % 2))
                yield
                yield

            def prep_d(h):
                if h == 0:
                    act.wait_ge(s_rope_tmp, 6 + 16)
                    tables(2)
                raw(("qd", h), A(8 + h % 2), A(22))
                yield
                root()
                raw(("kd", h), A(10 + h % 2), A(22))
                yield
                yield
                root()
                yield
                act.wait_ge(s_rope_tmp, 22 + 2 * h + 2)
                to_sbuf(("vd", h))
                yield
                to_tokens(("vdt", h), A(12 + h % 2))
                yield
                if h >= 2:
                    act.wait_ge(s_od_done, 160 + h - 1)
                gate(("gd", h), A(14 + h % 2))
                yield
                yield

            def attend(kind, nu, scale):
                base = cnt["unit"]
                nm = 2 if kind == "D" else 1
                for s in range(nu + LAG + 1 + (3 if kind == "D" else 0)):
                    if s < nu:
                        b = base + s
                        for m in range(nm):
                            c = (b % 2) * 2 + m
                            if kind != "A" and b >= base + 2:
                                act.wait_ge(filled[bank(("T", b - 2))], turn(("T", b - 2)))
                            elif kind != "A" and base >= 2:
                                act.wait_ge(filled[bank(("T", b - 2))], turn(("T", b - 2)))
                            pr = A(16 + (b % 2) * nm + m)
                            cnt["s"] += 1
                            act.wait_ge(s_negmax, cnt["s"])
                            if kind == "A":
                                for rr in range(2):
                                    act.activation(pr[:, rr * 512:rr * 512 + 512], pr[:, rr * 512:rr * 512 + 512], ACT.Exp,
                                         bias=SM[:, 20 + 2 * (b % 2) + rr:21 + 2 * (b % 2) + rr],
                                         accum_out=SM[:, 24 + 2 * (b % 2) + rr:25 + 2 * (b % 2) + rr]).then_inc((s_pexp if rr else s_act_step), 1)
                                    act.wait_ge((s_pexp if rr else s_act_step), tick((s_pexp if rr else s_act_step)))
                            else:
                                act.activation(pr, PS[J[("S", b, m)] % 4][:, :], ACT.Exp, scale=scale,
                                     bias=SM[:, 20 + c:21 + c], accum_out=SM[:, 24 + c:25 + c])\
                                    .then_inc(freed[bank(("S", b, m))], 1)
                                act.wait_ge(freed[bank(("S", b, m))], turn(("S", b, m)))
                    if LAG <= s < nu + LAG:
                        b = base + s - LAG
                        if b >= 2:
                            act.wait_ge(filled[bank(("O", b - 2))], turn(("O", b - 2)))
                        act.wait_ge(filled[bank(("T", b))], turn(("T", b)))
                        act.activation(A(20 + b % 2), PS[bank(("T", b))][:, :], ACT.Copy)\
                            .then_inc(freed[bank(("T", b))], 1)
                        act.wait_ge(freed[bank(("T", b))], turn(("T", b)))
                    yield
                cnt["unit"] += nu

            def att_a():
                return attend("A", 32, 1.0)

            def att_b():
                return attend("B", 64, 0.125)

            def att_c():
                return attend("C", 64, 96 ** -0.5)

            def att_d():
                base = cnt["unit"]
                for s, _ in enumerate(attend("D", 32, 0.125)):
                    yield
                    if s >= 8 and s % 8 == POST:
                        h = s // 8 - 1
                        last = ("O", base + 8 * h + 7)
                        act.wait_ge(freed[bank(last)], turn(last))
                        act.wait_ge(s_hn_done, cnt["hn"])
                        act.activation(A(22), A(4 + h), ACT.Square).then_inc(s_osq, 1)
                        act.wait_ge(s_osq, tick(s_osq))
                        act.wait_ge(filled[bank(("odn", h))], turn(("odn", h)))
                        act.activation(A(23), PS[bank(("odn", h))][:, :], ACT.Sqrt, bias=epsc)\
                            .then_inc(freed[bank(("odn", h))], 1)
                        act.wait_ge(freed[bank(("odn", h))], turn(("odn", h)))
                        act.wait_ge(s_od_done, 160 + h + 1)

            weave(prep_a(0), ())
            weave(att_a(), chain(8, prep_a(1), prep_a(2), prep_a(3)))
            weave(prep_bkv(), ())
            weave(prep_b(0), ())
            weave(att_b(), chain(16, prep_b(1), prep_b(2), prep_b(3)))
            for k in range(4):
                n = J["wout_e"] + 4 + k
                act.wait_ge(freed[n % 4], n // 4 + 1)
            norm(4)
            act.wait_ge(s_normed, 5 * KD)
            act.wait_ge(filled[bank(("lam",))], turn(("lam",)))
            act.activation(SM[:, 32:34], PS[bank(("lam",))][:, 0:2], ACT.Exp)\
                .then_inc(freed[bank(("lam",))], 1)
            act.wait_ge(freed[bank(("lam",))], turn(("lam",)))
            weave(prep_c0(), ())
            weave(prep_c(0), ())
            weave(att_c(), chain(8, *[prep_c(h) for h in range(1, 8)]))
            weave(prep_d(0), ())
            weave(att_d(), chain(8, *[prep_d(h) for h in range(1, 4)]))
            for t in range(NT):
                act.wait_ge(filled[bank(("out", t))], turn(("out", t)))
                act.activation(A(16 + t), PS[bank(("out", t))][:, :], ACT.Copy)\
                    .then_inc(freed[bank(("out", t))], 1)
                act.wait_ge(freed[bank(("out", t))], turn(("out", t)))
                act.dma_start(a["out"][0, t * P:t * P + P, :], A(16 + t)).then_inc(s_out_in, 16)
            act.wait_ge(s_out_in, 16 * NT)

        @block.vector
        def _(v):
            done = {}

            def tick(sem):
                done[sem.name] = done.get(sem.name, 0) + 1
                return done[sem.name]

            def TT(o, x, y, op):
                return v.tensor_tensor(o, x, y, op)

            def TS(o, x, s1, s2=None, op0=ALU.mult, op1=None):
                if op1 is None:
                    return v.tensor_scalar(o, x, s1, None, op0)
                return v.tensor_scalar(o, x, s1, s2, op0, op1)

            def STT(o, x, s, y, op0, op1):
                return v.scalar_tensor_tensor(out=o, in0=x, scalar=s, in1=y, op0=op0, op1=op1)

            def norm(i, w, dst):
                v.wait_ge(freed[bank(("norm", i))], turn(("norm", i)))
                v.reciprocal(A(25), A(25)).then_inc(s_dve_step, 1)
                v.wait_ge(s_dve_step, tick(s_dve_step))
                for k in range(KD):
                    STT(dst[:, k, :], H[:, k, :], par(w, k), A(25), ALU.mult, ALU.mult).then_inc(s_normed, 1)
                    v.wait_ge(s_normed, tick(s_normed))

            def conv(src, dst, w, nf, fi, b):
                TS(dst, src, par(w, 3 * nf + fi), par(b, fi), ALU.mult, ALU.add).then_inc(s_dve_step, 1)
                v.wait_ge(s_dve_step, tick(s_dve_step))
                for s in (1, 2, 3):
                    STT(dst[:, s:L], src[:, 0:L - s], par(w, (3 - s) * nf + fi), dst[:, s:L], ALU.mult, ALU.add).then_inc((s_conv if s == 3 else s_dve_step), 1)
                    v.wait_ge((s_conv if s == 3 else s_dve_step), tick((s_conv if s == 3 else s_dve_step)))

            norm(0, "nmix", XN)
            v.wait_ge(s_nega, 1)
            TS(SM[0:8, 1:2], SM[0:8, 0:1], -1.0).then_inc(s_dve_step, 1)
            v.wait_ge(s_dve_step, tick(s_dve_step))
            for k in range(6):
                v.wait_ge(freed[bank(("sx", k))], turn(("sx", k)))
                conv(A(25 + k % 2), A(8 + k), "scw", 6, k, "scb")
            v.wait_ge(s_dt_ln, 1)
            STT(A(0)[0:8, :], A(0)[0:8, :], 0.0, A(1)[0:8, :], ALU.max, ALU.add).then_inc(s_dve_step, 1)
            v.wait_ge(s_dve_step, tick(s_dve_step))
            TS(A(2)[0:8, :], A(0)[0:8, :], SM[0:8, 1:2]).then_inc(s_dt_done, 1)
            v.wait_ge(s_dt_done, tick(s_dt_done))
            T27 = A(27)
            v.wait_ge(filled[bank(("dtt",))], turn(("dtt",)))
            v.tensor_copy(T27[:, 0:128], PS[bank(("dtt",))][:, 0:128])\
                .then_inc(freed[bank(("dtt",))], 1)
            v.wait_ge(freed[bank(("dtt",))], turn(("dtt",)))
            v.wait_ge(filled[bank(("acs",))], turn(("acs",)))
            v.tensor_copy(T27[:, 128:256], PS[bank(("acs",))][:, 0:128])\
                .then_inc(freed[bank(("acs",))], 1)
            v.wait_ge(freed[bank(("acs",))], turn(("acs",)))
            TT(T27[:, 256:320], T27[:, 192:256], T27[:, 128:192], ALU.subtract).then_inc(s_dve_step, 1)
            v.wait_ge(s_dve_step, tick(s_dve_step))
            v.tensor_copy(T27[:, 320:384], T27[:, 192:256]).then_inc(s_dec_in, 1)
            v.wait_ge(s_dec_in, tick(s_dec_in))
            v.wait_ge(s_dec_ready, 1)
            xdt = AR[:, 17:21, :].rearrange("p a (b c) -> p (a b) c", c=512)
            xdd = AR[:, 21:25, :].rearrange("p a (b c) -> p (a b) c", c=512)
            sst = AR[:, 0:4, :].rearrange("p a (b c) -> p (a b) c", c=512)
            th = lambda c0: T27[:, c0:c0 + 64].rearrange("p (t h o) -> p t h o", h=8, o=1)
            for k in range(4):
                v.wait_ge(filled[bank(("xt", k))], turn(("xt", k)))
                t = PS[bank(("xt", k))]
                for hh in range(2):
                    h = 2 * k + hh
                    o = xdt[:, :, h * 64:h * 64 + 64]
                    step = TT(o, tt(t[:, :])[:, :, hh * 64:hh * 64 + 64],
                          th(0)[:, :, h, :].to_broadcast([P, NT, 64]), ALU.mult)
                    if hh:
                        step.then_inc(freed[bank(("xt", k))], 1)
                        v.wait_ge(freed[bank(("xt", k))], turn(("xt", k)))
                    else:
                        step.then_inc(s_dve_step, 1)
                        v.wait_ge(s_dve_step, tick(s_dve_step))
                for hh in range(2):
                    h = 2 * k + hh
                    TT(xdd[:, :, h * 64:h * 64 + 64], xdt[:, :, h * 64:h * 64 + 64],
                          th(256)[:, :, h, :].to_broadcast([P, NT, 64]), ALU.mult).then_inc((s_xdt if hh else s_dve_step), 1)
                    v.wait_ge((s_xdt if hh else s_dve_step), tick((s_xdt if hh else s_dve_step)))
            for j in range(4):
                v.wait_ge(filled[bank(("sU", j))], turn(("sU", j)))
                t = PS[bank(("sU", j))]
                for i in range(2 if j < 3 else 1):
                    c = 2 * j + i
                    last = (i == 1 or j == 3)
                    if c == 0:
                        v.tensor_copy(sst[:, 1, :], t[:, 0:512]).then_inc(s_ssd_state, 1)
                        v.wait_ge(s_ssd_state, tick(s_ssd_state))
                        continue
                    el = th(320)[:, c, :, :].to_broadcast([P, 8, 64])
                    TT(sst[:, c + 1, :].rearrange("p (h c) -> p h c", h=8),
                          sst[:, c, :].rearrange("p (h c) -> p h c", h=8), el, ALU.mult).then_inc(s_dve_step, 1)
                    v.wait_ge(s_dve_step, tick(s_dve_step))
                    TT(sst[:, c + 1, :], sst[:, c + 1, :], t[:, i * 512:i * 512 + 512], ALU.add).then_inc(s_ssd_state, 1)
                    v.wait_ge(s_ssd_state, tick(s_ssd_state))
                v.tensor_copy(SM[:, 2:3], t[:, 0:1])\
                    .then_inc(freed[bank(("sU", j))], 1)
                v.wait_ge(freed[bank(("sU", j))], turn(("sU", j)))
            v.wait_ge(s_ssd_silu, 6)

            def ssd_head(h):
                v.wait_ge(filled[bank(("seg", h))], turn(("seg", h)))
                t = PS[bank(("seg", h))]
                v.wait_ge(s_ea, h + 1)
                TT(tt(A(25)), tt(t[:, :]), th(128)[:, :, h, :].to_broadcast([P, NT, P]), ALU.subtract)\
                    .then_inc(freed[bank(("seg", h))], 1)
                v.wait_ge(freed[bank(("seg", h))], turn(("seg", h)))
                neg = cm("neg").rearrange("p (o i) -> p o i", o=1).to_broadcast([P, NT, P])
                TT(tt(A(25)), tt(A(25)), neg, ALU.add).then_inc(s_segm, 1)
                v.wait_ge(s_segm, tick(s_segm))
                v.wait_ge(s_lmat, h + 1)
                if h >= 2:
                    v.wait_ge(filled[bank(("y", h // 2 - 1))], turn(("y", h // 2 - 1)))
                v.wait_ge(freed[bank(("CB", h // 4))], turn(("CB", h // 4)))
                TT(A(21 + h % 2), A(25), A(15 + h // 4), ALU.mult).then_inc(s_dve_step, 1)
                v.wait_ge(s_dve_step, tick(s_dve_step))
                TT(A(23 + h % 2), A(26), A(13), ALU.mult).then_inc(s_mc, 1)
                v.wait_ge(s_mc, tick(s_mc))

            for k in range(4):
                ssd_head(2 * k)
                ssd_head(2 * k + 1)
                v.wait_ge(filled[bank(("y", k))], turn(("y", k)))
                STT(A(8 + k), A(8 + k), par("sd", k), PS[bank(("y", k))][:, :], ALU.mult, ALU.add)\
                    .then_inc(freed[bank(("y", k))], 1)
                v.wait_ge(freed[bank(("y", k))], turn(("y", k)))
                TT(A(8 + k), A(8 + k), A(4 + k), ALU.mult).then_inc(s_yz, 1)
                v.wait_ge(s_yz, tick(s_yz))
                if k % 2:
                    g = k // 2
                    v.wait_ge(freed[bank(("yn", g))], turn(("yn", g)))
                    v.reciprocal(A(28), A(28)).then_inc(s_dve_step, 1)
                    v.wait_ge(s_dve_step, tick(s_dve_step))
                    for j in (k - 1, k):
                        STT(A(4 + j), A(8 + j), par("snw", j), A(28), ALU.mult, ALU.mult).then_inc(s_ys, 1)
                        v.wait_ge(s_ys, tick(s_ys))

            v.memset(A(23), 0.0).then_inc(s_dve_step, 1)
            v.wait_ge(s_dve_step, tick(s_dve_step))
            for u in range(6):
                nh = 1 if u < 4 else 2
                if u == 4:
                    v.memset(A(12), 0.0).then_inc(s_dve_step, 1)
                    v.wait_ge(s_dve_step, tick(s_dve_step))
                v.wait_ge(s_lnr, u + 1)
                STT(A(18), A(18), 0.0, A(19), ALU.min, ALU.subtract).then_inc(s_dve_step, 1)
                v.wait_ge(s_dve_step, tick(s_dve_step))
                if nh == 2:
                    TS(A(18), A(18), 1.0 / 16.0).then_inc(s_dve_step, 1)
                    v.wait_ge(s_dve_step, tick(s_dve_step))
                for t in range(NT):
                    c = slice(t * P, t * P + P)
                    v.tensor_tensor_scan(A(20)[:, c], CST[:, CONE:CONE + 1].to_broadcast([P, P]), A(18)[:, c],
                                            0.0, ALU.mult, ALU.add).then_inc(s_dve_step, 1)
                    v.wait_ge(s_dve_step, tick(s_dve_step))

                def halves(ap, l):
                    s = 64 >> l
                    return ap.rearrange("p (b h s) -> p b h s", h=2, s=s)

                def expo(l):
                    s = 64 >> l
                    nb = L // (2 * s)
                    x, b = halves(A(21 + l % 2), l), halves(A(20), l)
                    mid = b[:, :, 0, s - 1:s].to_broadcast([P, nb, s])
                    TT(x[:, :, 0, :], mid, b[:, :, 0, :], ALU.subtract).then_inc(s_dve_step, 1)
                    v.wait_ge(s_dve_step, tick(s_dve_step))
                    TT(x[:, :, 1, :], b[:, :, 1, :], mid, ALU.subtract).then_inc(s_expo, 1)
                    v.wait_ge(s_expo, tick(s_expo))

                def pred(l):
                    m = MSK[:, l:l + 1, :].to_broadcast([P, NT, P])
                    for hh in range(nh):
                        am = [A(23), A(12)][hh]
                        v.wait_ge(filled[bank(("P", u, l if l < NLEV else -1, hh))], turn(("P", u, l if l < NLEV else -1, hh)))
                        v.copy_predicated(tt(am), m, tt(PS[bank(("P", u, l if l < NLEV else -1, hh))][:, :]))\
                            .then_inc(freed[bank(("P", u, l if l < NLEV else -1, hh))], 1)
                        v.wait_ge(freed[bank(("P", u, l if l < NLEV else -1, hh))], turn(("P", u, l if l < NLEV else -1, hh)))

                expo(0)
                v.wait_ge(freed[bank(("q", u))], turn(("q", u)))
                for l in range(NLEV):
                    pred(NLEV if l == 0 else l - 1)
                    if l < NLEV - 1:
                        expo(l + 1)
                    v.wait_ge(s_expd, u * NLEV + l + 1)
                    x = halves(A(21 + l % 2), l)
                    TT(x[:, :, 0, :], x[:, :, 0, :], halves(A(17), l)[:, :, 0, :], ALU.mult).then_inc(s_dve_step, 1)
                    v.wait_ge(s_dve_step, tick(s_dve_step))
                    TT(x[:, :, 1, :], x[:, :, 1, :], halves(A(16), l)[:, :, 1, :], ALU.mult).then_inc(s_xlev, 1)
                    v.wait_ge(s_xlev, tick(s_xlev))
                b = tt(A(20))
                TT(tt(A(15)), b[:, :, P - 1:P].to_broadcast([P, NT, P]), b, ALU.subtract).then_inc(s_qdec, 1)
                v.wait_ge(s_qdec, tick(s_qdec))
                pred(NLEV - 1)
                v.wait_ge(s_lru_t, 2 * u + 2)
                TT(A(15), A(15), A(17), ALU.mult).then_inc(s_kdec, 1)
                v.wait_ge(s_kdec, tick(s_kdec))
                TT(A(16), A(16), A(18), ALU.mult).then_inc(s_a_done, 1)
                v.wait_ge(s_a_done, tick(s_a_done))
                v.wait_ge(filled[bank(("U", u))], turn(("U", u)))
                t = PS[bank(("U", u))]
                s = A(19)
                v.tensor_copy(s[:, P:2 * P], t[:, 0:P]).then_inc(s_dve_step, 1)
                v.wait_ge(s_dve_step, tick(s_dve_step))
                for c in range(1, NT - 1):
                    el = A(18)[:, c * P + P - 1:c * P + P]
                    STT(s[:, (c + 1) * P:(c + 2) * P], s[:, c * P:c * P + P], el, t[:, c * P:c * P + P],
                           ALU.mult, ALU.add).then_inc((s_g_state if c == NT - 2 else s_dve_step), 1)
                    v.wait_ge((s_g_state if c == NT - 2 else s_dve_step), tick((s_g_state if c == NT - 2 else s_dve_step)))
                v.tensor_copy(SM[:, 2:3], t[:, 0:1])\
                    .then_inc(freed[bank(("U", u))], 1)
                v.wait_ge(freed[bank(("U", u))], turn(("U", u)))
                v.tensor_copy(SM[:, 3:4], SM[:, 2:3]).then_inc(s_qdec, 1)
                v.wait_ge(s_qdec, tick(s_qdec))
                for hh in range(nh):
                    v.wait_ge(freed[bank(("on", u, hh))], turn(("on", u, hh)))
                    v.reciprocal(A(22), A(22)).then_inc(s_dve_step, 1)
                    v.wait_ge(s_dve_step, tick(s_dve_step))
                    STT(A(24), A(24), par("hnw" if u < 4 else "gnw"), A(22), ALU.mult, ALU.mult).then_inc(s_dve_step, 1)
                    v.wait_ge(s_dve_step, tick(s_dve_step))
                    dst = A(u) if u < 4 else A(8 + 2 * (u - 4) + hh)
                    TT(dst, A(24), [A(26), A(14)][hh], ALU.mult).then_inc(s_ys, 1)
                    v.wait_ge(s_ys, tick(s_ys))

            v.memset(A(20), 0.0).then_inc(s_bd_zero, 1)
            v.wait_ge(s_bd_zero, tick(s_bd_zero))
            v.wait_ge(s_lsp_in, 1)
            e, z, z2, acc = SM[:, 4:8], SM[:, 8:12], SM[:, 12:16], SM[:, 16:20]
            TS(z, e, 2.0, None, ALU.add).then_inc(s_dve_step, 1)
            v.wait_ge(s_dve_step, tick(s_dve_step))
            v.reciprocal(z, z).then_inc(s_dve_step, 1)
            v.wait_ge(s_dve_step, tick(s_dve_step))
            TT(z, z, e, ALU.mult).then_inc(s_dve_step, 1)
            v.wait_ge(s_dve_step, tick(s_dve_step))
            TT(z2, z, z, ALU.mult).then_inc(s_dve_step, 1)
            v.wait_ge(s_dve_step, tick(s_dve_step))
            TS(acc, z2, 2.0 / 13, 2.0 / 11, ALU.mult, ALU.add).then_inc(s_dve_step, 1)
            v.wait_ge(s_dve_step, tick(s_dve_step))
            for o in (9, 7, 5, 3, 1):
                TT(acc, acc, z2, ALU.mult).then_inc(s_dve_step, 1)
                v.wait_ge(s_dve_step, tick(s_dve_step))
                TS(acc, acc, 2.0 / o, None, ALU.add).then_inc(s_dve_step, 1)
                v.wait_ge(s_dve_step, tick(s_dve_step))
            TT(acc, acc, z, ALU.mult).then_inc(s_dve_step, 1)
            v.wait_ge(s_dve_step, tick(s_dve_step))
            TS(e, PAR[:, PC["lam"]:PC["lam"] + 4], -1.0, 0.0, ALU.mult, ALU.max).then_inc(s_dve_step, 1)
            v.wait_ge(s_dve_step, tick(s_dve_step))
            TT(acc, acc, e, ALU.add).then_inc(s_dve_step, 1)
            v.wait_ge(s_dve_step, tick(s_dve_step))
            TS(SM[:, 8:12], acc, 8.0).then_inc(s_dve_step, 1)
            v.wait_ge(s_dve_step, tick(s_dve_step))
            TS(SM[:, 12:16], acc, -8.0).then_inc(s_lamv, 1)
            v.wait_ge(s_lamv, tick(s_lamv))
            for k in range(4):
                v.wait_ge(freed[bank(("lx", k))], turn(("lx", k)))
                conv(A(16), A(17), "lcw", 4, k, "lcb")
                v.wait_ge(s_lru_q, 3 * k + 2)
                TS(A(22), A(21), 1.0, None, ALU.add).then_inc(s_dve_step, 1)
                v.wait_ge(s_dve_step, tick(s_dve_step))
                v.reciprocal(A(22), A(22)).then_inc(s_dve_step, 1)
                v.wait_ge(s_dve_step, tick(s_dve_step))
                TT(A(21), A(21), A(22), ALU.mult).then_inc(s_lru_b, 1)
                v.wait_ge(s_lru_b, tick(s_lru_b))
                TT(A(19), A(19), A(17), ALU.mult).then_inc(s_dve_step, 1)
                v.wait_ge(s_dve_step, tick(s_dve_step))
                v.wait_ge(s_lru_q, 3 * k + 3)
                TT(A(21), A(21), A(19), ALU.mult).then_inc(s_dve_step, 1)
                v.wait_ge(s_dve_step, tick(s_dve_step))
                v.tensor_tensor_scan(A(22), A(18), A(21), 0.0, ALU.mult, ALU.add).then_inc(s_dve_step, 1)
                v.wait_ge(s_dve_step, tick(s_dve_step))
                TT(A(12 + k), A(22), A(23), ALU.mult).then_inc(s_ys, 1)
                v.wait_ge(s_ys, tick(s_ys))

            n0 = J["merge"]
            with v.Fori(0, KD) as i:
                dst = AR[:, bass.ds(i + 16, 1), :]
                for b in range(4):
                    nm, nb = n0 + 2 * b, n0 + 2 * b + 1
                    v.wait_ge(freed[nm % 4], i * 2 + (nm // 4 + 1))
                    v.wait_ge(filled[nb % 4], i * 2 + (nb // 4 + 1))
                    o = A(26)
                    v.tensor_tensor(dst if b == 0 else o, A(24 + b % 2), PS[nb % 4][:, :], ALU.mult)\
                        .then_inc(freed[nb % 4], 1)
                    v.wait_ge(freed[nb % 4], i * 2 + (nb // 4 + 1))
                    if b:
                        v.tensor_tensor(dst, dst, o, ALU.add).then_inc(s_merge_add, 1)
                        v.wait_ge(s_merge_add, i * 3 + b)

            def residual(name):
                n2 = J[name]
                with v.Fori(0, 2) as i:
                    for j in range(4):
                        n = n2 + j
                        v.wait_ge(filled[n % 4], i + (n // 4 + 1))
                        h = H[:, bass.ds(i * 4 + j, 1), :]
                        v.tensor_tensor(h, h, PS[n % 4][:, :], ALU.add).then_inc(freed[n % 4], 1)
                for j in range(4):
                    n = n2 + 4 + j
                    v.wait_ge(freed[n % 4], n // 4 + 1)
            residual("wout")
            norm(1, "nffn", XN)
            n1 = J["ffn_in"]
            with v.Fori(0, NF // 2) as i:
                for j in range(2):
                    ng, nu = n1 + 2 * j, n1 + 2 * j + 1
                    v.wait_ge(freed[ng % 4], i + (ng // 4 + 1))
                    v.wait_ge(filled[nu % 4], i + (nu // 4 + 1))
                    v.tensor_tensor(AR[:, bass.ds(i * 2 + j, 1), :], A(24 + j), PS[nu % 4][:, :], ALU.mult)\
                        .then_inc(freed[nu % 4], 1)
            residual("ffn_out")
            norm(2, "nf", H)
            norm(3, "ne", XN)

            cnt = {"hn": 0, "unit": 0, "rope": 0}
            TT(SM[0:64, 30:31], PAR[0:64, PC["lq1"]:PC["lq1"] + 1], PAR[0:64, PC["lk1"]:PC["lk1"] + 1], ALU.mult).then_inc(s_dve_step, 1)
            v.wait_ge(s_dve_step, tick(s_dve_step))
            TT(SM[0:64, 31:32], PAR[0:64, PC["lq2"]:PC["lq2"] + 1], PAR[0:64, PC["lk2"]:PC["lk2"] + 1], ALU.mult).then_inc(s_lam_e, 1)
            v.wait_ge(s_lam_e, tick(s_lam_e))

            def hn(x, g, m=P):
                v.wait_ge(freed[bank(("hn", cnt["hn"]))], turn(("hn", cnt["hn"])))
                cnt["hn"] += 1
                v.reciprocal(A(23)[0:m, :], A(23)[0:m, :]).then_inc(s_dve_step, 1)
                v.wait_ge(s_dve_step, tick(s_dve_step))
                STT(x[0:m, :], x[0:m, :], g[0:m], A(23)[0:m, :], ALU.mult, ALU.mult).then_inc(s_hn_done, 1)
                v.wait_ge(s_hn_done, tick(s_hn_done))

            def pad_keys(x, other):
                v.tensor_copy(other[64:128, :], x[64:128, :]).then_inc(s_dve_step, 1)
                v.wait_ge(s_dve_step, tick(s_dve_step))
                v.memset(other[0:64, :], 0.0).then_inc(s_dve_step, 1)
                v.wait_ge(s_dve_step, tick(s_dve_step))
                v.memset(x[64:128, :], 0.0).then_inc(s_kz, 1)
                v.wait_ge(s_kz, tick(s_kz))

            def rope(x, m=P):
                i = cnt["hn"] - 1
                cnt["rope"] += 1
                v.wait_ge(filled[bank(("rope", i))], turn(("rope", i)))
                t = PS[bank(("rope", i))]
                TT(A(27)[0:m, :], t[0:m, :], A(26)[0:m, :], ALU.mult)\
                    .then_inc(freed[bank(("rope", i))], 1)
                v.wait_ge(freed[bank(("rope", i))], turn(("rope", i)))
                TT(x[0:m, :], x[0:m, :], A(25)[0:m, :], ALU.mult).then_inc(s_dve_step, 1)
                v.wait_ge(s_dve_step, tick(s_dve_step))
                TT(x[0:m, :], x[0:m, :], A(27)[0:m, :], ALU.add).then_inc(s_rope_tmp, 1)
                v.wait_ge(s_rope_tmp, tick(s_rope_tmp))

            def prep_a(p):
                v.wait_ge(s_bias_in, 16 * (p + 1))
                b = A(25 + p % 2)[:, 0:960].rearrange("p (r c) -> p r c", c=64)
                m = CST[:, CNB:CNB + 64].rearrange("p (o c) -> p o c", o=1).to_broadcast([P, 15, 64])
                TT(b, b, m, ALU.add).then_inc(s_dve_step, 1)
                v.wait_ge(s_dve_step, tick(s_dve_step))
                yield
                hn(A(8 + p % 2), par("gqa"))
                yield
                hn(A(10 + p % 2), par("gka"))
                yield
                yield
                yield

            def prep_bkv():
                v.wait_ge(s_tab_in, 32)
                for j in range(2):
                    hn(A(10 + j), par("gkb"))
                    rope(A(10 + j))
                    pad_keys(A(10 + j), A(18 + j))
                yield

            def prep_b(p):
                yield
                hn(A(8 + p % 2), par("gqb"))
                yield
                rope(A(8 + p % 2))
                yield

            def prep_c0():
                v.wait_ge(freed[bank(("hn", cnt["hn"]))], turn(("hn", cnt["hn"])))
                cnt["hn"] += 1
                v.reciprocal(A(23), A(23)).then_inc(s_dve_step, 1)
                v.wait_ge(s_dve_step, tick(s_dve_step))
                STT(A(18), A(18), par("gcq", 0), A(23), ALU.mult, ALU.mult).then_inc(s_dve_step, 1)
                v.wait_ge(s_dve_step, tick(s_dve_step))
                STT(A(19), A(19), par("gcq", 1), A(23), ALU.mult, ALU.mult).then_inc(s_hn_done, 1)
                v.wait_ge(s_hn_done, tick(s_hn_done))
                hn(A(28), par("gckv"))
                v.wait_ge(s_tab_in, 64)
                yield

            def prep_c(h):
                yield
                hn(A(8 + h % 2), par("gqc"), 96)
                yield
                rope(A(8 + h % 2), 96)
                yield
                hn(A(10 + h % 2), par("gkc"), 96)
                yield
                rope(A(10 + h % 2), 96)
                yield
                yield
                yield
                yield

            def prep_d(h):
                yield
                if h == 0:
                    v.wait_ge(s_tab_in, 96)
                hn(A(8 + h % 2), par("gqd"))
                yield
                rope(A(8 + h % 2))
                yield
                hn(A(10 + h % 2), par("gkd"))
                yield
                rope(A(10 + h % 2))
                pad_keys(A(10 + h % 2), (A(24), MSKF)[h % 2])
                yield
                yield
                yield
                yield

            def attend(kind, nu, scale, odst, gate, nv, o0):
                base = cnt["unit"]
                nm = 2 if kind == "D" else 1
                for s in range(nu + LAG + 1 + (3 if kind == "D" else 0)):
                    if s < nu:
                        b = base + s
                        if kind == "A" and s % 8 == 0:
                            x = A(8 + s // 8 % 2).rearrange("p (r c) -> p r c", c=64)
                            v.tensor_copy(QBD[0:64, :, 0:64], x[0:64]).then_inc(s_dve_step, 1)
                            v.wait_ge(s_dve_step, tick(s_dve_step))
                            v.tensor_copy(QBD[64:128, :, 64:128], x[64:128]).then_inc(s_qbd, 1)
                            v.wait_ge(s_qbd, tick(s_qbd))
                        mx = SM[:, 34 + 2 * 0:36]
                        c0 = 2 * (b % 2)
                        for m in range(nm):
                            v.wait_ge(filled[bank(("S", b, m))], turn(("S", b, m)))
                            t = PS[bank(("S", b, m))]
                            if kind == "A":
                                if b >= 2:
                                    v.wait_ge(filled[bank(("T", b - 2))], turn(("T", b - 2)))
                                p = (b // 8)
                                for rr in range(2):
                                    r = 2 * (b % 8) + rr
                                    off = min(max(r - 4, 0), 8) - r + 7
                                    step = STT(A(16 + b % 2)[:, rr * 512:rr * 512 + 512], t[:, rr * 512:rr * 512 + 512],
                                           0.125, A(25 + p % 2)[:, off * 64:off * 64 + 512], ALU.mult, ALU.add)
                                    if rr:
                                        step.then_inc(freed[bank(("S", b, 0))], 1)
                                        v.wait_ge(freed[bank(("S", b, 0))], turn(("S", b, 0)))
                                    else:
                                        step.then_inc(s_dve_step, 1)
                                        v.wait_ge(s_dve_step, tick(s_dve_step))
                                v.tensor_reduce(mx, A(16 + b % 2).rearrange("p (r c) -> p r c", r=2), AX.X, ALU.max).then_inc(s_dve_step, 1)
                                v.wait_ge(s_dve_step, tick(s_dve_step))
                                TS(SM[:, 20 + c0:22 + c0], mx, -1.0).then_inc(s_negmax, 1)
                                v.wait_ge(s_negmax, tick(s_negmax))
                            else:
                                v.tensor_reduce(mx[:, 0:1], t[:, :], AX.X, ALU.max).then_inc(s_dve_step, 1)
                                v.wait_ge(s_dve_step, tick(s_dve_step))
                                TS(SM[:, 20 + c0 + m:21 + c0 + m], mx[:, 0:1], -scale).then_inc(s_negmax, 1)
                                v.wait_ge(s_negmax, tick(s_negmax))
                    if LAG + 1 <= s < nu + LAG + 1:
                        u = s - LAG - 1
                        b = base + u
                        v.wait_ge(filled[bank(("O", b))], turn(("O", b)))
                        t = PS[bank(("O", b))]
                        oo, od = o0(u), odst(u)
                        q = slice((u % 8) * P, (u % 8) * P + P)
                        if kind == "D":
                            v.tensor_copy(od[:, q], t[:, 0:P])\
                                .then_inc(freed[bank(("O", b))], 1)
                            v.wait_ge(freed[bank(("O", b))], turn(("O", b)))
                        else:
                            gname, g = gate(u)
                            v.wait_ge(freed[bank(gname)], turn(gname))
                            if kind == "A":
                                for hh in range(2):
                                    e = slice(hh * 64, hh * 64 + 64)
                                    v.tensor_tensor(od[e, q].rearrange("p (r c) -> p r c", r=2),
                                                    t[e, 0:256].rearrange("p (r c) -> p r c", r=2)[:, :, hh * 64:hh * 64 + 64],
                                                    g[e, q].rearrange("p (r c) -> p r c", r=2), ALU.mult)\
                                        .then_inc(s_od_done if hh else s_dve_step, 1)
                                    v.wait_ge(s_od_done if hh else s_dve_step, tick(s_od_done if hh else s_dve_step))
                            else:
                                v.tensor_tensor(od[oo:oo + nv, q], t[oo:oo + nv, 0:P], g[oo:oo + nv, q], ALU.mult)\
                                    .then_inc(s_od_done, 1)
                                v.wait_ge(s_od_done, tick(s_od_done))
                            v.tensor_copy(SM[:, 36:37], t[:, 0:1] if nv == P else SM[:, 34:35])\
                                .then_inc(freed[bank(("O", b))], 1)
                            v.wait_ge(freed[bank(("O", b))], turn(("O", b)))
                    if s < nu:
                        b = base + s
                        if kind == "A":
                            v.wait_ge(s_pexp, b + 1)
                        for m in range(nm):
                            if kind != "A":
                                v.wait_ge(freed[bank(("S", b, m))], turn(("S", b, m)))
                        if b >= 2:
                            v.wait_ge(filled[bank(("T", b - 2))], turn(("T", b - 2)))
                        n2 = 2 if kind in "AD" else 1
                        rc = SM[:, 38:40]
                        pr = A(16 + (b % 2) * nm)
                        v.reciprocal(rc[:, 0:n2], SM[:, 24 + c0:24 + c0 + n2]).then_inc(s_dve_step, 1)
                        v.wait_ge(s_dve_step, tick(s_dve_step))
                        if kind == "A":
                            TS(pr[:, 0:512], pr[:, 0:512], rc[:, 0:1]).then_inc(s_dve_step, 1)
                            v.wait_ge(s_dve_step, tick(s_dve_step))
                            TS(pr[:, 512:L], pr[:, 512:L], rc[:, 1:2]).then_inc(s_probs, 1)
                            v.wait_ge(s_probs, tick(s_probs))
                        elif kind == "D":
                            TT(rc[:, 1:2], rc[:, 1:2], SM[:, 29:30], ALU.mult).then_inc(s_dve_step, 1)
                            v.wait_ge(s_dve_step, tick(s_dve_step))
                            TS(pr, pr, rc[:, 0:1]).then_inc(s_dve_step, 1)
                            v.wait_ge(s_dve_step, tick(s_dve_step))
                            STT(pr, A(17 + (b % 2) * nm), rc[:, 1:2], pr, ALU.mult, ALU.add).then_inc(s_probs, 1)
                            v.wait_ge(s_probs, tick(s_probs))
                        else:
                            TS(pr, pr, rc[:, 0:1]).then_inc(s_probs, 1)
                            v.wait_ge(s_probs, tick(s_probs))
                    yield
                cnt["unit"] += nu

            def att_a():
                return attend("A", 32, 1.0, lambda u: A(u // 8), lambda u: (("ga", u // 8), A(14 + u // 8 % 2)), P,
                              lambda u: 0)

            def att_b():
                return attend("B", 64, 0.125, lambda u: A(4 + u // 16),
                              lambda u: (("gb", u // 16), A(14 + u // 16 % 2)), 64, lambda u: (u // 8 % 2) * 64)

            def att_c():
                return attend("C", 64, 96 ** -0.5, lambda u: A(u // 16),
                              lambda u: (("gc", u // 16), A(14 + u // 16 % 2)), 64, lambda u: (u // 8 % 2) * 64)

            def att_d():
                steps = attend("D", 32, 0.125, lambda u: A(4 + u // 8), None, P, lambda u: 0)
                for s, _ in enumerate(steps):
                    yield
                    if s >= 8 and s % 8 == POST:
                        h = s // 8 - 1
                        v.wait_ge(freed[bank(("odn", h))], turn(("odn", h)))
                        v.reciprocal(A(23), A(23)).then_inc(s_dve_step, 1)
                        v.wait_ge(s_dve_step, tick(s_dve_step))
                        STT(A(4 + h), A(4 + h), SM[:, 28:29], A(23), ALU.mult, ALU.mult).then_inc(s_dve_step, 1)
                        v.wait_ge(s_dve_step, tick(s_dve_step))
                        v.wait_ge(freed[bank(("gd", h))], turn(("gd", h)))
                        TT(A(4 + h), A(4 + h), A(14 + h % 2), ALU.mult).then_inc(s_od_done, 1)
                        v.wait_ge(s_od_done, tick(s_od_done))

            v.memset(AR[:, 4:6, :], 0.0).then_inc(s_dve_step, 1)
            v.wait_ge(s_dve_step, tick(s_dve_step))
            weave(prep_a(0), ())
            weave(att_a(), chain(8, prep_a(1), prep_a(2), prep_a(3)))
            weave(prep_bkv(), ())
            weave(prep_b(0), ())
            weave(att_b(), chain(16, prep_b(1), prep_b(2), prep_b(3)))
            residual("wout_e")
            norm(4, "no", XN)
            v.wait_ge(freed[bank(("lam",))], turn(("lam",)))
            TT(SM[:, 29:30], SM[:, 33:34], SM[:, 32:33], ALU.subtract).then_inc(s_dve_step, 1)
            v.wait_ge(s_dve_step, tick(s_dve_step))
            TS(SM[:, 29:30], SM[:, 29:30], -LAM_INIT, None, ALU.add).then_inc(s_dve_step, 1)
            v.wait_ge(s_dve_step, tick(s_dve_step))
            TS(SM[:, 28:29], par("gsub"), 1.0 - LAM_INIT).then_inc(s_dve_step, 1)
            v.wait_ge(s_dve_step, tick(s_dve_step))
            weave(prep_c0(), ())
            weave(prep_c(0), ())
            weave(att_c(), chain(8, *[prep_c(h) for h in range(1, 8)]))
            weave(prep_d(0), ())
            weave(att_d(), chain(8, *[prep_d(h) for h in range(1, 4)]))
            residual("wout_o")

        @block.gpsimd
        def _(pool):
            pool.wait_ge(s_bd_zero, 1)
            bd = A(20).rearrange("p (i f c) -> p i f c", i=2, c=P)
            for i, w in enumerate((a["lru_wa"][0], a["lru_wx"][0])):
                wv = w.rearrange("(f two) d e -> two d f e", two=2)
                for j in range(2):
                    pool.dma_start(bd[j * 64:j * 64 + 64, i, :, j * 64:j * 64 + 64], wv[j]).then_inc(s_bd_in, 16)
            pool.wait_ge(s_bd_in, 64)


def rotation(ang):
    return np.cos(ang).astype(np.float32), np.sin(ang).astype(np.float32)


def constants():
    cst = np.zeros((P, NCST), np.float32)

    def put(name, m):
        cst[:m.shape[0], CM[name]:CM[name] + m.shape[1]] = m
    i = np.arange(P)
    put("ident", np.eye(P))
    put("tri", (i[:, None] <= i[None, :]) * 1.0)
    put("neg", np.where(i[:, None] <= i[None, :], 0.0, -1e30))
    put("blk64", (i[:, None] // 64 == i[None, :] // 64) / 64.0)
    put("o1024", np.full((P, P), 1 / 1024.0))
    put("o128", np.full((P, P), 1 / 128.0))
    put("o256", np.full((P, P), 1 / 256.0))
    put("o96", np.full((P, P), 1 / 96.0))
    put("one", np.ones((P, P)))
    c = i % 64
    c0 = np.clip(c - 8, 0, 48)
    kc = np.arange(64)
    cst[:, CNB:CNB + 64] = np.where((kc[None] >= c0[:, None]) & (kc[None] < c0[:, None] + 16), 0.0, -1e30)
    cst[:, CEPS] = EPS
    cst[:, CONE] = 1.0
    msk = np.zeros((P, NLEV + 1, P), np.int32)
    for l in range(NLEV):
        s = 64 >> l
        msk[:, l] = ((i[:, None] // (2 * s) == i[None] // (2 * s)) & ((i[:, None] // s) % 2 == 0)
                     & ((i[None] // s) % 2 == 1))
    msk[:, NLEV] = np.eye(P)
    f = np.float32
    t = np.arange(L)

    def angles(pos, dim, theta):
        inv = np.power(f(theta), -np.arange(0, dim, 2, dtype=np.float32) / f(dim)).astype(np.float32)
        return pos.astype(np.float32)[:, None] * inv[None]
    rope = np.zeros((6, P, L), np.float32)

    def table(w, name, starts):
        perm = np.zeros((P, P))
        rope[2 * w] = 1.0
        for d0, half, ang in starts:
            co, si = rotation(ang)
            for j in range(half):
                rope[2 * w, d0 + j] = rope[2 * w, d0 + half + j] = co[:, j]
                rope[2 * w + 1, d0 + j] = -si[:, j]
                rope[2 * w + 1, d0 + half + j] = si[:, j]
                perm[d0 + j, d0 + half + j] = perm[d0 + half + j, d0 + j] = 1.0
        put(name, perm)
    row, col = angles(t // 64, 32, 10000.0), angles(t % 64, 32, 10000.0)
    table(0, "pB", [(b + o, 16, ang) for b in (0, 64) for o, ang in ((0, row), (32, col))])
    table(1, "pC", [(64, 16, angles(t, 32, 10000.0))])
    part = angles(t, 16, 500000.0)
    table(2, "pD", [(b, 8, part) for b in (0, 64)])
    return cst, msk.reshape(P, -1), rope


def pack(x):
    par = np.zeros((P, NPAR), np.float32)

    def put(name, v):
        v = np.asarray(v, dtype=np.float32)
        if v.ndim == 1:
            v = v.reshape(-1, P) if v.size >= P else v.reshape(1, -1)
        c = PC[name]
        par[:v.shape[1], c:c + v.shape[0]] = v.T
    g = lambda n: np.asarray(x[n])
    put("nmix", g("norm_mix_w")[0])
    put("nffn", g("norm_ffn_w")[0])
    put("nf", g("norm_f_w"))
    put("ne", g("norm_e_2")[0])
    put("no", g("norm_o_2")[0])
    put("hnw", g("hgrn_norm_w")[0])
    put("gnw", g("gla_norm_w")[0])
    put("scw", g("ssd_conv_w")[0].reshape(-1))
    put("scb", g("ssd_conv_b")[0])
    put("lcw", g("lru_conv_w")[0].reshape(-1))
    put("lcb", g("lru_conv_b")[0])
    put("ba", g("lru_ba")[0])
    put("bx", g("lru_bx")[0])
    put("lam", g("lru_lambda")[0])
    put("gb", g("gla_gate_b")[0])
    put("sd", np.repeat(g("ssd_d")[0], 64))
    put("snw", g("ssd_norm_w")[0])
    put("dtb", g("ssd_dt_bias")[0])
    put("alog", g("ssd_a_log")[0])
    for k, n in (("gqa", "gq_a_2"), ("gka", "gk_a_2"), ("gqb", "gq_b_2"), ("gkb", "gk_b_2"),
                 ("gqd", "gq_d_2"), ("gkd", "gk_d_2")):
        put(k, np.tile(g(n)[0], 2))
    put("gcq", g("g_cq_2")[0])
    put("gckv", g("g_ckv_2")[0])
    put("gqc", g("gq_c_2")[0])
    put("gkc", g("gk_c_2")[0])
    put("gsub", g("g_sub_d_2")[0])
    for k, n in (("lq1", "lam_q1_2"), ("lk1", "lam_k1_2"), ("lq2", "lam_q2_2"), ("lk2", "lam_k2_2")):
        put(k, g(n)[0])
    return par


def kernel(**inputs):
    import numpy as _np
    import concourse.bacc as _bacc
    from concourse.bass_utils import run_bass_kernel_spmd as _run

    nc = _bacc.Bacc("TRN2", target_bir_lowering=False, num_devices=1)
    arrays, a = {}, {}

    def give(name, arr):
        arr = _np.ascontiguousarray(arr)
        arrays[f"in_{name}"] = arr
        a[name] = nc.dram_tensor(f"in_{name}", arr.shape, mybir.dt.from_np(arr.dtype), kind="ExternalInput").ap()

    for n in ("x", "w_in", "w_branch", "w_out", "w_ffn_in", "w_ffn_out", "w_in_e_2", "w_out_e_2", "w_in_o_2",
              "w_out_o_2", "w_cq_b_2", "w_ckv_b_2", "gla_gate_w", "lru_wa", "lru_wx"):
        give(n, inputs[n])
    cst, msk, rope = constants()
    give("cst", cst)
    give("msk", msk)
    give("rope", rope)
    give("par", pack(inputs))
    r = _np.pad(_np.asarray(inputs["rpb_a_2"])[0], ((0, 0), (0, 0), (48, 48)))
    r = _np.lib.stride_tricks.sliding_window_view(r, 64, axis=2)[:, :, ::-1, :].transpose(0, 2, 1, 3)
    give("rpb", _np.ascontiguousarray(r).reshape(4, 128, 960))
    a["out"] = nc.dram_tensor("out", (1, L, D), F32, kind="ExternalOutput").ap()
    build(nc, a)
    res = _run(nc, [arrays], core_ids=[0])
    return res.results[0]["out"]
```

```python
from contextlib import ExitStack
import math
import numpy as np
import concourse.bass as bass
from concourse import mybir

F32 = mybir.dt.float32
F32R = mybir.dt.float32r
I32 = mybir.dt.int32
ALU = mybir.AluOpType
ACT = mybir.ActivationFunctionType
AX = mybir.AxisListType

P = 128
D = 1024
L = 1024
KD = D // P
NT = L // P
EPS = 1e-6

HQ, HF, HI, HG = 0, 512, 1024, 1536
SZ, SX, SDT = 2048, 2560, 3328
GQ, GK, GV, GG, GLR = 3336, 3592, 3848, 4360, 4872
LX, LG, MG = 4888, 5400, 5912
DFF = 2816
NF = DFF // P
EQA, EKA, EVA, EQB, EKB, EVB, EG = 0, 512, 1024, 1536, 2048, 2176, 2304
OCQ, OCKV, OKPE, OQD, OKD, OVD, OG = 0, 256, 384, 416, 928, 1440, 1952
LAM_INIT = 0.8 - 0.6 * math.exp(-0.3)
LAG = 2
POST = 5
NLEV = 7

PC = {}
_at = 0
for _name, _n in [("nmix", 8), ("nffn", 8), ("nf", 8), ("ne", 8), ("no", 8), ("hnw", 1), ("gnw", 1),
                  ("scw", 24), ("scb", 6), ("lcw", 16), ("lcb", 4), ("ba", 4), ("bx", 4), ("lam", 4),
                  ("gb", 2), ("sd", 4), ("snw", 4), ("dtb", 1), ("alog", 1), ("gqa", 1), ("gka", 1),
                  ("gqb", 1), ("gkb", 1), ("gcq", 2), ("gckv", 1), ("gqc", 1), ("gkc", 1), ("gqd", 1),
                  ("gkd", 1), ("gsub", 1), ("lq1", 1), ("lk1", 1), ("lq2", 1), ("lk2", 1)]:
    PC[_name] = _at
    _at += _n
NPAR = _at
CM = {n: i * P for i, n in enumerate(["ident", "tri", "neg", "blk64", "o1024", "o128", "o256", "o96",
                                      "one", "pB", "pC", "pD"])}
CNB = len(CM) * P
CEPS = CNB + 64
CONE = CEPS + 1
NCST = CONE + 1



def build(nc, a):
    with ExitStack() as ctx:
        def sb(name, shape, dt=F32):
            return ctx.enter_context(nc.sbuf_tensor(name, shape, dt))

        def room():
            return (nc.sbuf_base + 31) // 32 * 32

        h_at = room()
        H = sb("H", [P, KD, L])
        XH = sb("XH", [P, KD, L], F32R)
        XL = nc.alloc_sbuf_tensor_at("XL", [P, KD, L], F32R, offset=h_at)
        AR = sb("AR", [P, 29, L])
        w_at = room()
        WR = sb("WR", [P, 4, 8, P])
        WH = sb("WH", [P, 4, 8, P], F32R)
        WL = nc.alloc_sbuf_tensor_at("WL", [P, 4, 8, P], F32R, offset=w_at)
        CST = sb("CST", [P, NCST])
        MSK = sb("MSK", [P, NLEV + 1, P], I32)
        PAR = sb("PAR", [P, NPAR])
        SM = sb("SM", [P, 40])
        PS = [ctx.enter_context(nc.psum_tensor(f"ps{i}", [P, L], F32)) for i in range(4)]
        def sem(name):
            return ctx.enter_context(nc.semaphore(name))

        s_cst_in = sem("cst_in")
        s_dve_step = sem("dve_step")
        s_act_step = sem("act_step")
        s_nsq = sem("nsq")
        s_sumsq = sem("sumsq")
        s_normed = sem("normed")
        s_xhi = sem("xhi")
        s_xlo = [sem("xlo_even"), sem("xlo_odd")]
        s_whi = sem("whi")
        s_wsplit = sem("wsplit")
        s_spilled = sem("spilled")
        h_in = [sem(f"h_in{k}") for k in range(KD)]
        s_conv = sem("conv")
        s_ssd_silu = sem("ssd_silu")
        s_dt_ln = sem("dt_ln")
        s_dt_done = sem("dt_done")
        s_nega = sem("nega")
        s_dec_in = sem("dec_in")
        s_dec_ready = sem("dec_ready")
        s_xdt = sem("xdt")
        s_ea = sem("ea")
        s_segm = sem("segm")
        s_lmat = sem("lmat")
        s_mc = sem("mc")
        s_yz = sem("yz")
        s_ysq = sem("ysq")
        s_ys = sem("ys")
        s_ssd_state = sem("ssd_state")
        s_lnr = sem("lnr")
        s_expo = sem("expo")
        s_expd = sem("expd")
        s_xlev = sem("xlev")
        s_kdec = sem("kdec")
        s_qdec = sem("qdec")
        s_a_done = sem("a_done")
        s_g_state = sem("g_state")
        s_osq = sem("osq")
        s_bd_zero = sem("bd_zero")
        s_bd_in = sem("bd_in")
        s_dec_exp = sem("dec_exp")
        s_lru_q = sem("lru_q")
        s_lru_b = sem("lru_b")
        s_lsp_in = sem("lsp_in")
        s_merge_add = sem("merge_add")
        s_hn_done = sem("hn_done")
        s_rope_tmp = sem("rope_tmp")
        s_tab_in = sem("tab_in")
        s_vs_in = sem("vs_in")
        s_bias_in = sem("bias_in")
        s_negmax = sem("negmax")
        s_pexp = sem("pexp")
        s_probs = sem("probs")
        s_qbd = sem("qbd")
        s_kz = sem("kz")
        s_lam_e = sem("lam_e")
        s_out_in = sem("out_in")
        s_half_in = sem("half_in")
        s_kraw = sem("kraw")
        s_od_done = sem("od_done")
        s_lamv = sem("lamv")
        filled = [ctx.enter_context(nc.semaphore(f"filled{i}")) for i in range(4)]
        freed = [ctx.enter_context(nc.semaphore(f"freed{i}")) for i in range(4)]
        w_in = [ctx.enter_context(nc.semaphore(f"w_in{i}")) for i in range(4)]

        def A(i):
            return AR[:, i, :]

        def par(name, j=0, p=P):
            c = PC[name] + j
            return PAR[0:p, c:c + 1]

        def cm(name, p=P, q=P):
            return CST[0:p, CM[name]:CM[name] + q]

        IDENT = cm("ident")
        QBD = AR[:, 4:6, :].rearrange("p a (r c) -> p (a r) c", c=P)
        MSKF = MSK[:, :, :].rearrange("p a b -> p (a b)").bitcast(F32)
        epsc = CST[:, CEPS:CEPS + 1]

        def tt(ap):
            return ap.rearrange("p (t i) -> p t i", i=P)

        J = {}
        njobs = [0]
        loads = []
        splits = []
        nw = [0]
        nsplit = [0]

        def bank(name):
            return J[name] % 4

        def turn(name):
            return J[name] // 4 + 1

        XLEV = [21, 22, 28]
        LX_RAW, LXC, LX_GATE = [17, 24], [23, 25], [16, 26]
        FILL = {1: {0: [("g", 0)], 2: [("v", 0)], 4: [("vt", 0)]},
                2: {-1: [("g", 0)], 0: [("g", 1)], 1: [("v", 0)], 2: [("vt", 0), ("v", 1)], 4: [("vt", 1)]}}

        def norm_turn(i):
            return i - (i > 2)

        block = ctx.enter_context(nc.Block())

        def weave(main, side):
            main, side = iter(main), iter(side)
            for _ in main:
                next(side, None)
            for _ in side:
                pass

        def chain(steps, *preps):
            for prep in preps:
                n = 0
                for _ in prep:
                    n += 1
                    yield
                assert n <= steps
                for _ in range(steps - n):
                    yield

        win, wbr, wout, wfi, wfo = a["w_in"][0], a["w_branch"][0], a["w_out"][0], a["w_ffn_in"][0], a["w_ffn_out"][0]
        wie, woe, wio, woo = a["w_in_e_2"][0], a["w_out_e_2"][0], a["w_in_o_2"][0], a["w_out_o_2"][0]
        wcq, wckv = a["w_cq_b_2"][0], a["w_ckv_b_2"][0]

        def cols(w, c0, m=P, k0=0, nk=8):
            return w[k0 * P:(k0 + nk) * P, c0:c0 + m].rearrange("(k p) c -> p k c", p=P)

        @block.tensor
        def _(pe):
            def opn(name):
                n = njobs[0]
                njobs[0] += 1
                assert name not in J, name
                J[name] = n
                return PS[n % 4], n

            def weight(src, n, m=P, kp=P, nk=8, dup=False):
                w = nw[0]
                nw[0] += 1
                loads.append((src, n, m, kp, nk, dup))
                return w

            def gemm(name, src, rhs, m=P, kp=P, nk=8, dup=False):
                pt, n = opn(name)
                pe.wait_ge(freed[n % 4], n // 4)
                w = weight(src, n, m, kp, nk, dup)
                pe.wait_ge(w_in[w % 4], 16 * (w // 4 + 1))
                for h in range(2):
                    for k in range(nk):
                        mm = pe.matmul(pt[0:m, h * 512:h * 512 + 512], WR[0:kp, w % 4, k, 0:m],
                                       rhs(k)[0:kp, h * 512:h * 512 + 512], start=k == 0, stop=k == nk - 1)
                mm.then_inc(filled[n % 4], 1)

            def three(pt, slot, m, norm):
                for h in range(2):
                    first = norm is not None and h == 0
                    passes = [(k, WH, XH) for k in range(KD)] + [(k, WL, XH) for k in range(KD)] \
                        + [(k, WH, XL) for k in range(KD)]
                    for i, (k, wp, xp) in enumerate(passes):
                        if first and i < KD:
                            pe.wait_ge(s_xhi, norm_turn(norm) * KD + k + 1)
                        if first and xp is XL:
                            pe.wait_ge(s_xlo[k % 2], norm_turn(norm) * (KD // 2) + k // 2 + 1)
                        mm = pe.matmul(pt[0:m, h * 512:h * 512 + 512], wp[:, slot, k, 0:m],
                                       xp[:, k, h * 512:h * 512 + 512], start=i == 0, stop=i == 3 * KD - 1)
                return mm

            def xgemm(name, src, m=P, dup=False, norm=None):
                pt, n = opn(name)
                pe.wait_ge(freed[n % 4], n // 4)
                w = weight(src, n, m, P, 8, dup)
                splits.append(("weight", w, m))
                nsplit[0] += 1
                pe.wait_ge(s_wsplit, nsplit[0])
                if norm is not None:
                    splits.append(("norm", norm))
                three(pt, w % 4, m, norm).then_inc(filled[n % 4], 1)

            def transposes(name, src, p=P, m=P):
                pt, n = opn(name)
                pe.wait_ge(freed[n % 4], n // 4)
                for t in range(NT):
                    mm = pe.transpose(pt[:, t * P:t * P + P], src[:, t * P:t * P + P], IDENT)
                mm.then_inc(filled[n % 4], 1)

            def reduce_job(name, mat, srcs, m=P):
                pt, n = opn(name)
                pe.wait_ge(freed[n % 4], n // 4)
                for h in range(2):
                    for i, s in enumerate(srcs):
                        mm = pe.matmul(pt[0:m, h * 512:h * 512 + 512], mat, s[0:m, h * 512:h * 512 + 512],
                                       start=i == 0, stop=i == len(srcs) - 1)
                mm.then_inc(filled[n % 4], 1)

            def norm(i):
                pe.wait_ge(s_sumsq, (i + 1) * (KD - 1))
                reduce_job(("norm", i), cm("o1024"), [A(28)])

            pe.wait_ge(s_cst_in, 16 * 11)
            for f in range(KD):
                pt, n = opn(("x", f))
                if n >= 4:
                    pe.wait_ge(freed[n % 4], n // 4)
                for t in range(NT):
                    mm = pe.transpose(pt[:, t * P:t * P + P], AR[:, t, f * P:f * P + P], IDENT)
                mm.then_inc(filled[n % 4], 1)
            norm(0)

            for f in range(6):
                xgemm(("sx", f), cols(win, SX + f * P), norm=0 if f == 0 else None)
            xgemm(("dt",), cols(win, SDT, 8), m=8)
            for f in range(4):
                xgemm(("z", f), cols(win, SZ + f * P))
            for f in range(4):
                pe.wait_ge(s_ssd_silu, f + 1)
                if f == 0:
                    pe.wait_ge(s_dt_done, 1)
                    pt, n = opn(("dtt",))
                    pe.wait_ge(freed[n % 4], n // 4)
                    for i, src in enumerate((A(0), A(2))):
                        for t in range(NT):
                            mm = pe.matmul(pt[:, i * 64 + t * 8:i * 64 + t * 8 + 8], src[0:8, t * P:t * P + P],
                                           IDENT[0:8, 0:8], start=True, stop=True)
                    mm.then_inc(filled[n % 4], 1)
                    pe.wait_ge(freed[bank(("dtt",))], turn(("dtt",)))
                    pt, n = opn(("acs",))
                    pe.wait_ge(freed[n % 4], n // 4)
                    pe.matmul(pt[:, 0:64], cm("tri"), A(27)[:, 64:128], start=True, stop=True)
                    mm = pe.matmul(pt[:, 64:128], cm("one"), A(27)[:, 64:128], start=True, stop=True)
                    mm.then_inc(filled[n % 4], 1)
                transposes(("xt", f), A(8 + f))
            pe.wait_ge(s_ssd_silu, 6)
            transposes(("Bt",), A(12))
            for g in range(2):
                pt, n = opn(("CB", g))
                pe.wait_ge(freed[n % 4], n // 4)
                q = slice(g * 64, g * 64 + 64)
                for t in range(NT):
                    mm = pe.matmul(pt[:, t * P:t * P + P], A(12)[q, t * P:t * P + P], A(13)[q, t * P:t * P + P],
                                   start=True, stop=True)
                mm.then_inc(filled[n % 4], 1)
            pe.wait_ge(freed[bank(("Bt",))], turn(("Bt",)))
            pe.wait_ge(s_xdt, 4)
            xdt = AR[:, 17:21, :].rearrange("p a (b c) -> p (a b) c", c=512)
            xdd = AR[:, 21:25, :].rearrange("p a (b c) -> p (a b) c", c=512)
            sst = AR[:, 0:4, :].rearrange("p a (b c) -> p (a b) c", c=512)
            for j in range(4):
                pt, n = opn(("sU", j))
                pe.wait_ge(freed[n % 4], n // 4)
                for i in range(2 if j < 3 else 1):
                    t = 2 * j + i
                    mm = pe.matmul(pt[:, i * 512:i * 512 + 512], A(14)[:, t * P:t * P + P], xdd[:, t, :],
                                   start=True, stop=True)
                mm.then_inc(filled[n % 4], 1)

            def seg(h):
                pt, n = opn(("seg", h))
                pe.wait_ge(freed[n % 4], n // 4)
                for t in range(NT):
                    c = 64 + t * 8 + h
                    mm = pe.matmul(pt[:, t * P:t * P + P], A(27)[:, c:c + 1].to_broadcast([P, P]), cm("tri"),
                                   start=True, stop=True)
                mm.then_inc(filled[n % 4], 1)
            def gla_q(u):
                xgemm(("q", u), cols(win, HQ + u * P if u < 4 else GQ + (u - 4) * P))

            def gla_k(u):
                xgemm(("k", u), cols(win, HF + u * P if u < 4 else GK + (u - 4) * P))

            seg(0)
            seg(1)
            for f in range(4):
                if f < 3:
                    seg(2 * f + 2)
                else:
                    gla_q(0)
                pe.wait_ge(s_mc, 2 * f + 2)
                pe.wait_ge(s_ssd_state, 7)
                pt, n = opn(("y", f))
                pe.wait_ge(freed[n % 4], n // 4)
                for hh in range(2):
                    h = 2 * f + hh
                    g = slice((h // 4) * 64, (h // 4) * 64 + 64)
                    o = slice(hh * 64, hh * 64 + 64)
                    for t in range(NT):
                        c = slice(t * P, t * P + P)
                        mm = pe.matmul(pt[o, c], xdt[:, t, h * 64:h * 64 + 64], A(21 + hh)[:, c],
                                       start=True, stop=t == 0)
                        if t:
                            mm = pe.matmul(pt[o, c], sst[g, t, h * 64:h * 64 + 64], A(23 + hh)[g, c],
                                           start=False, stop=True)
                mm.then_inc(filled[n % 4], 1)
                if f < 3:
                    seg(2 * f + 3)
                if f == 3:
                    gla_k(0)
                if f % 2:
                    pe.wait_ge(s_ysq, f + 1)
                    reduce_job(("yn", f // 2), cm("o256"), [A(12), A(14)])

            for u in range(6):
                nh = 1 if u < 4 else 2
                if u == 4:
                    xgemm(("glr",), cols(win, GLR, 16), m=16)
                if u < 4:
                    vc, gc = [HI + u * P], [HG + u * P]
                else:
                    w = u - 4
                    pe.wait_ge(freed[bank(("glr",))], turn(("glr",)))
                    gemm(("gz", u), a["gla_gate_w"][0][:, w * P:w * P + P], rhs=lambda k: A(11), kp=16, nk=1)
                    vc = [GV + (2 * w + hh) * P for hh in range(2)]
                    gc = [GG + (2 * w + hh) * P for hh in range(2)]
                dk = P // nh
                pe.wait_ge(freed[bank(("q", u))], turn(("q", u)))
                pe.wait_ge(freed[bank(("k", u))], turn(("k", u)))
                for l in range(-1, NLEV):
                    if l >= 0:
                        pe.wait_ge(s_xlev, u * NLEV + l + 1)
                    x1, x2 = (A(17), A(16)) if l < 0 else (A(XLEV[l % 3]),) * 2
                    for hh in range(nh):
                        pt, n = opn(("P", u, l, hh))
                        pe.wait_ge(freed[n % 4], n // 4)
                        r = slice(hh * dk, hh * dk + dk)
                        for t in range(NT):
                            c = slice(t * P, t * P + P)
                            mm = pe.matmul(pt[:, c], x1[r, c], x2[r, c], start=True, stop=True)
                        mm.then_inc(filled[n % 4], 1)
                    for kind, hh in FILL[nh].get(l, ()):
                        if kind == "g":
                            xgemm(("g", u, hh), cols(win, gc[hh]))
                        elif kind == "v":
                            xgemm(("v", u, hh), cols(win, vc[hh]))
                        else:
                            pe.wait_ge(freed[bank(("v", u, hh))], turn(("v", u, hh)))
                            transposes(("vt", u, hh), A(24))
                pe.wait_ge(s_kdec, u + 1)
                transposes(("kdt", u), A(15))
                if u < 4:
                    gla_q(u + 1)
                elif u == 4:
                    gla_k(u + 1)
                else:
                    xgemm(("lx", 0), cols(win, LX))
                pe.wait_ge(freed[bank(("kdt", u))], turn(("kdt", u)))
                vtok = [A(25), A(13)]
                for hh in range(nh):
                    pe.wait_ge(freed[bank(("vt", u, hh))], turn(("vt", u, hh)))
                pt, n = opn(("U", u))
                pe.wait_ge(freed[n % 4], n // 4)
                for hh in range(nh):
                    for t in range(NT - 1):
                        c = slice(t * P, t * P + P)
                        mm = pe.matmul(pt[hh * dk:hh * dk + dk, c], A(27)[:, t * P + hh * dk:t * P + hh * dk + dk],
                                       vtok[hh][:, c], start=True, stop=True)
                mm.then_inc(filled[n % 4], 1)
                if u < 4:
                    gla_k(u + 1)
                elif u == 4:
                    gla_q(u + 1)
                else:
                    xgemm(("lg", 0), cols(win, LG))
                pe.wait_ge(s_a_done, u + 1)
                pe.wait_ge(s_g_state, u + 1)
                for hh in range(nh):
                    am = [A(23), A(12)][hh]
                    r = slice(hh * dk, hh * dk + dk)
                    pt, n = opn(("o", u, hh))
                    pe.wait_ge(freed[n % 4], n // 4)
                    for t in range(NT):
                        c = slice(t * P, t * P + P)
                        mm = pe.matmul(pt[:, c], vtok[hh][:, c], am[:, c], start=True, stop=t == 0)
                        if t:
                            mm = pe.matmul(pt[:, c], A(19)[r, c], A(16)[r, c], start=False, stop=True)
                    mm.then_inc(filled[n % 4], 1)
                    pe.wait_ge(freed[bank(("o", u, hh))], turn(("o", u, hh)))
                    reduce_job(("on", u, hh), cm("o128"), [A(21)])

            for f in range(4):
                if f < 3:
                    xgemm(("lx", f + 1), cols(win, LX + (f + 1) * P))
                pe.wait_ge(s_conv, 6 + f + 1)
                pe.wait_ge(s_bd_in, 64)
                for i, nm in enumerate(("lr", "li")):
                    pt, n = opn((nm, f))
                    pe.wait_ge(freed[n % 4], n // 4)
                    for h in range(2):
                        mm = pe.matmul(pt[:, h * 512:h * 512 + 512], A(20)[:, (i * 4 + f) * P:(i * 4 + f) * P + P],
                                       A(LXC[f % 2])[:, h * 512:h * 512 + 512], start=True, stop=True)
                    mm.then_inc(filled[n % 4], 1)
                if f < 3:
                    xgemm(("lg", f + 1), cols(win, LG + (f + 1) * P))
            def run(name, iters, jobs, first=None, norm=None, ready={}):
                n0, w0 = njobs[0], nw[0]
                nj = len(jobs)
                nwt = sum(len(ws) for ws, _ in jobs)
                assert nj % 4 == 0 and nwt % 4 == 0
                J[name] = n0
                body = []
                for k, (ws, _) in enumerate(jobs):
                    for src, nk in ws:
                        body.append((src, n0 + k, nk))
                loads.append(("run", iters, nj, body))
                ns0 = nsplit[0]
                per = sum(rhs is None for _, rhs in jobs)
                if per:
                    splits.extend(("weight", w0 + i * nwt + at, P) for i in range(iters)
                                  for at, (_, rhs) in enumerate(jobs) if rhs is None)
                    if norm is not None:
                        splits.insert(len(splits) - per * iters + 2, ("norm", norm))
                nsplit[0] += per * iters
                njobs[0] += nj * iters
                nw[0] += nwt * iters
                with pe.Fori(0, iters) as i:
                    w, ns = w0, ns0
                    for k, (ws, rhs) in enumerate(jobs):
                        n = n0 + k
                        pe.wait_ge(freed[n % 4], i * (nj // 4) + n // 4)
                        pt = PS[n % 4]
                        if rhs is None:
                            ns += 1
                            pe.wait_ge(s_wsplit, i * per + ns)
                            mm = three(pt, w % 4, P, norm if k == 0 else None)
                            w += 1
                            mm.then_inc(filled[n % 4], 1)
                            continue
                        tot = sum(nk for _, nk in ws)
                        at = 0
                        for src, nk in ws:
                            if k in ready:
                                pe.wait_ge(s_ys, ready[k])
                            pe.wait_ge(w_in[w % 4], i * (nwt // 4 * 16) + 16 * (w // 4 + 1))
                            for h in range(2):
                                for kk in range(nk):
                                    c = at + kk
                                    if first and k == 0 and h == 0:
                                        first(c)
                                    mm = pe.matmul(pt[:, h * 512:h * 512 + 512], WR[:, w % 4, kk, :],
                                                   rhs(c)[:, h * 512:h * 512 + 512],
                                                   start=c == 0, stop=c == tot - 1)
                            at += nk
                            w += 1
                        mm.then_inc(filled[n % 4], 1)

            jobs = []
            for b in range(4):
                jobs.append(([(lambda i, b=b: (win, MG + b * D, i, 1, 0), 8)], None))
                jobs.append(([(lambda i, b=b: (wbr[b], 0, i, 1, 0), 4)], lambda k, b=b: A(4 * b + k)))
            run("merge", KD, jobs, ready={1: 12, 7: 16})

            def proj(name, w, rhs, chunks, first):
                run(name, 2, [([(lambda i, j=j, k0=k0: (w, j * P, i, 4, k0), nk) for k0, nk in chunks], rhs)
                              for j in range(4)], first)
            proj("wout", wout, lambda k: A(16 + k), [(0, 8)], lambda k: pe.wait_ge(s_merge_add, 3 * (k + 1)))
            norm(1)
            run("ffn_in", NF // 2, [([(lambda i, j=j, s=s: (wfi, s * DFF + j * P, i, 2, 0), 8)], None)
                                    for j in range(2) for s in range(2)], norm=1)

            def hidden(k):
                n = J["ffn_in"] + 2 * k + 1
                pe.wait_ge(freed[n % 4], n // 4 + 1)
            proj("ffn_out", wfo, lambda k: A(k), [(0, 8), (8, 8), (16, 6)], hidden)
            norm(2)

            def rope(i, mat, x, m=P):
                pe.wait_ge(s_hn_done, i + 1)
                pt, n = opn(("rope", i))
                pe.wait_ge(freed[n % 4], n // 4)
                for h in range(2):
                    mm = pe.matmul(pt[0:m, h * 512:h * 512 + 512], mat, x[0:m, h * 512:h * 512 + 512],
                                   start=True, stop=True)
                mm.then_inc(filled[n % 4], 1)

            cnt = {"hn": 0, "s": 0, "unit": 0}

            def hn(name, mat, m=P):
                pe.wait_ge(freed[bank(name)], turn(name))
                reduce_job(("hn", cnt["hn"]), mat, [A(22)], m)
                cnt["hn"] += 1

            def prep_a(p):
                xgemm(("qa", p), cols(wie, EQA + p * P), norm=3 if p == 0 else None)
                yield
                hn(("qa", p), cm("blk64"))
                xgemm(("ka", p), cols(wie, EKA + p * P))
                yield
                xgemm(("va", p), cols(wie, EVA + p * P))
                yield
                hn(("ka", p), cm("blk64"))
                pe.wait_ge(freed[bank(("va", p))], turn(("va", p)))
                transposes(("vat", p), A(27))
                yield
                xgemm(("ga", p), cols(wie, EG + p * P))
                yield

            def prep_bkv():
                for j in range(2):
                    xgemm(("kb", j), cols(wie, EKB + j * 64, 64), dup=True)
                    hn(("kb", j), cm("blk64"))
                    rope(cnt["hn"] - 1, cm("pB"), A(10 + j))
                xgemm(("vb",), cols(wie, EVB))
                pe.wait_ge(freed[bank(("vb",))], turn(("vb",)))
                transposes(("vbt",), A(27))
                yield

            def prep_b(p):
                xgemm(("qb", p), cols(wie, EQB + p * P))
                yield
                hn(("qb", p), cm("blk64"))
                xgemm(("gb", p), cols(wie, EG + 512 + p * P))
                yield
                yield
                rope(cnt["hn"] - 1, cm("pB"), A(8 + p % 2))
                yield

            def prep_c0():
                xgemm(("cq", 0), cols(wio, OCQ), norm=4)
                xgemm(("cq", 1), cols(wio, OCQ + P))
                pe.wait_ge(freed[bank(("cq", 0))], turn(("cq", 0)))
                pe.wait_ge(freed[bank(("cq", 1))], turn(("cq", 1)))
                reduce_job(("hn", cnt["hn"]), cm("o256"), [A(22), A(24)])
                cnt["hn"] += 1
                xgemm(("ckv",), cols(wio, OCKV))
                hn(("ckv",), cm("o128"))
                xgemm(("kpe",), cols(wio, OKPE, 32), m=32)
                pe.wait_ge(s_hn_done, cnt["hn"])
                yield

            def prep_c(h):
                gemm(("qc", h), cols(wcq, h * 96, 96, nk=2), rhs=lambda k: A(18 + k), m=96, nk=2)
                yield
                hn(("qc", h), cm("o96", 96, 96), 96)
                if h % 2 == 0:
                    xgemm(("gc", h // 2), cols(wio, OG + h // 2 * P))
                yield
                gemm(("kc", h), cols(wckv, h * 128, 64, nk=1), rhs=lambda k: A(28), m=64, nk=1)
                yield
                rope(cnt["hn"] - 1, cm("pC", 96, 96), A(8 + h % 2), 96)
                pe.wait_ge(s_kraw, h + 1)
                reduce_job(("hn", cnt["hn"]), cm("o96", 96, 96), [A(22)], 96)
                cnt["hn"] += 1
                yield
                yield
                rope(cnt["hn"] - 1, cm("pC", 96, 96), A(10 + h % 2), 96)
                if h % 2 == 0:
                    p = h // 2
                    src = wckv.rearrange("k (h c) -> k h c", c=128)[:, 2 * p:2 * p + 2, 64:128]
                    gemm(("vc", p), src, rhs=lambda k: A(28), nk=1)
                yield
                if h % 2 == 0:
                    pe.wait_ge(freed[bank(("vc", p))], turn(("vc", p)))
                    transposes(("vct", p), A(27))
                yield
                yield

            def prep_d(h):
                xgemm(("qd", h), cols(wio, OQD + h * P))
                yield
                hn(("qd", h), cm("blk64"))
                xgemm(("kd", h), cols(wio, OKD + h * P))
                yield
                yield
                rope(cnt["hn"] - 1, cm("pD"), A(8 + h % 2))
                hn(("kd", h), cm("blk64"))
                yield
                yield
                rope(cnt["hn"] - 1, cm("pD"), A(10 + h % 2))
                xgemm(("vd", h), cols(wio, OVD + h * P))
                yield
                pe.wait_ge(freed[bank(("vd", h))], turn(("vd", h)))
                transposes(("vdt", h), A(27))
                yield
                xgemm(("gd", h), cols(wio, OG + 512 + h * P))
                yield

            def attend(kind, units, q, k, v, dk, ready, o0, dv):
                nu = len(units)
                base = cnt["unit"]
                nm = 2 if kind == "D" else 1
                for s in range(nu + LAG + 1 + (3 if kind == "D" else 0)):
                    if s < nu:
                        un = units[s]
                        if un[2] == 0:
                            ready(un[1])
                        for m in range(nm):
                            pt, n = opn(("S", base + s, m))
                            pe.wait_ge(freed[n % 4], n // 4)
                            if kind == "A":
                                for rr in range(2):
                                    r = 2 * un[2] + rr
                                    r0 = min(max(r - 4, 0), 8)
                                    mm = pe.matmul(pt[:, rr * 512:rr * 512 + 512], QBD[:, r, :],
                                                   k(un)[:, r0 * 64:r0 * 64 + 512], start=True, stop=True)
                            else:
                                for h in range(2):
                                    mm = pe.matmul(pt[:, h * 512:h * 512 + 512],
                                                   q(un)[0:dk, un[2] * P:un[2] * P + P],
                                                   k(un, m)[0:dk, h * 512:h * 512 + 512], start=True, stop=True)
                            mm.then_inc(filled[n % 4], 1)
                    if LAG <= s < nu + LAG:
                        b = base + s - LAG
                        pe.wait_ge(s_probs, b + 1)
                        pt, n = opn(("T", b))
                        pe.wait_ge(freed[n % 4], n // 4)
                        pr = A(16 + (b % 2) * nm)
                        for c in range(NT):
                            mm = pe.transpose(pt[:, c * P:c * P + P], pr[:, c * P:c * P + P], IDENT)
                        mm.then_inc(filled[n % 4], 1)
                    if LAG + 1 <= s < nu + LAG + 1:
                        b = base + s - LAG - 1
                        un = units[s - LAG - 1]
                        pe.wait_ge(freed[bank(("T", b))], turn(("T", b)))
                        pt, n = opn(("O", b))
                        pe.wait_ge(freed[n % 4], n // 4)
                        pT = A(20 + b % 2)
                        if kind == "A":
                            for rr in range(2):
                                r = 2 * un[2] + rr
                                r0 = min(max(r - 4, 0), 8)
                                vt = (A(12 + un[1] % 2) if r0 % 2 == 0 else A(18 + un[1] % 2))
                                for c in range(4):
                                    x0 = (r0 // 2 + c) * P
                                    y0 = (rr * 4 + c) * P
                                    mm = pe.matmul(pt[:, rr * P:rr * P + P], vt[:, x0:x0 + P],
                                                   pT[:, y0:y0 + P], start=c == 0, stop=c == 3)
                        else:
                            oo = o0(un)
                            for c in range(NT):
                                mm = pe.matmul(pt[oo:oo + dv, 0:P], v(un, c), pT[:, c * P:c * P + P],
                                               start=c == 0, stop=c == NT - 1)
                        mm.then_inc(filled[n % 4], 1)
                    yield
                cnt["unit"] += nu

            def att_a():
                def ready(p):
                    pe.wait_ge(s_qbd, p + 1)
                    pe.wait_ge(s_vs_in, 32 * (p + 1))
                return attend("A", [("A", p, u) for p in range(4) for u in range(8)], None,
                              lambda un: A(10 + un[1] % 2), None, None, ready, None, P)

            def att_b():
                def ready(h):
                    pe.wait_ge(s_rope_tmp, 2 + h // 2 + 1)
                    pe.wait_ge(s_kz, 2)
                return attend("B", [("B", h, u) for h in range(8) for u in range(8)],
                              lambda un: A(8 + un[1] // 2 % 2), lambda un, m: A([10, 18][un[1] % 2] + un[1] // 4),
                              lambda un, c: A(12)[:, c * P + un[1] // 4 * 64:c * P + un[1] // 4 * 64 + 64],
                              P, ready, lambda un: (un[1] % 2) * 64, 64)

            def att_c():
                def ready(h):
                    pe.wait_ge(s_rope_tmp, 6 + 2 * h + 2)
                    pe.wait_ge(freed[bank(("vct", h // 2))], turn(("vct", h // 2)))
                return attend("C", [("C", h, u) for h in range(8) for u in range(8)],
                              lambda un: A(8 + un[1] % 2), lambda un, m: A(10 + un[1] % 2),
                              lambda un, c: A(12 + un[1] // 2 % 2)[:, c * P + un[1] % 2 * 64:c * P + un[1] % 2 * 64 + 64],
                              96, ready, lambda un: (un[1] % 2) * 64, 64)

            def att_d():
                def ready(h):
                    pe.wait_ge(s_kz, 2 + h + 1)
                    pe.wait_ge(freed[bank(("vdt", h))], turn(("vdt", h)))
                steps = attend("D", [("D", h, u) for h in range(4) for u in range(8)], lambda un: A(8 + un[1] % 2),
                               lambda un, m: (A(10 + un[1] % 2), (A(24), MSKF)[un[1] % 2])[m],
                               lambda un, c: A(12 + un[1] % 2)[:, c * P:c * P + P], P, ready, lambda un: 0, 128)
                for s, _ in enumerate(steps):
                    yield
                    if s >= 8 and s % 8 == POST:
                        h = s // 8 - 1
                        pe.wait_ge(s_osq, h + 1)
                        reduce_job(("odn", h), cm("o128"), [A(22)])

            norm(3)
            weave(prep_a(0), ())
            weave(att_a(), chain(8, prep_a(1), prep_a(2), prep_a(3)))
            weave(prep_bkv(), ())
            weave(prep_b(0), ())
            weave(att_b(), chain(16, prep_b(1), prep_b(2), prep_b(3)))
            proj("wout_e", woe, lambda k: A(k), [(0, 8)],
                 lambda k: pe.wait_ge(s_od_done, 32 + max(0, 16 * (k - 3))))
            norm(4)
            pe.wait_ge(s_lam_e, 1)
            pt, n = opn(("lam",))
            pe.wait_ge(freed[n % 4], n // 4)
            mm = pe.matmul(pt[:, 0:2], cm("one", 64), SM[0:64, 30:32], start=True, stop=True)
            mm.then_inc(filled[n % 4], 1)
            weave(prep_c0(), ())
            weave(prep_c(0), ())
            weave(att_c(), chain(8, *[prep_c(h) for h in range(1, 8)]))
            weave(prep_d(0), ())
            weave(att_d(), chain(8, *[prep_d(h) for h in range(1, 4)]))
            proj("wout_o", woo, lambda k: A(k), [(0, 8)],
                 lambda k: pe.wait_ge(s_od_done, 32 + 64 + 64 + max(0, k - 3)))
            for k in range(4):
                n = J["wout_o"] + 4 + k
                pe.wait_ge(freed[n % 4], n // 4 + 1)
            for t in range(NT):
                pt, n = opn(("out", t))
                pe.wait_ge(freed[n % 4], n // 4)
                for f in range(KD):
                    mm = pe.transpose(pt[:, f * P:f * P + P], H[:, f, t * P:t * P + P], IDENT)
                mm.then_inc(filled[n % 4], 1)

        @block.sync
        def _(sp):
            sp.dma_start(CST[:, :], a["cst"]).then_inc(s_cst_in, 16)
            sp.dma_start(PAR[:, :], a["par"]).then_inc(s_cst_in, 16)
            sp.dma_start(MSK[:, :, :].rearrange("p a b -> p (a b)"), a["msk"]).then_inc(s_cst_in, 16)
            for t in range(NT):
                sp.dma_start(AR[:, t, :], a["x"][0, t * P:t * P + P, :]).then_inc(s_cst_in, 16)
            users = []

            def load(w, src, m, kp, nk, dup):
                dst = WR[:, w % 4]
                if len(src.shape) == 2:
                    dst = dst[0:kp, 0, 0:m]
                elif src.shape[1] == 2 and src.shape[2] == 64:
                    dst = dst[:, 0, :].rearrange("p (h c) -> p h c", h=2)
                elif dup:
                    dst = dst.rearrange("p k (two c) -> p k two c", two=2)[:, 0:nk, 0, :]
                    sp.dma_start(dst, src).then_inc(s_half_in, 16)
                    dst = WR[:, w % 4].rearrange("p k (two c) -> p k two c", two=2)[:, 0:nk, 1, :]
                    sp.wait_ge(s_half_in, 16 * (dups[0] + 1))
                    dups[0] += 1
                else:
                    dst = dst[:, 0:nk, 0:m]
                sp.dma_start(dst, src).then_inc(w_in[w % 4], 16)

            dups = [0]
            w = 0
            for e in loads:
                if e[0] == "run":
                    _, iters, nj, body = e
                    nb = len(body)

                    def issue(i, kk, prev):
                        src, _, nk = body[kk]
                        wm, c0, ii, step, k0 = src(i)
                        if isinstance(ii, int):
                            col = slice(c0 + ii * step * P, c0 + ii * step * P + P)
                        else:
                            col = bass.ds(sp.snap(ii * (step * P) + c0 if c0 else ii * (step * P // 2) * 2), P)
                        ap = wm[k0 * P:(k0 + nk) * P, col].rearrange("(k p) c -> p k c", p=P)
                        n, di = prev
                        sp.wait_ge(filled[n % 4], di + (n // 4 + 1))
                        sp.dma_start(WR[:, (w + kk) % 4, 0:nk, :], ap).then_inc(w_in[(w + kk) % 4], 16)

                    for kk in range(nb):
                        n = users[w + kk - 4] if kk < 4 else body[kk - 4][1]
                        issue(0, kk, (n, 0))
                    with sp.Fori(1, iters) as i:
                        for kk in range(nb):
                            if kk >= 4:
                                issue(i, kk, (body[kk - 4][1], i * (nj // 4)))
                            else:
                                issue(i, kk, (body[kk - 4 + nb][1], (i - 1) * (nj // 4)))
                    for i in range(iters):
                        users += [n + i * nj for _, n, _ in body]
                    w += nb * iters
                else:
                    src, n, m, kp, nk, dup = e
                    if w >= 4:
                        u = users[w - 4]
                        sp.wait_ge(filled[u % 4], u // 4 + 1)
                    load(w, src, m, kp, nk, dup)
                    users.append(n)
                    w += 1

        @block.scalar
        def _(act):
            done = {}

            def tick(sem):
                done[sem.name] = done.get(sem.name, 0) + 1
                return done[sem.name]

            reloads = [1]

            def square(i, k):
                if k >= 3:
                    act.wait_ge(s_sumsq, i * (KD - 1) + k - 2)
                act.activation(A(26 + k % 2) if k else A(28), H[:, k, :], ACT.Square).then_inc(s_nsq, 1)
                act.wait_ge(s_nsq, tick(s_nsq))
                if i != 2:
                    act.dma_start(a["spill"][k], H[:, k, :]).then_inc(s_spilled, 16)

            def rms(i):
                act.wait_ge(filled[bank(("norm", i))], turn(("norm", i)))
                act.activation(A(25), PS[bank(("norm", i))][:, :], ACT.Sqrt, bias=epsc)\
                    .then_inc(freed[bank(("norm", i))], 1)
                act.wait_ge(freed[bank(("norm", i))], turn(("norm", i)))
                if i != 2:
                    for k in range(KD):
                        act.wait_ge(s_normed, i * KD + k + 1)
                        act.activation(XH[:, k, :], A(26 + k % 3), ACT.Copy).then_inc(s_xhi, 1)
                        act.wait_ge(s_xhi, tick(s_xhi))

            def reload():
                act.wait_ge(s_spilled, 16 * KD * reloads[0])
                for k in range(KD):
                    act.dma_start(H[:, k, :], a["spill"][k]).then_inc(h_in[k], 16)
                reloads[0] += 1

            def norm_after(name, i):
                for k in range(KD):
                    n = J[name] + k
                    act.wait_ge(freed[n % 4], n // 4 + 1)
                    square(i, k)
                rms(i)

            act.wait_ge(s_cst_in, 16 * 11)
            for k in range(KD):
                act.wait_ge(filled[bank(("x", k))], turn(("x", k)))
                act.activation(H[:, k, :], PS[bank(("x", k))][:, :], ACT.Copy)\
                    .then_inc(freed[bank(("x", k))], 1)
                act.wait_ge(freed[bank(("x", k))], turn(("x", k)))
                square(0, k)
            rms(0)
            act.activation(SM[0:8, 0:1], par("alog", 0, 8), ACT.Exp).then_inc(s_nega, 1)
            act.wait_ge(s_nega, tick(s_nega))
            def ssd_silu(k):
                act.wait_ge(s_conv, k + 1)
                act.activation(A(8 + k), A(8 + k), ACT.Silu).then_inc(s_ssd_silu, 1)
                act.wait_ge(s_ssd_silu, tick(s_ssd_silu))
            for k in range(6):
                if k >= 2:
                    act.wait_ge(s_conv, k - 1)
                if k == 0:
                    act.wait_ge(s_xlo[0], 1 * KD // 2)
                    act.wait_ge(s_xlo[1], 1 * KD // 2)
                act.wait_ge(filled[bank(("sx", k))], turn(("sx", k)))
                act.activation(A(25 + k % 2), PS[bank(("sx", k))][:, :], ACT.Copy)\
                    .then_inc(freed[bank(("sx", k))], 1)
                act.wait_ge(freed[bank(("sx", k))], turn(("sx", k)))
                if k >= 1:
                    ssd_silu(k - 1)
            act.wait_ge(filled[bank(("dt",))], turn(("dt",)))
            act.activation(A(0)[0:8, :], PS[bank(("dt",))][0:8, :], ACT.Identity, bias=par("dtb", 0, 8))\
                .then_inc(freed[bank(("dt",))], 1)
            act.wait_ge(freed[bank(("dt",))], turn(("dt",)))
            act.activation(A(1)[0:8, :], A(0)[0:8, :], ACT.Abs).then_inc(s_act_step, 1)
            act.wait_ge(s_act_step, tick(s_act_step))
            act.activation(A(1)[0:8, :], A(1)[0:8, :], ACT.Exp, scale=-1.0).then_inc(s_act_step, 1)
            act.wait_ge(s_act_step, tick(s_act_step))
            act.activation(A(1)[0:8, :], A(1)[0:8, :], ACT.Ln, bias=1.0).then_inc(s_dt_ln, 1)
            act.wait_ge(s_dt_ln, tick(s_dt_ln))
            ssd_silu(5)
            for k in range(4):
                act.wait_ge(filled[bank(("z", k))], turn(("z", k)))
                act.activation(A(4 + k), PS[bank(("z", k))][:, :], ACT.Silu)\
                    .then_inc(freed[bank(("z", k))], 1)
                act.wait_ge(freed[bank(("z", k))], turn(("z", k)))
            act.wait_ge(s_dec_in, 1)
            act.activation(A(27)[:, 256:384], A(27)[:, 256:384], ACT.Exp).then_inc(s_dec_ready, 1)
            act.wait_ge(s_dec_ready, tick(s_dec_ready))
            act.wait_ge(filled[bank(("Bt",))], turn(("Bt",)))
            act.activation(A(14), PS[bank(("Bt",))][:, :], ACT.Copy)\
                .then_inc(freed[bank(("Bt",))], 1)
            act.wait_ge(freed[bank(("Bt",))], turn(("Bt",)))
            for g in range(2):
                act.wait_ge(filled[bank(("CB", g))], turn(("CB", g)))
                act.activation(A(15 + g), PS[bank(("CB", g))][:, :], ACT.Copy)\
                    .then_inc(freed[bank(("CB", g))], 1)
                act.wait_ge(freed[bank(("CB", g))], turn(("CB", g)))

            def ssd_head(h):
                if h:
                    act.wait_ge(s_mc, h)
                act.wait_ge(filled[bank(("seg", h))], turn(("seg", h)))
                act.activation(A(26), PS[bank(("seg", h))][:, :], ACT.Exp).then_inc(s_ea, 1)
                act.wait_ge(s_ea, tick(s_ea))
                act.wait_ge(s_segm, h + 1)
                act.activation(A(25), A(25), ACT.Exp).then_inc(s_lmat, 1)
                act.wait_ge(s_lmat, tick(s_lmat))
            for fz in range(4):
                ssd_head(2 * fz)
                ssd_head(2 * fz + 1)
                act.wait_ge(s_yz, fz + 1)
                if fz == 2:
                    act.wait_ge(s_ys, 2)
                act.activation(A(12 + 2 * (fz % 2)), A(8 + fz), ACT.Square).then_inc(s_ysq, 1)
                act.wait_ge(s_ysq, tick(s_ysq))
                if fz % 2:
                    g = fz // 2
                    act.wait_ge(filled[bank(("yn", g))], turn(("yn", g)))
                    act.activation(A(28), PS[bank(("yn", g))][:, :], ACT.Sqrt, bias=epsc)\
                        .then_inc(freed[bank(("yn", g))], 1)
                    act.wait_ge(freed[bank(("yn", g))], turn(("yn", g)))
            act.activation(SM[:, 4:8], PAR[:, PC["lam"]:PC["lam"] + 4], ACT.Abs).then_inc(s_act_step, 1)
            act.wait_ge(s_act_step, tick(s_act_step))
            act.activation(SM[:, 4:8], SM[:, 4:8], ACT.Exp, scale=-1.0).then_inc(s_lsp_in, 1)
            act.wait_ge(s_lsp_in, tick(s_lsp_in))
            def lru_x(k):
                if k >= 2:
                    act.wait_ge(s_conv, 6 + k - 1)
                act.wait_ge(filled[bank(("lx", k))], turn(("lx", k)))
                act.activation(A(LX_RAW[k % 2]), PS[bank(("lx", k))][:, :], ACT.Copy)\
                    .then_inc(freed[bank(("lx", k))], 1)
                act.wait_ge(freed[bank(("lx", k))], turn(("lx", k)))

            def lru_gate(k):
                if k >= 2:
                    act.wait_ge(s_ys, 12 + k - 1)
                act.wait_ge(filled[bank(("lg", k))], turn(("lg", k)))
                act.activation(A(LX_GATE[k % 2]), PS[bank(("lg", k))][:, :], ACT.Gelu_apprx_tanh)\
                    .then_inc(freed[bank(("lg", k))], 1)
                act.wait_ge(freed[bank(("lg", k))], turn(("lg", k)))

            def block_diagonal():
                act.wait_ge(s_bd_zero, 1)
                bd = A(20).rearrange("p (i f c) -> p i f c", i=2, c=P)
                for i, w in enumerate((a["lru_wa"][0], a["lru_wx"][0])):
                    wv = w.rearrange("(f two) d e -> two d f e", two=2)
                    for j in range(2):
                        act.dma_start(bd[j * 64:j * 64 + 64, i, :, j * 64:j * 64 + 64], wv[j]).then_inc(s_bd_in, 16)

            def gla_q(u):
                act.wait_ge(filled[bank(("q", u))], turn(("q", u)))
                act.activation(A(16), PS[bank(("q", u))][:, :], ACT.Silu if u < 4 else ACT.Copy,
                               scale=1.0 if u < 4 else 0.125).then_inc(freed[bank(("q", u))], 1)
                act.wait_ge(freed[bank(("q", u))], turn(("q", u)))

            def gla_k(u):
                act.wait_ge(filled[bank(("k", u))], turn(("k", u)))
                t = PS[bank(("k", u))]
                if u < 4:
                    act.activation(A(17), t[:, :], ACT.Sigmoid, scale=-1.0).then_inc(s_act_step, 1)
                    act.wait_ge(s_act_step, tick(s_act_step))
                    act.activation(A(18), t[:, :], ACT.Copy)\
                        .then_inc(freed[bank(("k", u))], 1)
                else:
                    act.activation(A(17), t[:, :], ACT.Copy)\
                        .then_inc(freed[bank(("k", u))], 1)
                act.wait_ge(freed[bank(("k", u))], turn(("k", u)))

            act.wait_ge(s_ys, 4)
            gla_q(0)
            gla_k(0)
            for u in range(6):
                nh = 1 if u < 4 else 2
                if u == 4:
                    act.wait_ge(filled[bank(("glr",))], turn(("glr",)))
                    act.activation(A(11)[0:16, :], PS[bank(("glr",))][0:16, :], ACT.Copy)\
                        .then_inc(freed[bank(("glr",))], 1)
                    act.wait_ge(freed[bank(("glr",))], turn(("glr",)))
                if u >= 4:
                    act.wait_ge(filled[bank(("gz", u))], turn(("gz", u)))
                    act.activation(A(18), PS[bank(("gz", u))][:, :], ACT.Identity, bias=par("gb", u - 4))\
                        .then_inc(freed[bank(("gz", u))], 1)
                    act.wait_ge(freed[bank(("gz", u))], turn(("gz", u)))
                act.activation(A(19), A(18), ACT.Abs).then_inc(s_act_step, 1)
                act.wait_ge(s_act_step, tick(s_act_step))
                act.activation(A(19), A(19), ACT.Exp, scale=-1.0).then_inc(s_act_step, 1)
                act.wait_ge(s_act_step, tick(s_act_step))
                act.activation(A(19), A(19), ACT.Ln, bias=1.0).then_inc(s_lnr, 1)
                act.wait_ge(s_lnr, tick(s_lnr))
                for l in range(NLEV):
                    act.wait_ge(s_expo, u * NLEV + l + 1)
                    act.activation(A(XLEV[l % 3]), A(XLEV[l % 3]), ACT.Exp).then_inc(s_expd, 1)
                    act.wait_ge(s_expd, tick(s_expd))
                    for kind, hh in FILL[nh].get(l - 2, ()):
                        name = (kind, u, hh)
                        act.wait_ge(s_ys, 4 + u if u < 4 else 8 + 2 * (u - 4))
                        act.wait_ge(filled[bank(name)], turn(name))
                        dst = {"g": [A(26), A(14)], "v": [A(24), A(24)], "vt": [A(25), A(13)]}[kind][hh]
                        act.activation(dst, PS[bank(name)][:, :], ACT.Silu if kind == "g" else ACT.Copy)\
                            .then_inc(freed[bank(name)], 1)
                        act.wait_ge(freed[bank(name)], turn(name))
                act.wait_ge(s_qdec, u + 1)
                act.activation(A(15), A(15), ACT.Exp).then_inc(s_dec_exp, 1)
                act.wait_ge(s_dec_exp, tick(s_dec_exp))
                act.activation(A(18), A(20), ACT.Exp).then_inc(s_dec_exp, 1)
                act.wait_ge(s_dec_exp, tick(s_dec_exp))
                act.wait_ge(filled[bank(("kdt", u))], turn(("kdt", u)))
                act.activation(A(27), PS[bank(("kdt", u))][:, :], ACT.Copy)\
                    .then_inc(freed[bank(("kdt", u))], 1)
                act.wait_ge(freed[bank(("kdt", u))], turn(("kdt", u)))
                if u == 4:
                    gla_k(u + 1)
                elif u == 5:
                    lru_x(0)
                    block_diagonal()
                for hh in range(nh):
                    if hh:
                        act.wait_ge(s_ys, 8 + 2 * (u - 4) + 1)
                    act.wait_ge(filled[bank(("o", u, hh))], turn(("o", u, hh)))
                    t = PS[bank(("o", u, hh))]
                    act.activation(A(24), t[:, :], ACT.Copy).then_inc(s_act_step, 1)
                    act.wait_ge(s_act_step, tick(s_act_step))
                    act.activation(A(21), t[:, :], ACT.Square)\
                        .then_inc(freed[bank(("o", u, hh))], 1)
                    act.wait_ge(freed[bank(("o", u, hh))], turn(("o", u, hh)))
                    if u < 4 or u == 4 and hh:
                        gla_q(u + 1)
                    elif hh:
                        lru_gate(0)
                    act.wait_ge(filled[bank(("on", u, hh))], turn(("on", u, hh)))
                    act.activation(A(22), PS[bank(("on", u, hh))][:, :], ACT.Sqrt, bias=epsc)\
                        .then_inc(freed[bank(("on", u, hh))], 1)
                    act.wait_ge(freed[bank(("on", u, hh))], turn(("on", u, hh)))
                    if u < 4:
                        gla_k(u + 1)
            act.wait_ge(s_ys, 12)
            for k in range(4):
                if k < 3:
                    lru_x(k + 1)
                act.wait_ge(s_ys, 12 + k)
                act.wait_ge(filled[bank(("lr", k))], turn(("lr", k)))
                act.activation(A(18), PS[bank(("lr", k))][:, :], ACT.Sigmoid, bias=par("ba", k))\
                    .then_inc(freed[bank(("lr", k))], 1)
                act.wait_ge(freed[bank(("lr", k))], turn(("lr", k)))
                act.wait_ge(filled[bank(("li", k))], turn(("li", k)))
                act.activation(A(19), PS[bank(("li", k))][:, :], ACT.Sigmoid, bias=par("bx", k))\
                    .then_inc(freed[bank(("li", k))], 1)
                act.wait_ge(freed[bank(("li", k))], turn(("li", k)))
                act.wait_ge(s_lamv, 1)
                act.activation(A(21), A(18), ACT.Tanh, scale=SM[:, 8 + k:9 + k]).then_inc(s_lru_q, 1)
                act.wait_ge(s_lru_q, tick(s_lru_q))
                act.activation(A(18), A(18), ACT.Exp, scale=SM[:, 12 + k:13 + k]).then_inc(s_lru_q, 1)
                act.wait_ge(s_lru_q, tick(s_lru_q))
                act.wait_ge(s_lru_b, k + 1)
                act.activation(A(21), A(21), ACT.Sqrt, scale=2.0).then_inc(s_lru_q, 1)
                act.wait_ge(s_lru_q, tick(s_lru_q))
                if k < 3:
                    lru_gate(k + 1)

            n0 = J["merge"]

            def merge(i):
                for b in range(4):
                    nm, nb = n0 + 2 * b, n0 + 2 * b + 1
                    if not isinstance(i, int) or i > 0 or b >= 2:
                        np_ = nb - 4
                        act.wait_ge(freed[np_ % 4], i * 2 + (np_ // 4 + 1))
                    act.wait_ge(filled[nm % 4], i * 2 + (nm // 4 + 1))
                    act.activation(A(24 + b % 2), PS[nm % 4][:, :], ACT.Sigmoid).then_inc(freed[nm % 4], 1)
            act.wait_ge(s_ys, 16)
            merge(0)
            with act.Fori(1, KD) as i:
                merge(i)
            n = n0 + 8 * KD - 2
            act.wait_ge(filled[n % 4], n // 4 + 1)
            reload()
            norm_after("wout", 1)
            n1 = J["ffn_in"]
            act.wait_ge(s_xlo[0], 2 * KD // 2)
            act.wait_ge(s_xlo[1], 2 * KD // 2)

            def ffn(i):
                for j in range(2):
                    ng, nu = n1 + 2 * j, n1 + 2 * j + 1
                    if not isinstance(i, int):
                        act.wait_ge(freed[nu % 4], i + nu // 4)
                    act.wait_ge(filled[ng % 4], i + (ng // 4 + 1))
                    act.activation(A(24 + j), PS[ng % 4][:, :], ACT.Silu).then_inc(freed[ng % 4], 1)
            ffn(0)
            with act.Fori(1, NF // 2) as i:
                ffn(i)
            n = n1 + 2 * NF - 1
            act.wait_ge(filled[n % 4], n // 4 + 1)
            reload()
            norm_after("ffn_out", 2)
            for k in range(KD):
                act.wait_ge(s_normed, 2 * KD + k + 1)
                square(3, k)
            rms(3)

            act.wait_ge(s_xlo[0], 3 * KD // 2)
            act.wait_ge(s_xlo[1], 3 * KD // 2)
            cnt = {"hn": 0, "unit": 0, "s": 0, "vs": 0}

            def raw(name, dst, sq, m=P):
                act.wait_ge(filled[bank(name)], turn(name))
                t = PS[bank(name)]
                act.activation(dst[0:m, :], t[0:m, :], ACT.Copy).then_inc(s_act_step, 1)
                act.wait_ge(s_act_step, tick(s_act_step))
                act.activation(sq[0:m, :], t[0:m, :], ACT.Square)\
                    .then_inc(freed[bank(name)], 1)
                act.wait_ge(freed[bank(name)], turn(name))

            def root(m=P):
                i = cnt["hn"]
                if i:
                    act.wait_ge(s_hn_done, i)
                act.wait_ge(filled[bank(("hn", i))], turn(("hn", i)))
                act.activation(A(23)[0:m, :], PS[bank(("hn", i))][0:m, :], ACT.Sqrt, bias=epsc[0:m])\
                    .then_inc(freed[bank(("hn", i))], 1)
                act.wait_ge(freed[bank(("hn", i))], turn(("hn", i)))
                cnt["hn"] += 1

            def to_sbuf(name):
                act.wait_ge(filled[bank(name)], turn(name))
                act.activation(A(27), PS[bank(name)][:, :], ACT.Copy).then_inc(freed[bank(name)], 1)
                act.wait_ge(freed[bank(name)], turn(name))

            def to_tokens(name, dst):
                act.wait_ge(filled[bank(name)], turn(name))
                act.activation(dst, PS[bank(name)][:, :], ACT.Copy).then_inc(freed[bank(name)], 1)
                act.wait_ge(freed[bank(name)], turn(name))

            def prep_a(p):
                if p >= 2:
                    act.wait_ge(s_negmax, 8 * (p - 1))
                act.dma_start(A(25 + p % 2)[:, 0:960], a["rpb"][p]).then_inc(s_bias_in, 16)
                raw(("qa", p), A(8 + p % 2), A(22))
                yield
                root()
                raw(("ka", p), A(10 + p % 2), A(22))
                yield
                to_sbuf(("va", p))
                yield
                root()
                to_tokens(("vat", p), A(12 + p % 2))
                v, vs = tt(A(12 + p % 2)), tt(A(18 + p % 2))
                act.dma_start(vs[0:64, 0:7, :], v[64:128, 0:7, :]).then_inc(s_vs_in, 16)
                act.dma_start(vs[64:128, 0:7, :], v[0:64, 1:8, :]).then_inc(s_vs_in, 16)
                yield
                if p >= 2:
                    act.wait_ge(s_od_done, 8 * (p - 1))
                act.wait_ge(filled[bank(("ga", p))], turn(("ga", p)))
                act.activation(A(14 + p % 2), PS[bank(("ga", p))][:, :], ACT.Silu)\
                    .then_inc(freed[bank(("ga", p))], 1)
                act.wait_ge(freed[bank(("ga", p))], turn(("ga", p)))
                yield

            def tables(which):
                act.dma_start(A(25), a["rope"][2 * which]).then_inc(s_tab_in, 16)
                act.dma_start(A(26), a["rope"][2 * which + 1]).then_inc(s_tab_in, 16)

            def gate(name, dst):
                act.wait_ge(filled[bank(name)], turn(name))
                act.activation(dst, PS[bank(name)][:, :], ACT.Silu).then_inc(freed[bank(name)], 1)
                act.wait_ge(freed[bank(name)], turn(name))

            def prep_bkv():
                act.wait_ge(s_od_done, 32)
                tables(0)
                for j in range(2):
                    raw(("kb", j), A(10 + j), A(22))
                    root()
                act.wait_ge(s_rope_tmp, 2)
                to_sbuf(("vb",))
                to_tokens(("vbt",), A(12))
                yield

            def prep_b(p):
                raw(("qb", p), A(8 + p % 2), A(22))
                yield
                root()
                if p >= 2:
                    act.wait_ge(s_od_done, 32 + 16 * (p - 1))
                gate(("gb", p), A(14 + p % 2))
                yield
                yield

            def prep_c0():
                tables(1)
                act.wait_ge(s_hn_done, cnt["hn"])
                for j in range(2):
                    act.wait_ge(filled[bank(("cq", j))], turn(("cq", j)))
                    t = PS[bank(("cq", j))]
                    act.activation(A(18 + j), t[:, :], ACT.Copy).then_inc(s_act_step, 1)
                    act.wait_ge(s_act_step, tick(s_act_step))
                    act.activation(A(22 + 2 * j), t[:, :], ACT.Square)\
                        .then_inc(freed[bank(("cq", j))], 1)
                    act.wait_ge(freed[bank(("cq", j))], turn(("cq", j)))
                root()
                raw(("ckv",), A(28), A(22))
                root()
                act.wait_ge(filled[bank(("kpe",))], turn(("kpe",)))
                act.activation(MSKF[64:96, :], PS[bank(("kpe",))][0:32, :], ACT.Copy)\
                    .then_inc(freed[bank(("kpe",))], 1)
                act.wait_ge(freed[bank(("kpe",))], turn(("kpe",)))
                yield

            def prep_c(h):
                p = h // 2
                raw(("qc", h), A(8 + h % 2), A(22), 96)
                yield
                root(96)
                if h % 2 == 0:
                    if p >= 2:
                        act.wait_ge(s_od_done, 96 + 16 * (p - 1))
                    gate(("gc", p), A(14 + p % 2))
                yield
                act.wait_ge(filled[bank(("kc", h))], turn(("kc", h)))
                t = PS[bank(("kc", h))]
                kt = A(10 + h % 2)
                act.activation(kt[0:64, :], t[0:64, :], ACT.Copy).then_inc(s_act_step, 1)
                act.wait_ge(s_act_step, tick(s_act_step))
                act.activation(A(22)[0:64, :], t[0:64, :], ACT.Square)\
                    .then_inc(freed[bank(("kc", h))], 1)
                act.wait_ge(freed[bank(("kc", h))], turn(("kc", h)))
                act.activation(kt[64:96, :], MSKF[64:96, :], ACT.Copy).then_inc(s_act_step, 1)
                act.wait_ge(s_act_step, tick(s_act_step))
                act.activation(A(22)[64:96, :], MSKF[64:96, :], ACT.Square).then_inc(s_kraw, 1)
                act.wait_ge(s_kraw, tick(s_kraw))
                yield
                root(96)
                yield
                yield
                if h % 2 == 0:
                    act.wait_ge(s_rope_tmp, 6 + 2 * h + 2)
                    to_sbuf(("vc", p))
                yield
                if h % 2 == 0:
                    to_tokens(("vct", p), A(12 + p % 2))
                yield
                yield

            def prep_d(h):
                if h == 0:
                    act.wait_ge(s_rope_tmp, 6 + 16)
                    tables(2)
                raw(("qd", h), A(8 + h % 2), A(22))
                yield
                root()
                raw(("kd", h), A(10 + h % 2), A(22))
                yield
                yield
                root()
                yield
                yield
                act.wait_ge(s_rope_tmp, 22 + 2 * h + 2)
                to_sbuf(("vd", h))
                yield
                to_tokens(("vdt", h), A(12 + h % 2))
                yield
                if h >= 2:
                    act.wait_ge(s_od_done, 160 + h - 1)
                gate(("gd", h), A(14 + h % 2))
                yield

            def attend(kind, nu, scale):
                base = cnt["unit"]
                nm = 2 if kind == "D" else 1
                for s in range(nu + LAG + 1 + (3 if kind == "D" else 0)):
                    if s < nu:
                        b = base + s
                        for m in range(nm):
                            c = (b % 2) * 2 + m
                            if kind != "A" and b >= 2:
                                act.wait_ge(filled[bank(("T", b - 2))], turn(("T", b - 2)))
                            pr = A(16 + (b % 2) * nm + m)
                            cnt["s"] += 1
                            act.wait_ge(s_negmax, cnt["s"])
                            if kind == "A":
                                for rr in range(2):
                                    act.activation(pr[:, rr * 512:rr * 512 + 512], pr[:, rr * 512:rr * 512 + 512], ACT.Exp,
                                         bias=SM[:, 20 + 2 * (b % 2) + rr:21 + 2 * (b % 2) + rr],
                                         accum_out=SM[:, 24 + 2 * (b % 2) + rr:25 + 2 * (b % 2) + rr]).then_inc((s_pexp if rr else s_act_step), 1)
                                    act.wait_ge((s_pexp if rr else s_act_step), tick((s_pexp if rr else s_act_step)))
                            else:
                                act.activation(pr, PS[J[("S", b, m)] % 4][:, :], ACT.Exp, scale=scale,
                                     bias=SM[:, 20 + c:21 + c], accum_out=SM[:, 24 + c:25 + c])\
                                    .then_inc(freed[bank(("S", b, m))], 1)
                                act.wait_ge(freed[bank(("S", b, m))], turn(("S", b, m)))
                    if LAG <= s < nu + LAG:
                        b = base + s - LAG
                        if b >= 2:
                            act.wait_ge(filled[bank(("O", b - 2))], turn(("O", b - 2)))
                        act.wait_ge(filled[bank(("T", b))], turn(("T", b)))
                        act.activation(A(20 + b % 2), PS[bank(("T", b))][:, :], ACT.Copy)\
                            .then_inc(freed[bank(("T", b))], 1)
                        act.wait_ge(freed[bank(("T", b))], turn(("T", b)))
                    yield
                cnt["unit"] += nu

            def att_a():
                return attend("A", 32, 1.0)

            def att_b():
                return attend("B", 64, 0.125)

            def att_c():
                return attend("C", 64, 96 ** -0.5)

            def att_d():
                base = cnt["unit"]
                for s, _ in enumerate(attend("D", 32, 0.125)):
                    yield
                    if s >= 8 and s % 8 == POST:
                        h = s // 8 - 1
                        last = ("O", base + 8 * h + 7)
                        act.wait_ge(freed[bank(last)], turn(last))
                        act.wait_ge(s_hn_done, cnt["hn"])
                        act.activation(A(22), A(4 + h), ACT.Square).then_inc(s_osq, 1)
                        act.wait_ge(s_osq, tick(s_osq))
                        act.wait_ge(filled[bank(("odn", h))], turn(("odn", h)))
                        act.activation(A(23), PS[bank(("odn", h))][:, :], ACT.Sqrt, bias=epsc)\
                            .then_inc(freed[bank(("odn", h))], 1)
                        act.wait_ge(freed[bank(("odn", h))], turn(("odn", h)))
                        act.wait_ge(s_od_done, 160 + h + 1)

            weave(prep_a(0), ())
            weave(att_a(), chain(8, prep_a(1), prep_a(2), prep_a(3)))
            weave(prep_bkv(), ())
            weave(prep_b(0), ())
            weave(att_b(), chain(16, prep_b(1), prep_b(2), prep_b(3)))
            act.wait_ge(filled[bank(("gb", 3))], turn(("gb", 3)))
            reload()
            norm_after("wout_e", 4)
            act.wait_ge(s_xlo[0], 4 * KD // 2)
            act.wait_ge(s_xlo[1], 4 * KD // 2)
            act.wait_ge(filled[bank(("lam",))], turn(("lam",)))
            act.activation(SM[:, 32:34], PS[bank(("lam",))][:, 0:2], ACT.Exp)\
                .then_inc(freed[bank(("lam",))], 1)
            act.wait_ge(freed[bank(("lam",))], turn(("lam",)))
            weave(prep_c0(), ())
            weave(prep_c(0), ())
            weave(att_c(), chain(8, *[prep_c(h) for h in range(1, 8)]))
            weave(prep_d(0), ())
            weave(att_d(), chain(8, *[prep_d(h) for h in range(1, 4)]))
            act.wait_ge(filled[bank(("gd", 3))], turn(("gd", 3)))
            reload()
            for t in range(NT):
                act.wait_ge(filled[bank(("out", t))], turn(("out", t)))
                act.activation(A(16 + t), PS[bank(("out", t))][:, :], ACT.Copy)\
                    .then_inc(freed[bank(("out", t))], 1)
                act.wait_ge(freed[bank(("out", t))], turn(("out", t)))
                act.dma_start(a["out"][0, t * P:t * P + P, :], A(16 + t)).then_inc(s_out_in, 16)
            act.wait_ge(s_out_in, 16 * NT)

        @block.vector
        def _(v):
            done = {}

            def tick(sem):
                done[sem.name] = done.get(sem.name, 0) + 1
                return done[sem.name]

            def TT(o, x, y, op):
                return v.tensor_tensor(o, x, y, op)

            def TS(o, x, s1, s2=None, op0=ALU.mult, op1=None):
                if op1 is None:
                    return v.tensor_scalar(o, x, s1, None, op0)
                return v.tensor_scalar(o, x, s1, s2, op0, op1)

            def STT(o, x, s, y, op0, op1):
                return v.scalar_tensor_tensor(out=o, in0=x, scalar=s, in1=y, op0=op0, op1=op1)

            def add_square(i, k):
                v.wait_ge(s_nsq, i * KD + k + 1)
                TT(A(28), A(28), A(26 + k % 2), ALU.add).then_inc(s_sumsq, 1)
                v.wait_ge(s_sumsq, tick(s_sumsq))

            def norm(i, w, then=None):
                v.wait_ge(freed[bank(("norm", i))], turn(("norm", i)))
                v.reciprocal(A(25), A(25)).then_inc(s_dve_step, 1)
                v.wait_ge(s_dve_step, tick(s_dve_step))
                def lower(k):
                    if k == 1:
                        v.wait_ge(s_spilled, 16 * KD * (norm_turn(i) + 1))
                    v.wait_ge(s_xhi, norm_turn(i) * KD + k + 1)
                    TT(XL[:, k, :], A(26 + k % 3), XH[:, k, :], ALU.subtract).then_inc(s_xlo[1], 1)
                    v.wait_ge(s_xlo[1], tick(s_xlo[1]))

                for k in range(KD):
                    if then is None and k >= 3 and k % 2:
                        v.wait_ge(s_xlo[0], norm_turn(i) * (KD // 2) + (k - 3) // 2 + 1)
                    dst = H[:, k, :] if then is not None else A(26 + k % 3)
                    STT(dst, H[:, k, :], par(w, k), A(25), ALU.mult, ALU.mult).then_inc(s_normed, 1)
                    v.wait_ge(s_normed, tick(s_normed))
                    if then is not None and k >= 2:
                        add_square(then, k - 1)
                    if then is None and k % 2 == 0 and k:
                        lower(k - 1)
                if then is not None:
                    add_square(then, KD - 1)
                else:
                    lower(KD - 1)

            def residual_norm(name, i):
                for k in range(KD):
                    n = J[name] + k
                    v.wait_ge(h_in[k], 16 * ["wout", "ffn_out", "wout_e"].index(name) + 16)
                    v.wait_ge(filled[n % 4], n // 4 + 1)
                    TT(H[:, k, :], H[:, k, :], PS[n % 4][:, :], ALU.add).then_inc(freed[n % 4], 1)
                    v.wait_ge(freed[n % 4], n // 4 + 1)
                    if k >= 2:
                        add_square(i, k - 1)
                add_square(i, KD - 1)

            def conv(src, dst, w, nf, fi, b):
                TS(dst, src, par(w, 3 * nf + fi), par(b, fi), ALU.mult, ALU.add).then_inc(s_dve_step, 1)
                v.wait_ge(s_dve_step, tick(s_dve_step))
                for s in (1, 2, 3):
                    STT(dst[:, s:L], src[:, 0:L - s], par(w, (3 - s) * nf + fi), dst[:, s:L], ALU.mult, ALU.add).then_inc((s_conv if s == 3 else s_dve_step), 1)
                    v.wait_ge((s_conv if s == 3 else s_dve_step), tick((s_conv if s == 3 else s_dve_step)))

            for k in range(1, KD):
                add_square(0, k)
            norm(0, "nmix")
            v.wait_ge(s_nega, 1)
            TS(SM[0:8, 1:2], SM[0:8, 0:1], -1.0).then_inc(s_dve_step, 1)
            v.wait_ge(s_dve_step, tick(s_dve_step))
            for k in range(6):
                v.wait_ge(freed[bank(("sx", k))], turn(("sx", k)))
                conv(A(25 + k % 2), A(8 + k), "scw", 6, k, "scb")
            v.wait_ge(s_dt_ln, 1)
            STT(A(0)[0:8, :], A(0)[0:8, :], 0.0, A(1)[0:8, :], ALU.max, ALU.add).then_inc(s_dve_step, 1)
            v.wait_ge(s_dve_step, tick(s_dve_step))
            TS(A(2)[0:8, :], A(0)[0:8, :], SM[0:8, 1:2]).then_inc(s_dt_done, 1)
            v.wait_ge(s_dt_done, tick(s_dt_done))
            T27 = A(27)
            v.wait_ge(filled[bank(("dtt",))], turn(("dtt",)))
            v.tensor_copy(T27[:, 0:128], PS[bank(("dtt",))][:, 0:128])\
                .then_inc(freed[bank(("dtt",))], 1)
            v.wait_ge(freed[bank(("dtt",))], turn(("dtt",)))
            v.wait_ge(filled[bank(("acs",))], turn(("acs",)))
            v.tensor_copy(T27[:, 128:256], PS[bank(("acs",))][:, 0:128])\
                .then_inc(freed[bank(("acs",))], 1)
            v.wait_ge(freed[bank(("acs",))], turn(("acs",)))
            TT(T27[:, 256:320], T27[:, 192:256], T27[:, 128:192], ALU.subtract).then_inc(s_dve_step, 1)
            v.wait_ge(s_dve_step, tick(s_dve_step))
            v.tensor_copy(T27[:, 320:384], T27[:, 192:256]).then_inc(s_dec_in, 1)
            v.wait_ge(s_dec_in, tick(s_dec_in))
            v.wait_ge(s_dec_ready, 1)
            xdt = AR[:, 17:21, :].rearrange("p a (b c) -> p (a b) c", c=512)
            xdd = AR[:, 21:25, :].rearrange("p a (b c) -> p (a b) c", c=512)
            sst = AR[:, 0:4, :].rearrange("p a (b c) -> p (a b) c", c=512)
            th = lambda c0: T27[:, c0:c0 + 64].rearrange("p (t h o) -> p t h o", h=8, o=1)
            for k in range(4):
                v.wait_ge(filled[bank(("xt", k))], turn(("xt", k)))
                t = PS[bank(("xt", k))]
                for hh in range(2):
                    h = 2 * k + hh
                    o = xdt[:, :, h * 64:h * 64 + 64]
                    step = TT(o, tt(t[:, :])[:, :, hh * 64:hh * 64 + 64],
                          th(0)[:, :, h, :].to_broadcast([P, NT, 64]), ALU.mult)
                    if hh:
                        step.then_inc(freed[bank(("xt", k))], 1)
                        v.wait_ge(freed[bank(("xt", k))], turn(("xt", k)))
                    else:
                        step.then_inc(s_dve_step, 1)
                        v.wait_ge(s_dve_step, tick(s_dve_step))
                for hh in range(2):
                    h = 2 * k + hh
                    TT(xdd[:, :, h * 64:h * 64 + 64], xdt[:, :, h * 64:h * 64 + 64],
                          th(256)[:, :, h, :].to_broadcast([P, NT, 64]), ALU.mult).then_inc((s_xdt if hh else s_dve_step), 1)
                    v.wait_ge((s_xdt if hh else s_dve_step), tick((s_xdt if hh else s_dve_step)))
            for j in range(4):
                v.wait_ge(filled[bank(("sU", j))], turn(("sU", j)))
                t = PS[bank(("sU", j))]
                for i in range(2 if j < 3 else 1):
                    c = 2 * j + i
                    last = (i == 1 or j == 3)
                    if c == 0:
                        v.tensor_copy(sst[:, 1, :], t[:, 0:512]).then_inc(s_ssd_state, 1)
                        v.wait_ge(s_ssd_state, tick(s_ssd_state))
                        continue
                    el = th(320)[:, c, :, :].to_broadcast([P, 8, 64])
                    TT(sst[:, c + 1, :].rearrange("p (h c) -> p h c", h=8),
                          sst[:, c, :].rearrange("p (h c) -> p h c", h=8), el, ALU.mult).then_inc(s_dve_step, 1)
                    v.wait_ge(s_dve_step, tick(s_dve_step))
                    TT(sst[:, c + 1, :], sst[:, c + 1, :], t[:, i * 512:i * 512 + 512], ALU.add).then_inc(s_ssd_state, 1)
                    v.wait_ge(s_ssd_state, tick(s_ssd_state))
                v.tensor_copy(SM[:, 2:3], t[:, 0:1])\
                    .then_inc(freed[bank(("sU", j))], 1)
                v.wait_ge(freed[bank(("sU", j))], turn(("sU", j)))
            v.wait_ge(s_ssd_silu, 6)

            def ssd_head(h):
                v.wait_ge(filled[bank(("seg", h))], turn(("seg", h)))
                t = PS[bank(("seg", h))]
                v.wait_ge(s_ea, h + 1)
                TT(tt(A(25)), tt(t[:, :]), th(128)[:, :, h, :].to_broadcast([P, NT, P]), ALU.subtract)\
                    .then_inc(freed[bank(("seg", h))], 1)
                v.wait_ge(freed[bank(("seg", h))], turn(("seg", h)))
                neg = cm("neg").rearrange("p (o i) -> p o i", o=1).to_broadcast([P, NT, P])
                TT(tt(A(25)), tt(A(25)), neg, ALU.add).then_inc(s_segm, 1)
                v.wait_ge(s_segm, tick(s_segm))
                v.wait_ge(s_lmat, h + 1)
                if h >= 2:
                    v.wait_ge(filled[bank(("y", h // 2 - 1))], turn(("y", h // 2 - 1)))
                v.wait_ge(freed[bank(("CB", h // 4))], turn(("CB", h // 4)))
                TT(A(21 + h % 2), A(25), A(15 + h // 4), ALU.mult).then_inc(s_dve_step, 1)
                v.wait_ge(s_dve_step, tick(s_dve_step))
                TT(A(23 + h % 2), A(26), A(13), ALU.mult).then_inc(s_mc, 1)
                v.wait_ge(s_mc, tick(s_mc))

            for k in range(4):
                ssd_head(2 * k)
                ssd_head(2 * k + 1)
                v.wait_ge(filled[bank(("y", k))], turn(("y", k)))
                STT(A(8 + k), A(8 + k), par("sd", k), PS[bank(("y", k))][:, :], ALU.mult, ALU.add)\
                    .then_inc(freed[bank(("y", k))], 1)
                v.wait_ge(freed[bank(("y", k))], turn(("y", k)))
                TT(A(8 + k), A(8 + k), A(4 + k), ALU.mult).then_inc(s_yz, 1)
                v.wait_ge(s_yz, tick(s_yz))
                if k % 2:
                    g = k // 2
                    v.wait_ge(freed[bank(("yn", g))], turn(("yn", g)))
                    v.reciprocal(A(28), A(28)).then_inc(s_dve_step, 1)
                    v.wait_ge(s_dve_step, tick(s_dve_step))
                    for j in (k - 1, k):
                        STT(A(4 + j), A(8 + j), par("snw", j), A(28), ALU.mult, ALU.mult).then_inc(s_ys, 1)
                        v.wait_ge(s_ys, tick(s_ys))

            v.wait_ge(s_lsp_in, 1)
            e, z, z2, acc = SM[:, 4:8], SM[:, 8:12], SM[:, 12:16], SM[:, 16:20]
            TS(z, e, 2.0, None, ALU.add).then_inc(s_dve_step, 1)
            v.wait_ge(s_dve_step, tick(s_dve_step))
            v.reciprocal(z, z).then_inc(s_dve_step, 1)
            v.wait_ge(s_dve_step, tick(s_dve_step))
            TT(z, z, e, ALU.mult).then_inc(s_dve_step, 1)
            v.wait_ge(s_dve_step, tick(s_dve_step))
            TT(z2, z, z, ALU.mult).then_inc(s_dve_step, 1)
            v.wait_ge(s_dve_step, tick(s_dve_step))
            TS(acc, z2, 2.0 / 13, 2.0 / 11, ALU.mult, ALU.add).then_inc(s_dve_step, 1)
            v.wait_ge(s_dve_step, tick(s_dve_step))
            for o in (9, 7, 5, 3, 1):
                TT(acc, acc, z2, ALU.mult).then_inc(s_dve_step, 1)
                v.wait_ge(s_dve_step, tick(s_dve_step))
                TS(acc, acc, 2.0 / o, None, ALU.add).then_inc(s_dve_step, 1)
                v.wait_ge(s_dve_step, tick(s_dve_step))
            TT(acc, acc, z, ALU.mult).then_inc(s_dve_step, 1)
            v.wait_ge(s_dve_step, tick(s_dve_step))
            TS(e, PAR[:, PC["lam"]:PC["lam"] + 4], -1.0, 0.0, ALU.mult, ALU.max).then_inc(s_dve_step, 1)
            v.wait_ge(s_dve_step, tick(s_dve_step))
            TT(acc, acc, e, ALU.add).then_inc(s_dve_step, 1)
            v.wait_ge(s_dve_step, tick(s_dve_step))
            TS(SM[:, 8:12], acc, 8.0).then_inc(s_dve_step, 1)
            v.wait_ge(s_dve_step, tick(s_dve_step))
            TS(SM[:, 12:16], acc, -8.0).then_inc(s_lamv, 1)
            v.wait_ge(s_lamv, tick(s_lamv))
            v.memset(A(23), 0.0).then_inc(s_dve_step, 1)
            v.wait_ge(s_dve_step, tick(s_dve_step))
            for u in range(6):
                nh = 1 if u < 4 else 2
                if u == 4:
                    v.memset(A(12), 0.0).then_inc(s_dve_step, 1)
                    v.wait_ge(s_dve_step, tick(s_dve_step))
                v.wait_ge(s_lnr, u + 1)
                STT(A(18), A(18), 0.0, A(19), ALU.min, ALU.subtract).then_inc(s_dve_step, 1)
                v.wait_ge(s_dve_step, tick(s_dve_step))
                if nh == 2:
                    TS(A(18), A(18), 1.0 / 16.0).then_inc(s_dve_step, 1)
                    v.wait_ge(s_dve_step, tick(s_dve_step))
                for t in range(NT):
                    c = slice(t * P, t * P + P)
                    v.tensor_tensor_scan(A(20)[:, c], CST[:, CONE:CONE + 1].to_broadcast([P, P]), A(18)[:, c],
                                            0.0, ALU.mult, ALU.add).then_inc(s_dve_step, 1)
                    v.wait_ge(s_dve_step, tick(s_dve_step))

                def halves(ap, l):
                    s = 64 >> l
                    return ap.rearrange("p (b h s) -> p b h s", h=2, s=s)

                def expo(l):
                    s = 64 >> l
                    nb = L // (2 * s)
                    x, b = halves(A(XLEV[l % 3]), l), halves(A(20), l)
                    mid = b[:, :, 0, s - 1:s].to_broadcast([P, nb, s])
                    TT(x[:, :, 0, :], mid, b[:, :, 0, :], ALU.subtract).then_inc(s_dve_step, 1)
                    v.wait_ge(s_dve_step, tick(s_dve_step))
                    TT(x[:, :, 1, :], b[:, :, 1, :], mid, ALU.subtract).then_inc(s_expo, 1)
                    v.wait_ge(s_expo, tick(s_expo))

                def pred(l):
                    m = MSK[:, l % (NLEV + 1):l % (NLEV + 1) + 1, :].to_broadcast([P, NT, P])
                    for hh in range(nh):
                        am = [A(23), A(12)][hh]
                        v.wait_ge(filled[bank(("P", u, l, hh))], turn(("P", u, l, hh)))
                        v.copy_predicated(tt(am), m, tt(PS[bank(("P", u, l, hh))][:, :]))\
                            .then_inc(freed[bank(("P", u, l, hh))], 1)
                        v.wait_ge(freed[bank(("P", u, l, hh))], turn(("P", u, l, hh)))

                expo(0)
                v.wait_ge(freed[bank(("q", u))], turn(("q", u)))
                for l in range(NLEV):
                    if l >= 1:
                        pred(l - 2)
                    if l < NLEV - 1:
                        expo(l + 1)
                    v.wait_ge(s_expd, u * NLEV + l + 1)
                    x = halves(A(XLEV[l % 3]), l)
                    TT(x[:, :, 0, :], x[:, :, 0, :], halves(A(17), l)[:, :, 0, :], ALU.mult).then_inc(s_dve_step, 1)
                    v.wait_ge(s_dve_step, tick(s_dve_step))
                    TT(x[:, :, 1, :], x[:, :, 1, :], halves(A(16), l)[:, :, 1, :], ALU.mult).then_inc(s_xlev, 1)
                    v.wait_ge(s_xlev, tick(s_xlev))
                pred(NLEV - 2)
                b = tt(A(20))
                TT(tt(A(15)), b[:, :, P - 1:P].to_broadcast([P, NT, P]), b, ALU.subtract).then_inc(s_qdec, 1)
                v.wait_ge(s_qdec, tick(s_qdec))
                pred(NLEV - 1)
                v.wait_ge(s_dec_exp, 2 * u + 2)
                TT(A(15), A(15), A(17), ALU.mult).then_inc(s_kdec, 1)
                v.wait_ge(s_kdec, tick(s_kdec))
                TT(A(16), A(16), A(18), ALU.mult).then_inc(s_a_done, 1)
                v.wait_ge(s_a_done, tick(s_a_done))
                if u == 5:
                    v.memset(A(20), 0.0).then_inc(s_bd_zero, 1)
                    v.wait_ge(s_bd_zero, tick(s_bd_zero))
                v.wait_ge(filled[bank(("U", u))], turn(("U", u)))
                t = PS[bank(("U", u))]
                s = A(19)
                v.tensor_copy(s[:, P:2 * P], t[:, 0:P]).then_inc(s_dve_step, 1)
                v.wait_ge(s_dve_step, tick(s_dve_step))
                for c in range(1, NT - 1):
                    el = A(18)[:, c * P + P - 1:c * P + P]
                    STT(s[:, (c + 1) * P:(c + 2) * P], s[:, c * P:c * P + P], el, t[:, c * P:c * P + P],
                           ALU.mult, ALU.add).then_inc((s_g_state if c == NT - 2 else s_dve_step), 1)
                    v.wait_ge((s_g_state if c == NT - 2 else s_dve_step), tick((s_g_state if c == NT - 2 else s_dve_step)))
                v.tensor_copy(SM[:, 2:3], t[:, 0:1])\
                    .then_inc(freed[bank(("U", u))], 1)
                v.wait_ge(freed[bank(("U", u))], turn(("U", u)))
                for hh in range(nh):
                    v.wait_ge(freed[bank(("on", u, hh))], turn(("on", u, hh)))
                    v.reciprocal(A(22), A(22)).then_inc(s_dve_step, 1)
                    v.wait_ge(s_dve_step, tick(s_dve_step))
                    STT(A(24), A(24), par("hnw" if u < 4 else "gnw"), A(22), ALU.mult, ALU.mult).then_inc(s_dve_step, 1)
                    v.wait_ge(s_dve_step, tick(s_dve_step))
                    dst = A(u) if u < 4 else A(8 + 2 * (u - 4) + hh)
                    TT(dst, A(24), [A(26), A(14)][hh], ALU.mult).then_inc(s_ys, 1)
                    v.wait_ge(s_ys, tick(s_ys))

            def lru_conv(k):
                v.wait_ge(freed[bank(("lx", k))], turn(("lx", k)))
                conv(A(LX_RAW[k % 2]), A(LXC[k % 2]), "lcw", 4, k, "lcb")
            lru_conv(0)
            for k in range(4):
                if k < 3:
                    lru_conv(k + 1)
                v.wait_ge(s_lru_q, 3 * k + 2)
                TS(A(22), A(21), 1.0, None, ALU.add).then_inc(s_dve_step, 1)
                v.wait_ge(s_dve_step, tick(s_dve_step))
                v.reciprocal(A(22), A(22)).then_inc(s_dve_step, 1)
                v.wait_ge(s_dve_step, tick(s_dve_step))
                TT(A(21), A(21), A(22), ALU.mult).then_inc(s_lru_b, 1)
                v.wait_ge(s_lru_b, tick(s_lru_b))
                TT(A(19), A(19), A(LXC[k % 2]), ALU.mult).then_inc(s_dve_step, 1)
                v.wait_ge(s_dve_step, tick(s_dve_step))
                v.wait_ge(s_lru_q, 3 * k + 3)
                TT(A(21), A(21), A(19), ALU.mult).then_inc(s_dve_step, 1)
                v.wait_ge(s_dve_step, tick(s_dve_step))
                v.tensor_tensor_scan(A(22), A(18), A(21), 0.0, ALU.mult, ALU.add).then_inc(s_dve_step, 1)
                v.wait_ge(s_dve_step, tick(s_dve_step))
                TT(A(12 + k), A(22), A(LX_GATE[k % 2]), ALU.mult).then_inc(s_ys, 1)
                v.wait_ge(s_ys, tick(s_ys))

            n0 = J["merge"]
            with v.Fori(0, KD) as i:
                dst = AR[:, bass.ds(i + 16, 1), :]
                for b in range(4):
                    nm, nb = n0 + 2 * b, n0 + 2 * b + 1
                    v.wait_ge(freed[nm % 4], i * 2 + (nm // 4 + 1))
                    v.wait_ge(filled[nb % 4], i * 2 + (nb // 4 + 1))
                    o = A(26)
                    v.tensor_tensor(dst if b == 0 else o, A(24 + b % 2), PS[nb % 4][:, :], ALU.mult)\
                        .then_inc(freed[nb % 4], 1)
                    v.wait_ge(freed[nb % 4], i * 2 + (nb // 4 + 1))
                    if b:
                        v.tensor_tensor(dst, dst, o, ALU.add).then_inc(s_merge_add, 1)
                        v.wait_ge(s_merge_add, i * 3 + b)

            residual_norm("wout", 1)
            norm(1, "nffn")
            n1 = J["ffn_in"]
            with v.Fori(0, NF // 2) as i:
                for j in range(2):
                    ng, nu = n1 + 2 * j, n1 + 2 * j + 1
                    v.wait_ge(freed[ng % 4], i + (ng // 4 + 1))
                    v.wait_ge(filled[nu % 4], i + (nu // 4 + 1))
                    v.tensor_tensor(AR[:, bass.ds(i * 2 + j, 1), :], A(24 + j), PS[nu % 4][:, :], ALU.mult)\
                        .then_inc(freed[nu % 4], 1)
            residual_norm("ffn_out", 2)
            norm(2, "nf", then=3)
            norm(3, "ne")

            cnt = {"hn": 0, "unit": 0, "rope": 0}
            TT(SM[0:64, 30:31], PAR[0:64, PC["lq1"]:PC["lq1"] + 1], PAR[0:64, PC["lk1"]:PC["lk1"] + 1], ALU.mult).then_inc(s_dve_step, 1)
            v.wait_ge(s_dve_step, tick(s_dve_step))
            TT(SM[0:64, 31:32], PAR[0:64, PC["lq2"]:PC["lq2"] + 1], PAR[0:64, PC["lk2"]:PC["lk2"] + 1], ALU.mult).then_inc(s_lam_e, 1)
            v.wait_ge(s_lam_e, tick(s_lam_e))

            def hn(x, g, m=P):
                v.wait_ge(freed[bank(("hn", cnt["hn"]))], turn(("hn", cnt["hn"])))
                cnt["hn"] += 1
                v.reciprocal(A(23)[0:m, 0:512], A(23)[0:m, 0:512]).then_inc(s_dve_step, 1)
                v.wait_ge(s_dve_step, tick(s_dve_step))
                yield
                v.reciprocal(A(23)[0:m, 512:L], A(23)[0:m, 512:L]).then_inc(s_dve_step, 1)
                v.wait_ge(s_dve_step, tick(s_dve_step))
                STT(x[0:m, :], x[0:m, :], g[0:m], A(23)[0:m, :], ALU.mult, ALU.mult).then_inc(s_hn_done, 1)
                v.wait_ge(s_hn_done, tick(s_hn_done))

            def pad_keys(x, other):
                v.tensor_copy(other[64:128, :], x[64:128, :]).then_inc(s_dve_step, 1)
                v.wait_ge(s_dve_step, tick(s_dve_step))
                v.memset(other[0:64, :], 0.0).then_inc(s_dve_step, 1)
                v.wait_ge(s_dve_step, tick(s_dve_step))
                v.memset(x[64:128, :], 0.0).then_inc(s_kz, 1)
                v.wait_ge(s_kz, tick(s_kz))

            def rope(x, m=P):
                i = cnt["hn"] - 1
                cnt["rope"] += 1
                v.wait_ge(filled[bank(("rope", i))], turn(("rope", i)))
                t = PS[bank(("rope", i))]
                TT(A(27)[0:m, :], t[0:m, :], A(26)[0:m, :], ALU.mult)\
                    .then_inc(freed[bank(("rope", i))], 1)
                v.wait_ge(freed[bank(("rope", i))], turn(("rope", i)))
                TT(x[0:m, :], x[0:m, :], A(25)[0:m, :], ALU.mult).then_inc(s_dve_step, 1)
                v.wait_ge(s_dve_step, tick(s_dve_step))
                TT(x[0:m, :], x[0:m, :], A(27)[0:m, :], ALU.add).then_inc(s_rope_tmp, 1)
                v.wait_ge(s_rope_tmp, tick(s_rope_tmp))

            def prep_a(p):
                v.wait_ge(s_bias_in, 16 * (p + 1))
                b = A(25 + p % 2)[:, 0:960].rearrange("p (r c) -> p r c", c=64)
                m = CST[:, CNB:CNB + 64].rearrange("p (o c) -> p o c", o=1).to_broadcast([P, 15, 64])
                TT(b, b, m, ALU.add).then_inc(s_dve_step, 1)
                v.wait_ge(s_dve_step, tick(s_dve_step))
                yield
                yield from hn(A(8 + p % 2), par("gqa"))
                yield
                yield from hn(A(10 + p % 2), par("gka"))
                yield

            def prep_bkv():
                v.wait_ge(s_tab_in, 32)
                for j in range(2):
                    yield from hn(A(10 + j), par("gkb"))
                    rope(A(10 + j))
                    pad_keys(A(10 + j), A(18 + j))
                yield

            def prep_b(p):
                yield
                yield from hn(A(8 + p % 2), par("gqb"))
                yield
                rope(A(8 + p % 2))
                yield

            def prep_c0():
                v.wait_ge(freed[bank(("hn", cnt["hn"]))], turn(("hn", cnt["hn"])))
                cnt["hn"] += 1
                v.reciprocal(A(23), A(23)).then_inc(s_dve_step, 1)
                v.wait_ge(s_dve_step, tick(s_dve_step))
                STT(A(18), A(18), par("gcq", 0), A(23), ALU.mult, ALU.mult).then_inc(s_dve_step, 1)
                v.wait_ge(s_dve_step, tick(s_dve_step))
                STT(A(19), A(19), par("gcq", 1), A(23), ALU.mult, ALU.mult).then_inc(s_hn_done, 1)
                v.wait_ge(s_hn_done, tick(s_hn_done))
                yield from hn(A(28), par("gckv"))
                v.wait_ge(s_tab_in, 64)
                yield

            def prep_c(h):
                yield
                yield from hn(A(8 + h % 2), par("gqc"), 96)
                yield
                rope(A(8 + h % 2), 96)
                yield from hn(A(10 + h % 2), par("gkc"), 96)
                yield
                rope(A(10 + h % 2), 96)
                yield

            def prep_d(h):
                yield
                if h == 0:
                    v.wait_ge(s_tab_in, 96)
                yield from hn(A(8 + h % 2), par("gqd"))
                yield
                rope(A(8 + h % 2))
                yield from hn(A(10 + h % 2), par("gkd"))
                yield
                rope(A(10 + h % 2))
                pad_keys(A(10 + h % 2), (A(24), MSKF)[h % 2])
                yield

            def attend(kind, nu, scale, odst, gate, nv, o0):
                base = cnt["unit"]
                nm = 2 if kind == "D" else 1
                for s in range(nu + LAG + 1 + (3 if kind == "D" else 0)):
                    if s < nu:
                        b = base + s
                        if kind == "A" and s % 8 == 0:
                            x = A(8 + s // 8 % 2).rearrange("p (r c) -> p r c", c=64)
                            v.tensor_copy(QBD[0:64, :, 0:64], x[0:64]).then_inc(s_dve_step, 1)
                            v.wait_ge(s_dve_step, tick(s_dve_step))
                            v.tensor_copy(QBD[64:128, :, 64:128], x[64:128]).then_inc(s_qbd, 1)
                            v.wait_ge(s_qbd, tick(s_qbd))
                        mx = SM[:, 34:36]
                        c0 = 2 * (b % 2)
                        for m in range(nm):
                            v.wait_ge(filled[bank(("S", b, m))], turn(("S", b, m)))
                            t = PS[bank(("S", b, m))]
                            if kind == "A":
                                if b >= 2:
                                    v.wait_ge(filled[bank(("T", b - 2))], turn(("T", b - 2)))
                                p = (b // 8)
                                for rr in range(2):
                                    r = 2 * (b % 8) + rr
                                    off = min(max(r - 4, 0), 8) - r + 7
                                    step = STT(A(16 + b % 2)[:, rr * 512:rr * 512 + 512], t[:, rr * 512:rr * 512 + 512],
                                           0.125, A(25 + p % 2)[:, off * 64:off * 64 + 512], ALU.mult, ALU.add)
                                    if rr:
                                        step.then_inc(freed[bank(("S", b, 0))], 1)
                                        v.wait_ge(freed[bank(("S", b, 0))], turn(("S", b, 0)))
                                    else:
                                        step.then_inc(s_dve_step, 1)
                                        v.wait_ge(s_dve_step, tick(s_dve_step))
                                v.tensor_reduce(mx, A(16 + b % 2).rearrange("p (r c) -> p r c", r=2), AX.X, ALU.max).then_inc(s_dve_step, 1)
                                v.wait_ge(s_dve_step, tick(s_dve_step))
                                TS(SM[:, 20 + c0:22 + c0], mx, -1.0).then_inc(s_negmax, 1)
                                v.wait_ge(s_negmax, tick(s_negmax))
                            else:
                                v.tensor_reduce(mx[:, 0:1], t[:, :], AX.X, ALU.max).then_inc(s_dve_step, 1)
                                v.wait_ge(s_dve_step, tick(s_dve_step))
                                TS(SM[:, 20 + c0 + m:21 + c0 + m], mx[:, 0:1], -scale).then_inc(s_negmax, 1)
                                v.wait_ge(s_negmax, tick(s_negmax))
                    if LAG + 1 <= s < nu + LAG + 1:
                        u = s - LAG - 1
                        b = base + u
                        v.wait_ge(filled[bank(("O", b))], turn(("O", b)))
                        t = PS[bank(("O", b))]
                        oo, od = o0(u), odst(u)
                        q = slice((u % 8) * P, (u % 8) * P + P)
                        if kind == "D":
                            v.tensor_copy(od[:, q], t[:, 0:P])\
                                .then_inc(freed[bank(("O", b))], 1)
                            v.wait_ge(freed[bank(("O", b))], turn(("O", b)))
                        else:
                            gname, g = gate(u)
                            v.wait_ge(freed[bank(gname)], turn(gname))
                            if kind == "A":
                                for hh in range(2):
                                    e = slice(hh * 64, hh * 64 + 64)
                                    v.tensor_tensor(od[e, q].rearrange("p (r c) -> p r c", r=2),
                                                    t[e, 0:256].rearrange("p (r c) -> p r c", r=2)[:, :, hh * 64:hh * 64 + 64],
                                                    g[e, q].rearrange("p (r c) -> p r c", r=2), ALU.mult)\
                                        .then_inc(s_od_done if hh else s_dve_step, 1)
                                    v.wait_ge(s_od_done if hh else s_dve_step, tick(s_od_done if hh else s_dve_step))
                            else:
                                v.tensor_tensor(od[oo:oo + nv, q], t[oo:oo + nv, 0:P], g[oo:oo + nv, q], ALU.mult)\
                                    .then_inc(s_od_done, 1)
                                v.wait_ge(s_od_done, tick(s_od_done))
                            v.tensor_copy(SM[:, 36:37], t[:, 0:1] if nv == P else SM[:, 34:35])\
                                .then_inc(freed[bank(("O", b))], 1)
                            v.wait_ge(freed[bank(("O", b))], turn(("O", b)))
                    if s < nu:
                        b = base + s
                        if kind == "A":
                            v.wait_ge(s_pexp, b + 1)
                        for m in range(nm):
                            if kind != "A":
                                v.wait_ge(freed[bank(("S", b, m))], turn(("S", b, m)))
                        if b >= 2:
                            v.wait_ge(filled[bank(("T", b - 2))], turn(("T", b - 2)))
                        n2 = 2 if kind in "AD" else 1
                        rc = SM[:, 38:40]
                        pr = A(16 + (b % 2) * nm)
                        v.reciprocal(rc[:, 0:n2], SM[:, 24 + c0:24 + c0 + n2]).then_inc(s_dve_step, 1)
                        v.wait_ge(s_dve_step, tick(s_dve_step))
                        if kind == "A":
                            TS(pr[:, 0:512], pr[:, 0:512], rc[:, 0:1]).then_inc(s_dve_step, 1)
                            v.wait_ge(s_dve_step, tick(s_dve_step))
                            TS(pr[:, 512:L], pr[:, 512:L], rc[:, 1:2]).then_inc(s_probs, 1)
                            v.wait_ge(s_probs, tick(s_probs))
                        elif kind == "D":
                            TT(rc[:, 1:2], rc[:, 1:2], SM[:, 29:30], ALU.mult).then_inc(s_dve_step, 1)
                            v.wait_ge(s_dve_step, tick(s_dve_step))
                            TS(pr, pr, rc[:, 0:1]).then_inc(s_dve_step, 1)
                            v.wait_ge(s_dve_step, tick(s_dve_step))
                            STT(pr, A(17 + (b % 2) * nm), rc[:, 1:2], pr, ALU.mult, ALU.add).then_inc(s_probs, 1)
                            v.wait_ge(s_probs, tick(s_probs))
                        else:
                            TS(pr, pr, rc[:, 0:1]).then_inc(s_probs, 1)
                            v.wait_ge(s_probs, tick(s_probs))
                    yield
                cnt["unit"] += nu

            def att_a():
                return attend("A", 32, 1.0, lambda u: A(u // 8), lambda u: (("ga", u // 8), A(14 + u // 8 % 2)), P,
                              lambda u: 0)

            def att_b():
                return attend("B", 64, 0.125, lambda u: A(4 + u // 16),
                              lambda u: (("gb", u // 16), A(14 + u // 16 % 2)), 64, lambda u: (u // 8 % 2) * 64)

            def att_c():
                return attend("C", 64, 96 ** -0.5, lambda u: A(u // 16),
                              lambda u: (("gc", u // 16), A(14 + u // 16 % 2)), 64, lambda u: (u // 8 % 2) * 64)

            def att_d():
                steps = attend("D", 32, 0.125, lambda u: A(4 + u // 8), None, P, lambda u: 0)
                for s, _ in enumerate(steps):
                    yield
                    if s >= 8 and s % 8 == POST:
                        h = s // 8 - 1
                        v.wait_ge(freed[bank(("odn", h))], turn(("odn", h)))
                        v.reciprocal(A(23), A(23)).then_inc(s_dve_step, 1)
                        v.wait_ge(s_dve_step, tick(s_dve_step))
                        STT(A(4 + h), A(4 + h), SM[:, 28:29], A(23), ALU.mult, ALU.mult).then_inc(s_dve_step, 1)
                        v.wait_ge(s_dve_step, tick(s_dve_step))
                        v.wait_ge(freed[bank(("gd", h))], turn(("gd", h)))
                        TT(A(4 + h), A(4 + h), A(14 + h % 2), ALU.mult).then_inc(s_od_done, 1)
                        v.wait_ge(s_od_done, tick(s_od_done))

            v.memset(AR[:, 4:6, :], 0.0).then_inc(s_dve_step, 1)
            v.wait_ge(s_dve_step, tick(s_dve_step))
            weave(prep_a(0), ())
            weave(att_a(), chain(8, prep_a(1), prep_a(2), prep_a(3)))
            weave(prep_bkv(), ())
            weave(prep_b(0), ())
            weave(att_b(), chain(16, prep_b(1), prep_b(2), prep_b(3)))
            residual_norm("wout_e", 4)
            norm(4, "no")
            v.wait_ge(freed[bank(("lam",))], turn(("lam",)))
            TT(SM[:, 29:30], SM[:, 33:34], SM[:, 32:33], ALU.subtract).then_inc(s_dve_step, 1)
            v.wait_ge(s_dve_step, tick(s_dve_step))
            TS(SM[:, 29:30], SM[:, 29:30], -LAM_INIT, None, ALU.add).then_inc(s_dve_step, 1)
            v.wait_ge(s_dve_step, tick(s_dve_step))
            TS(SM[:, 28:29], par("gsub"), 1.0 - LAM_INIT).then_inc(s_dve_step, 1)
            v.wait_ge(s_dve_step, tick(s_dve_step))
            weave(prep_c0(), ())
            weave(prep_c(0), ())
            weave(att_c(), chain(8, *[prep_c(h) for h in range(1, 8)]))
            weave(prep_d(0), ())
            weave(att_d(), chain(8, *[prep_d(h) for h in range(1, 4)]))
            for k in range(KD):
                n = J["wout_o"] + k
                v.wait_ge(h_in[k], 16 * 4)
                v.wait_ge(filled[n % 4], n // 4 + 1)
                TT(H[:, k, :], H[:, k, :], PS[n % 4][:, :], ALU.add).then_inc(freed[n % 4], 1)
                v.wait_ge(freed[n % 4], n // 4 + 1)

        @block.gpsimd
        def _(pool):
            done = {}

            def tick(sem):
                done[sem.name] = done.get(sem.name, 0) + 1
                return done[sem.name]

            for e in splits:
                if e[0] == "weight":
                    _, w, m = e
                    hi, lo, full = WH[:, w % 4, :, 0:m], WL[:, w % 4, :, 0:m], WR[:, w % 4, :, 0:m]
                    pool.wait_ge(w_in[w % 4], 16 * (w // 4 + 1))
                    pool.tensor_copy(hi, full).then_inc(s_whi, 1)
                    pool.wait_ge(s_whi, tick(s_whi))
                    pool.tensor_tensor(lo, full, hi, ALU.subtract).then_inc(s_wsplit, 1)
                    pool.wait_ge(s_wsplit, tick(s_wsplit))
                elif e[0] == "norm":
                    i = e[1]
                    t = norm_turn(i)
                    pool.wait_ge(s_spilled, 16 * KD * (t + 1))
                    for k in range(0, KD, 2):
                        pool.wait_ge(s_xhi, t * KD + k + 1)
                        pool.tensor_tensor(XL[:, k, :], A(26 + k % 3), XH[:, k, :], ALU.subtract)\
                            .then_inc(s_xlo[0], 1)
                        pool.wait_ge(s_xlo[0], tick(s_xlo[0]))


def rotation(ang):
    return np.cos(ang).astype(np.float32), np.sin(ang).astype(np.float32)


def constants():
    cst = np.zeros((P, NCST), np.float32)

    def put(name, m):
        cst[:m.shape[0], CM[name]:CM[name] + m.shape[1]] = m
    i = np.arange(P)
    put("ident", np.eye(P))
    put("tri", (i[:, None] <= i[None, :]) * 1.0)
    put("neg", np.where(i[:, None] <= i[None, :], 0.0, -1e30))
    put("blk64", (i[:, None] // 64 == i[None, :] // 64) / 64.0)
    put("o1024", np.full((P, P), 1 / 1024.0))
    put("o128", np.full((P, P), 1 / 128.0))
    put("o256", np.full((P, P), 1 / 256.0))
    put("o96", np.full((P, P), 1 / 96.0))
    put("one", np.ones((P, P)))
    c = i % 64
    c0 = np.clip(c - 8, 0, 48)
    kc = np.arange(64)
    cst[:, CNB:CNB + 64] = np.where((kc[None] >= c0[:, None]) & (kc[None] < c0[:, None] + 16), 0.0, -1e30)
    cst[:, CEPS] = EPS
    cst[:, CONE] = 1.0
    msk = np.zeros((P, NLEV + 1, P), np.int32)
    for l in range(NLEV):
        s = 64 >> l
        msk[:, l] = ((i[:, None] // (2 * s) == i[None] // (2 * s)) & ((i[:, None] // s) % 2 == 0)
                     & ((i[None] // s) % 2 == 1))
    msk[:, NLEV] = np.eye(P)
    f = np.float32
    t = np.arange(L)

    def angles(pos, dim, theta):
        inv = np.power(f(theta), -np.arange(0, dim, 2, dtype=np.float32) / f(dim)).astype(np.float32)
        return pos.astype(np.float32)[:, None] * inv[None]
    rope = np.zeros((6, P, L), np.float32)

    def table(w, name, starts):
        perm = np.zeros((P, P))
        rope[2 * w] = 1.0
        for d0, half, ang in starts:
            co, si = rotation(ang)
            for j in range(half):
                rope[2 * w, d0 + j] = rope[2 * w, d0 + half + j] = co[:, j]
                rope[2 * w + 1, d0 + j] = -si[:, j]
                rope[2 * w + 1, d0 + half + j] = si[:, j]
                perm[d0 + j, d0 + half + j] = perm[d0 + half + j, d0 + j] = 1.0
        put(name, perm)
    row, col = angles(t // 64, 32, 10000.0), angles(t % 64, 32, 10000.0)
    table(0, "pB", [(b + o, 16, ang) for b in (0, 64) for o, ang in ((0, row), (32, col))])
    table(1, "pC", [(64, 16, angles(t, 32, 10000.0))])
    part = angles(t, 16, 500000.0)
    table(2, "pD", [(b, 8, part) for b in (0, 64)])
    return cst, msk.reshape(P, -1), rope


def pack(x):
    par = np.zeros((P, NPAR), np.float32)

    def put(name, v):
        v = np.asarray(v, dtype=np.float32)
        if v.ndim == 1:
            v = v.reshape(-1, P) if v.size >= P else v.reshape(1, -1)
        c = PC[name]
        par[:v.shape[1], c:c + v.shape[0]] = v.T
    g = lambda n: np.asarray(x[n])
    put("nmix", g("norm_mix_w")[0])
    put("nffn", g("norm_ffn_w")[0])
    put("nf", g("norm_f_w"))
    put("ne", g("norm_e_2")[0])
    put("no", g("norm_o_2")[0])
    put("hnw", g("hgrn_norm_w")[0])
    put("gnw", g("gla_norm_w")[0])
    put("scw", g("ssd_conv_w")[0].reshape(-1))
    put("scb", g("ssd_conv_b")[0])
    put("lcw", g("lru_conv_w")[0].reshape(-1))
    put("lcb", g("lru_conv_b")[0])
    put("ba", g("lru_ba")[0])
    put("bx", g("lru_bx")[0])
    put("lam", g("lru_lambda")[0])
    put("gb", g("gla_gate_b")[0])
    put("sd", np.repeat(g("ssd_d")[0], 64))
    put("snw", g("ssd_norm_w")[0])
    put("dtb", g("ssd_dt_bias")[0])
    put("alog", g("ssd_a_log")[0])
    for k, n in (("gqa", "gq_a_2"), ("gka", "gk_a_2"), ("gqb", "gq_b_2"), ("gkb", "gk_b_2"),
                 ("gqd", "gq_d_2"), ("gkd", "gk_d_2")):
        put(k, np.tile(g(n)[0], 2))
    put("gcq", g("g_cq_2")[0])
    put("gckv", g("g_ckv_2")[0])
    put("gqc", g("gq_c_2")[0])
    put("gkc", g("gk_c_2")[0])
    put("gsub", g("g_sub_d_2")[0])
    for k, n in (("lq1", "lam_q1_2"), ("lk1", "lam_k1_2"), ("lq2", "lam_q2_2"), ("lk2", "lam_k2_2")):
        put(k, g(n)[0])
    return par


def kernel(**inputs):
    import numpy as _np
    import concourse.bacc as _bacc
    from concourse.bass_utils import run_bass_kernel_spmd as _run

    nc = _bacc.Bacc("TRN2", target_bir_lowering=False, num_devices=1,
                     dynamic_dma_scratch_size=512)
    arrays, a = {}, {}

    def give(name, arr):
        arr = _np.ascontiguousarray(arr)
        arrays[f"in_{name}"] = arr
        a[name] = nc.dram_tensor(f"in_{name}", arr.shape, mybir.dt.from_np(arr.dtype), kind="ExternalInput").ap()

    for n in ("x", "w_in", "w_branch", "w_out", "w_ffn_in", "w_ffn_out", "w_in_e_2", "w_out_e_2", "w_in_o_2",
              "w_out_o_2", "w_cq_b_2", "w_ckv_b_2", "gla_gate_w", "lru_wa", "lru_wx"):
        give(n, inputs[n])
    cst, msk, rope = constants()
    give("cst", cst)
    give("msk", msk)
    give("rope", rope)
    give("par", pack(inputs))
    r = _np.pad(_np.asarray(inputs["rpb_a_2"])[0], ((0, 0), (0, 0), (48, 48)))
    r = _np.lib.stride_tricks.sliding_window_view(r, 64, axis=2)[:, :, ::-1, :].transpose(0, 2, 1, 3)
    give("rpb", _np.ascontiguousarray(r).reshape(4, 128, 960))
    a["spill"] = nc.dram_tensor("spill", (KD, P, L), F32, kind="Internal").ap()
    a["out"] = nc.dram_tensor("out", (1, L, D), F32, kind="ExternalOutput").ap()
    build(nc, a)
    res = _run(nc, [arrays], core_ids=[0])
    return res.results[0]["out"]
```
